# Optimizing a Trainium2 kernel written in Bass

```python
import jax, jax.numpy as jnp
from jax import lax
import numpy as np

"""Hybrid autoregressive decoder trunk, one inference step for two request groups sharing weights.

Each of DEPTH layers (sandwich RMSNorm around every sub-layer):
  1. parallel token mixers on one normalised input h, with ONE combined input projection h @ w_in whose columns
     are partitioned as [RWKV-7 r|k|v|decay-lora-down|iclr-lora-down|gate-lora-down] [Conformer GLU value|gate]
     [merge gate A|merge gate B]:
       A: RWKV-7 time mixing (token shift, data-dependent decay, generalised delta-rule matrix state), -> D_MODEL
       B: Conformer conv module (GLU -> causal depthwise conv width 31 -> LayerNorm -> swish -> pointwise), -> D_MODEL
     merged as sigmoid(gA)*yA + sigmoid(gB)*yB, then one output projection w_out;
  2. cross-attention (4 heads) into 256 memory tokens (keys/values per layer);
  3. dense SwiGLU FFN.

Inputs: x_prompt (BATCH,SEQ,D_MODEL), x_sample (DEC_BATCH,DEC_SEQ,D_MODEL), mem_prompt (BATCH,256,D_MODEL),
  state_rwkv (DEPTH,DEC_BATCH,H_A,64,64), state_shift (DEPTH,DEC_BATCH,W_RWKV),
  state_conv (DEPTH,DEC_BATCH,30,C_CONV), cache_mem_k / cache_mem_v (DEPTH,DEC_BATCH,256,4,256), weights.
Returns the tuple:
  y_prompt (BATCH,SEQ,D_MODEL), y_sample (DEC_BATCH,DEC_SEQ,D_MODEL),
  new_state_rwkv_prompt (DEPTH,BATCH,H_A,64,64), new_state_shift_prompt (DEPTH,BATCH,W_RWKV),
  new_state_conv_prompt (DEPTH,BATCH,30,C_CONV), new_cache_mem_k_prompt (DEPTH,BATCH,256,4,256),
  new_cache_mem_v_prompt (DEPTH,BATCH,256,4,256),
  new_state_rwkv_sample (DEPTH,DEC_BATCH,H_A,64,64), new_state_shift_sample (DEPTH,DEC_BATCH,W_RWKV),
  new_state_conv_sample (DEPTH,DEC_BATCH,30,C_CONV).
"""

D_MODEL = 1024
BATCH = 1
SEQ = 512
DEPTH = 1
DEC_BATCH = 8
DEC_SEQ = 1
PAST_LEN = 4096
PAGE_SIZE = 128

HEAD_SIZE = 64
C_RWKV = D_MODEL // 2
N_RWKV_HEADS = C_RWKV // HEAD_SIZE
D_DECAY_LORA = 64
D_ICLR_LORA = 64
D_GATE_LORA = 128
GN_EPS = 64e-5
C_CONV = D_MODEL // 2
CONV_WIDTH = 31
N_MEM = 256
N_XHEADS = 4
XHEAD_DIM = D_MODEL // N_XHEADS
D_FF = -(-8 * D_MODEL // (3 * 256)) * 256
W_RWKV = 3 * C_RWKV + D_DECAY_LORA + D_ICLR_LORA + D_GATE_LORA
W_IN = W_RWKV + 2 * C_CONV + 2 * D_MODEL
NORM_EPS = 1e-6
LN_EPS = 1e-5

kernel_name = "rwkv7_conformer_gated_hybrid_step"

def rms_norm(x, g):
    xf = x.astype(jnp.float32)
    y = xf * lax.rsqrt(jnp.mean(xf * xf, axis=-1, keepdims=True) + NORM_EPS)
    return y.astype(x.dtype) * g

def layer_norm(x, g, b):
    xf = x.astype(jnp.float32)
    mu = jnp.mean(xf, axis=-1, keepdims=True)
    var = jnp.mean(jnp.square(xf - mu), axis=-1, keepdims=True)
    return ((xf - mu) * lax.rsqrt(var + LN_EPS)).astype(x.dtype) * g + b

def wkv_scan(S0, r, w, k, v, a, b):
    def step(S, inp):
        r_t, w_t, k_t, v_t, a_t, b_t = inp
        sa = jnp.einsum("bhij,bhj->bhi", S, a_t)
        S = S * w_t[:, :, None, :] + sa[..., None] * b_t[:, :, None, :] + v_t[..., None] * k_t[:, :, None, :]
        y = jnp.einsum("bhij,bhj->bhi", S, r_t)
        return S, y
    seq = tuple(jnp.moveaxis(t, 1, 0) for t in (r, w, k, v, a, b))
    S, ys = lax.scan(step, S0, seq)
    return jnp.moveaxis(ys, 0, 1), S

def rwkv_branch(p, shift0, S0, lp):
    B, T, _ = p.shape
    f32 = jnp.float32
    p_prev = jnp.concatenate([shift0[:, None, :].astype(p.dtype), p[:, :-1]], axis=1)
    xs = p + (p_prev - p) * lp["tshift_mu"]
    c = C_RWKV
    r, k, v, wd, ad, gd = jnp.split(xs, [c, 2 * c, 3 * c, 3 * c + D_DECAY_LORA,
                                          3 * c + D_DECAY_LORA + D_ICLR_LORA], axis=-1)
    w = -jax.nn.softplus(-(lp["decay_w0"] + jnp.tanh(wd) @ lp["decay_w2"]).astype(f32)) - 0.5
    decay = jnp.exp(-jnp.exp(w))
    a = jax.nn.sigmoid((lp["iclr_a0"] + ad @ lp["iclr_a2"]).astype(f32))
    g = jax.nn.sigmoid(gd) @ lp["gate_g2"]
    heads = lambda t: t.reshape(B, T, N_RWKV_HEADS, HEAD_SIZE)
    kk = heads((k * lp["k_k"]).astype(f32))
    kk = kk * lax.rsqrt(jnp.maximum(jnp.sum(kk * kk, axis=-1, keepdims=True), 1e-24))
    k_h = heads(k.astype(f32) * (1.0 + (a - 1.0) * lp["k_a"].astype(f32)))
    a_h = heads(a)
    r_h = heads(r.astype(f32))
    v_h = heads(v.astype(f32))
    y, S = wkv_scan(S0.astype(f32), r_h, heads(decay), k_h, v_h, -kk, kk * a_h)
    mu = jnp.mean(y, axis=-1, keepdims=True)
    var = jnp.mean(jnp.square(y - mu), axis=-1, keepdims=True)
    yn = ((y - mu) * lax.rsqrt(var + GN_EPS)).reshape(B, T, C_RWKV)
    yn = yn * lp["lnx_g"].astype(f32) + lp["lnx_b"].astype(f32)
    bonus = (jnp.sum(r_h * k_h * lp["r_k"].astype(f32), axis=-1, keepdims=True) * v_h).reshape(B, T, C_RWKV)
    out = ((yn + bonus).astype(p.dtype) * g) @ lp["w_out_rwkv"]
    return out, S.astype(p.dtype), p[:, -1]

def conformer_branch(u, buf0, lp):
    u = u + lp["glu_b"]
    val, gate = jnp.split(u, 2, axis=-1)
    glu = val * jax.nn.sigmoid(gate)
    xpad = jnp.concatenate([buf0.astype(glu.dtype), glu], axis=1)
    y = lax.conv_general_dilated(xpad, lp["conv_w"][:, None, :].astype(xpad.dtype),
                                 window_strides=(1,), padding="VALID",
                                 dimension_numbers=("NWC", "WIO", "NWC"),
                                 feature_group_count=C_CONV) + lp["conv_b"]
    y = jax.nn.silu(layer_norm(y, lp["conv_ln_g"], lp["conv_ln_b"]))
    return y @ lp["w_pw"] + lp["b_pw"], xpad[:, -(CONV_WIDTH - 1):]

def mem_kv(mem, g_mem, w_k, w_v):
    B, M, _ = mem.shape
    h = rms_norm(mem, g_mem)
    return ((h @ w_k).reshape(B, M, N_XHEADS, XHEAD_DIM),
            (h @ w_v).reshape(B, M, N_XHEADS, XHEAD_DIM))

def decoder_layer(x, mem_k, mem_v, S0, shift0, buf0, lp):
    B, T, _ = x.shape
    h = rms_norm(x, lp["g_mix_pre"])
    proj = h @ lp["w_in"]
    p_rwkv, p_conv, p_gate = jnp.split(proj, [W_RWKV, W_RWKV + 2 * C_CONV], axis=-1)
    y_a, S1, shift1 = rwkv_branch(p_rwkv, shift0, S0, lp)
    y_b, buf1 = conformer_branch(p_conv, buf0, lp)
    g_a, g_b = jnp.split(jax.nn.sigmoid(p_gate + lp["merge_gate_b"]), 2, axis=-1)
    mixed = (g_a * y_a + g_b * y_b) @ lp["w_out"]
    x = x + rms_norm(mixed, lp["g_mix_post"])
    h = rms_norm(x, lp["g_x_pre"])
    q = (h @ lp["w_q"]).reshape(B, T, N_XHEADS, XHEAD_DIM)
    s = jnp.einsum("bthd,bmhd->bhtm", q.astype(jnp.float32), mem_k.astype(jnp.float32)) * (XHEAD_DIM ** -0.5)
    pr = jax.nn.softmax(s, axis=-1)
    o = jnp.einsum("bhtm,bmhd->bthd", pr, mem_v.astype(jnp.float32)).astype(x.dtype).reshape(B, T, D_MODEL)
    x = x + rms_norm(o @ lp["w_o_x"], lp["g_x_post"])
    h = rms_norm(x, lp["g_ffn_pre"])
    gt, up = jnp.split(h @ lp["w_gate_up"], 2, axis=-1)
    f = (jax.nn.silu(gt) * up) @ lp["w_down"]
    x = x + rms_norm(f, lp["g_ffn_post"])
    return x, S1, shift1, buf1

def setup_inputs(seed: int = 0) -> dict:
    key = jax.random.key(seed)
    ks = iter(jax.random.split(key, 64))
    f32 = jnp.float32
    nrm = lambda shape, s: jax.random.normal(next(ks), shape, f32) * s
    gain = lambda shape: 1.0 + nrm(shape, 0.05)
    L = DEPTH
    d = {}
    d["x_prompt"] = nrm((BATCH, SEQ, D_MODEL), 1.0)
    d["x_sample"] = nrm((DEC_BATCH, DEC_SEQ, D_MODEL), 1.0)
    d["mem_prompt"] = nrm((BATCH, N_MEM, D_MODEL), 1.0)
    d["state_rwkv"] = nrm((L, DEC_BATCH, N_RWKV_HEADS, HEAD_SIZE, HEAD_SIZE), 0.3)
    d["state_shift"] = nrm((L, DEC_BATCH, W_RWKV), 1.0)
    d["state_conv"] = nrm((L, DEC_BATCH, CONV_WIDTH - 1, C_CONV), 0.5)
    d["cache_mem_k"] = nrm((L, DEC_BATCH, N_MEM, N_XHEADS, XHEAD_DIM), 1.0)
    d["cache_mem_v"] = nrm((L, DEC_BATCH, N_MEM, N_XHEADS, XHEAD_DIM), 1.0)
    d["w_in"] = nrm((L, D_MODEL, W_IN), D_MODEL ** -0.5)
    d["tshift_mu"] = jax.random.uniform(next(ks), (L, W_RWKV), f32)
    d["decay_w0"] = nrm((L, C_RWKV), 0.5) - 1.0
    d["decay_w2"] = nrm((L, D_DECAY_LORA, C_RWKV), 0.1)
    d["iclr_a0"] = nrm((L, C_RWKV), 0.5)
    d["iclr_a2"] = nrm((L, D_ICLR_LORA, C_RWKV), 0.1)
    d["gate_g2"] = nrm((L, D_GATE_LORA, C_RWKV), D_GATE_LORA ** -0.5)
    d["k_k"] = 0.85 + nrm((L, C_RWKV), 0.05)
    d["k_a"] = gain((L, C_RWKV))
    d["r_k"] = nrm((L, N_RWKV_HEADS, HEAD_SIZE), 0.1)
    d["lnx_g"] = gain((L, C_RWKV))
    d["lnx_b"] = nrm((L, C_RWKV), 0.01)
    d["w_out_rwkv"] = nrm((L, C_RWKV, D_MODEL), C_RWKV ** -0.5)
    d["glu_b"] = nrm((L, 2 * C_CONV), 0.01)
    d["conv_w"] = nrm((L, CONV_WIDTH, C_CONV), CONV_WIDTH ** -0.5)
    d["conv_b"] = nrm((L, C_CONV), 0.01)
    d["conv_ln_g"] = gain((L, C_CONV))
    d["conv_ln_b"] = nrm((L, C_CONV), 0.01)
    d["w_pw"] = nrm((L, C_CONV, D_MODEL), C_CONV ** -0.5)
    d["b_pw"] = nrm((L, D_MODEL), 0.01)
    d["merge_gate_b"] = nrm((L, 2 * D_MODEL), 0.01)
    d["w_out"] = nrm((L, D_MODEL, D_MODEL), D_MODEL ** -0.5)
    d["g_mix_pre"] = gain((L, D_MODEL))
    d["g_mix_post"] = gain((L, D_MODEL))
    d["g_mem"] = gain((L, D_MODEL))
    d["w_q"] = nrm((L, D_MODEL, D_MODEL), D_MODEL ** -0.5)
    d["w_k"] = nrm((L, D_MODEL, D_MODEL), D_MODEL ** -0.5)
    d["w_v"] = nrm((L, D_MODEL, D_MODEL), D_MODEL ** -0.5)
    d["w_o_x"] = nrm((L, D_MODEL, D_MODEL), D_MODEL ** -0.5)
    d["g_x_pre"] = gain((L, D_MODEL))
    d["g_x_post"] = gain((L, D_MODEL))
    d["g_ffn_pre"] = gain((L, D_MODEL))
    d["g_ffn_post"] = gain((L, D_MODEL))
    d["w_gate_up"] = nrm((L, D_MODEL, 2 * D_FF), D_MODEL ** -0.5)
    d["w_down"] = nrm((L, D_FF, D_MODEL), D_FF ** -0.5)
    return d

def reference(x_prompt, x_sample, mem_prompt, state_rwkv, state_shift, state_conv, cache_mem_k, cache_mem_v,
              w_in, tshift_mu, decay_w0, decay_w2, iclr_a0, iclr_a2, gate_g2, k_k, k_a, r_k, lnx_g, lnx_b,
              w_out_rwkv, glu_b, conv_w, conv_b, conv_ln_g, conv_ln_b, w_pw, b_pw, merge_gate_b, w_out,
              g_mix_pre, g_mix_post, g_mem, w_q, w_k, w_v, w_o_x, g_x_pre, g_x_post, g_ffn_pre, g_ffn_post,
              w_gate_up, w_down):
    xp, xs = x_prompt, x_sample
    Bp = x_prompt.shape[0]
    rwkv_p, shift_p, conv_p, memk_p, memv_p = [], [], [], [], []
    rwkv_s, shift_s, conv_s = [], [], []
    for l in range(DEPTH):
        lp = {"w_in": w_in[l], "tshift_mu": tshift_mu[l], "decay_w0": decay_w0[l], "decay_w2": decay_w2[l],
              "iclr_a0": iclr_a0[l], "iclr_a2": iclr_a2[l], "gate_g2": gate_g2[l], "k_k": k_k[l],
              "k_a": k_a[l], "r_k": r_k[l], "lnx_g": lnx_g[l], "lnx_b": lnx_b[l],
              "w_out_rwkv": w_out_rwkv[l], "glu_b": glu_b[l], "conv_w": conv_w[l], "conv_b": conv_b[l],
              "conv_ln_g": conv_ln_g[l], "conv_ln_b": conv_ln_b[l], "w_pw": w_pw[l], "b_pw": b_pw[l],
              "merge_gate_b": merge_gate_b[l], "w_out": w_out[l], "g_mix_pre": g_mix_pre[l],
              "g_mix_post": g_mix_post[l], "w_q": w_q[l], "w_o_x": w_o_x[l], "g_x_pre": g_x_pre[l],
              "g_x_post": g_x_post[l], "g_ffn_pre": g_ffn_pre[l], "g_ffn_post": g_ffn_post[l],
              "w_gate_up": w_gate_up[l], "w_down": w_down[l]}
        mk_p, mv_p = mem_kv(mem_prompt, g_mem[l], w_k[l], w_v[l])
        S0 = jnp.zeros((Bp, N_RWKV_HEADS, HEAD_SIZE, HEAD_SIZE), xp.dtype)
        sh0 = jnp.zeros((Bp, W_RWKV), xp.dtype)
        cb0 = jnp.zeros((Bp, CONV_WIDTH - 1, C_CONV), xp.dtype)
        xp, S_p, sh_p, cb_p = decoder_layer(xp, mk_p, mv_p, S0, sh0, cb0, lp)
        rwkv_p.append(S_p); shift_p.append(sh_p); conv_p.append(cb_p); memk_p.append(mk_p); memv_p.append(mv_p)
        xs, S_s, sh_s, cb_s = decoder_layer(xs, cache_mem_k[l], cache_mem_v[l], state_rwkv[l], state_shift[l],
                                            state_conv[l], lp)
        rwkv_s.append(S_s); shift_s.append(sh_s); conv_s.append(cb_s)
    return (xp, xs, jnp.stack(rwkv_p), jnp.stack(shift_p), jnp.stack(conv_p), jnp.stack(memk_p),
            jnp.stack(memv_p), jnp.stack(rwkv_s), jnp.stack(shift_s), jnp.stack(conv_s))


_drawn_inputs = setup_inputs


def setup_inputs(seed=0):
    import zlib

    import numpy as np

    out = dict(_drawn_inputs(seed))
    spreads = {}
    factors = {'k_k': 4.293,
     'lnx_b': 8.0,
     'glu_b': 5.209,
     'conv_b': 4.741,
     'conv_ln_b': 8.0,
     'b_pw': 6.581,
     'merge_gate_b': 8.0}
    for name, (base, spread) in spreads.items():
        noise = np.random.default_rng([zlib.crc32(name.encode()), seed]).standard_normal(out[name].shape)
        drawn = base * np.exp(spread * noise) if base else spread * noise
        out[name] = __import__('jax').numpy.asarray(drawn.astype(out[name].dtype))
    for name, factor in factors.items():
        out[name] = (out[name] * factor).astype(out[name].dtype)
    return out
```

```python
import concourse.bass as bass
from concourse import mybir

F32 = mybir.dt.float32
F32R = mybir.dt.float32r
ALU = mybir.AluOpType
ACT = mybir.ActivationFunctionType
AX = mybir.AxisListType

P = 128
D = 1024
KT = D // P
T = 512
B = 8
NT = T + B
HALF = NT // 2
C = 512
NP = C // P
HS = 64
NC = T // HS
W_RWKV = 3 * C + 256
N_SHIFT = W_RWKV // P
TAPS = 31
MEM = 256
CACHE_SLOTS = 11
XH, XHD = 4, D // 4
FF = 2816
FT = FF // P
NORM_EPS, LN_EPS, GN_EPS = 1e-6, 1e-5, 64e-5
DECAY = -0.6065306597126334
LN_SCALE = 2.0 ** 30
LN_HALF = 10.397207708399179

VECTORS = [("decay_w0", 4), ("iclr_a0", 4), ("k_k", 4), ("k_a", 4), ("r_k", 4), ("lnx_g", 4), ("lnx_b", 4),
           ("glu_b", 8), ("conv_b", 4), ("conv_ln_g", 4), ("conv_ln_b", 4), ("b_pw", 8), ("merge_gate_b", 16),
           ("g_mix_pre", 8), ("g_mix_post", 8), ("g_mem", 8), ("g_x_pre", 8), ("g_x_post", 8),
           ("g_ffn_pre", 8), ("g_ffn_post", 8)]

B_PAIR = 0
B_GB = 30
B_K = 38
B_V = 46
B_MIX = 54
B_OUT = 70
B_Q = 78
B_O = 86
B_UP = 94
B_DOWN = 138
N_BLOCKS = B_DOWN + 3 * KT
DOWN_KT = (8, 8, 6)
RAW_SLOTS = 4

STEP_ENGINES = [("gram_b", "v"), ("gram_k", "v"), ("gram_a", "v"), ("tok_kv", "a"), ("tok_b", "a"), ("akv", "a"),
                ("dbl0", "va"), ("dbl1", "va"), ("dbl2", "va"), ("dbl3", "va"), ("dbl4", "va"), ("dbl5", "v"),
                ("pw", "v"), ("h", "a")]
STEPS = [(name, q, e) for name, e in STEP_ENGINES for q in range(2)]
N_LOCKSTEP = len(STEPS)
STEPS += [("chain", c, "v") for c in range(1, NC)] + [("y", q, "a") for q in range(2)]
N_STEPS = len(STEPS)


def emptied(engine, pair, upto):
    per_pair = sum(engine in e for _, _, e in STEPS)
    return pair * per_pair + sum(engine in e for _, _, e in STEPS[:upto])


def hybrid_step_kernel(nc, A, O):
    (y_prompt, y_sample, o_rwkv_p, o_shift_p, o_conv_p, o_memk, o_memv, o_rwkv_s, o_shift_s, o_conv_s) = O
    vec_scratch = nc.dram_tensor("vec_scratch", [6, B, C], F32, kind="Internal").ap()
    y_scratch = nc.dram_tensor("y_scratch", [B, C], F32, kind="Internal").ap()
    q_scratch = nc.dram_tensor("q_scratch", [B, D], F32, kind="Internal").ap()

    cursor = [(nc.sbuf_base + 63) // 64 * 64]

    def buf(name, shape, dt=F32):
        size = 4
        for n in shape[1:]:
            size *= n
        t = nc.alloc_sbuf_tensor_at(name, shape, dt, offset=cursor[0])
        cursor[0] += (size + 31) // 32 * 32
        assert cursor[0] <= nc.sbuf_usable_end, (name, cursor[0])
        return t

    ident = buf("ident", [P, P])
    stack_id = buf("stack_id", [P, HS])
    head_ones = buf("head_ones", [P, P])
    head_mean = buf("head_mean", [P, P])
    model_mean = buf("model_mean", [P, P])
    conv_mean = buf("conv_mean", [P, P])
    mask_s = buf("mask_s", [P, 2, HS])
    mask_t = buf("mask_t", [P, 2, HS])
    eps = buf("eps", [P, 4])
    eps_copy = buf("eps_copy", [P, 4])
    prm = buf("prm", [P, 3, P])
    rs = buf("rs", [P, NT])
    w_raw = buf("w_raw", [P, RAW_SLOTS, KT, P])
    w_hi = buf("w_hi", [P, 2, KT, P], F32R)
    w_lo = buf("w_lo", [P, 2, KT, P], F32R)
    h_hi = buf("h_hi", [P, KT, NT], F32R)
    h_lo = buf("h_lo", [P, KT, NT], F32R)
    shared = cursor[0]

    gate_a = buf("gate_a", [P, KT, NT])
    y_fm = buf("y_fm", [P, NP, NT])
    bonus = buf("bonus", [P, NP, NT])
    g_fm = buf("g_fm", [P, NP, NT])
    conv_y = buf("conv_y", [P, NP, NT])
    small_base = cursor[0]
    s_vec = buf("s_vec", [P, 6, NP, B])
    s_final = buf("s_final", [P, NP, HS])
    p_last = buf("p_last", [P, N_SHIFT, 1 + B])
    glu_last = buf("glu_last", [P, NP, TAPS - 1])
    glu_s = buf("glu_s", [P, NP, B])
    pair_base = cursor[0]
    p_ext = buf("p_ext", [P, 3, 1 + NT])
    lora = buf("lora", [P, 2, NT])
    lora_w = buf("lora_w", [P, C])
    gate_w = buf("gate_w", [P, C])
    shift_t = buf("shift_t", [P, N_SHIFT, B])
    scan_mask = buf("scan_mask", [P, T])
    xs = buf("xs", [P, 3, NT])
    sig = buf("sig", [P, NT])
    cum = buf("cum", [P, T])
    e_dec = buf("e_dec", [P, T])
    iclr = buf("iclr", [P, NT])
    kkn = buf("kkn", [P, NT])
    tmp1 = buf("tmp1", [P, NT])
    tmp2 = buf("tmp2", [P, NT])
    kh = buf("kh", [P, NT])
    glu_sig = rs
    glu = buf("glu", [P, TAPS - 1 + NT])
    ar = buf("ar", [P, NC, 2, HS])
    bi = buf("bi", [P, NC, 2, HS])
    kt_fm = buf("kt_fm", [P, NC, HS])
    bh_fm = buf("bh_fm", [P, NC, HS])
    kh_fm = buf("kh_fm", [P, NC, HS])
    g1 = buf("g1", [P, NC, 3 * HS])
    g2 = buf("g2", [P, NC, 2 * HS])
    axb = buf("axb", [P, NC, 3 * HS])
    kv_tok = buf("kv_tok", [P, NC, 2 * HS])
    wg = buf("wg", [P, NC, 2 * HS])
    h_add = buf("h_add", [P, NC, HS])
    s_all = buf("s_all", [P, NC + 1, HS])
    pair_end = cursor[0]
    cursor[0] = shared
    x_tok = buf("x_tok", [P, T // P, D])
    xs_tok = buf("xs_tok", [B, D])
    x_fm = buf("x_fm", [P, KT, NT])
    h_fm = buf("h_fm", [P, KT, NT])
    p_rows = buf("p_rows", [P, 3, P])
    shift_rows = buf("shift_rows", [B, W_RWKV])
    pro_end = cursor[0]
    cursor[0] = pair_base
    kt = buf("kt", [P, KT, MEM])
    v_tok = buf("v_tok", [P, 2, D])
    attn_base = cursor[0]
    gate_b = buf("gate_b", [P, KT, NT])
    m_hi = buf("m_hi", [P, KT, MEM], F32R)
    m_lo = buf("m_lo", [P, KT, MEM], F32R)
    kv_base = cursor[0]
    ss = buf("ss", [P, HS // 2, HS])
    ss_tmp = buf("ss_tmp", [P, HS // 2, HS])
    vs = buf("vs", [P, 5, HS])
    vs_v = buf("vs_v", [P, HS // 2])
    vs_sa = buf("vs_sa", [P, HS // 2])
    vs_y = buf("vs_y", [P, HS // 2])
    win = buf("win", [P, NP, B, TAPS])
    win_rows = buf("win_rows", [120, 2, C])
    y_rows = buf("y_rows", [B, C])
    ln_base = cursor[0]
    ln_tmp = buf("ln_tmp", [P, NT])
    ln_mu = buf("ln_mu", [P, NT])
    cursor[0] = pair_base
    mem_tok = buf("mem_tok", [P, 2, D])
    mem_fm = buf("mem_fm", [P, KT, MEM])
    cursor[0] = kv_base
    k_tok = buf("k_tok", [P, 2, D])
    v_fm = buf("v_fm", [P, KT, MEM])
    cursor[0] = kv_base
    vt1 = buf("vt1", [B, 4, C])
    cursor[0] = ln_base
    vt2 = buf("vt2", [B, 2, C])
    cursor[0] = shared
    x_res = buf("x_res", [P, KT, NT])
    y_buf = buf("y_buf", [P, KT, NT])
    sq_acc = buf("sq_acc", [P, NT])
    sq_tmp = buf("sq_tmp", [P, 2, NT])
    stream_end = cursor[0]
    sc = buf("sc", [P, 2, B * XH])
    prob_s = buf("prob_s", [B * XH, MEM])
    head_pick = buf("head_pick", [B * XH, XH])
    o_pick = buf("o_pick", [B * XH, XHD])
    stat = buf("stat", [P, 2, 16])
    stat_s = buf("stat_s", [B * XH, 4])
    q_tok = buf("q_tok", [B, D])
    assert cursor[0] <= small_base
    cursor[0] = attn_base
    cache = buf("cache", [P, CACHE_SLOTS, D])
    q_bc = buf("q_bc", [P, 2, D])
    prob = buf("prob", [P, 4, MEM])
    prob_t = buf("prob_t", [P, 2, T])
    prob_z = buf("prob_z", [P, 2, B * B * XH])
    cursor[0] = attn_base
    x_tok2 = buf("x_tok2", [P, T // P, D])
    xs_tok2 = buf("xs_tok2", [B, D])
    cursor[0] = attn_base
    shift_out = buf("shift_out", [1 + B, N_SHIFT, P])
    conv_out = buf("conv_out", [TAPS - 1, C])
    glu_out = buf("glu_out", [B, C])
    rwkv_out = buf("rwkv_out", [HS, NP, P])
    cursor[0] = stream_end
    f_hi = buf("f_hi", [P, FT, NT], F32R)
    f_lo = buf("f_lo", [P, FT, NT], F32R)
    silu = buf("silu", [P, NT])
    f_tmp = buf("f_tmp", [P, 2, NT])
    cursor[0] = stream_end
    y_tok = buf("y_tok", [P, T // P, D])
    ys_tok = buf("ys_tok", [B, D])

    ps = nc.alloc_psum_tensor("ps", [P, 8, 512], F32)

    def sem(name):
        return nc.alloc_semaphore(name)

    w_landed = [sem(f"w_landed{i}") for i in range(RAW_SLOTS)]
    w_hi_ready, w_lo_ready, block_done = sem("w_hi_ready"), sem("w_lo_ready"), sem("block_done")
    out_taken = [sem("out_taken0"), sem("out_taken1")]
    consts_made = sem("consts_made")
    x_landed, prm_landed, shift_landed = sem("x_landed"), sem("prm_landed"), sem("shift_landed")
    prm_turned, shift_turned, x_turned = sem("prm_turned"), sem("shift_turned"), sem("x_turned")
    prm_ready, xs_turned, xs_taken = sem("prm_ready"), sem("xs_turned"), sem("xs_taken")
    x_taken_v, x_taken_a = sem("x_taken_v"), sem("x_taken_a")
    pair_consts, lora_landed = sem("pair_consts"), sem("lora_landed")

    norm_squares, norm_stats, norm_rsqrt = sem("norm_squares"), sem("norm_stats"), sem("norm_rsqrt")
    norm_scaled, norm_hi, norm_lo = sem("norm_scaled"), sem("norm_hi"), sem("norm_lo")

    class Norm:
        squares, stats, rsqrt, scaled, hi, lo = (norm_squares, norm_stats, norm_rsqrt, norm_scaled, norm_hi, norm_lo)

        def __init__(self, turn):
            self.turn, self.tiles = turn, KT * turn

    n_mix, n_mem, n_x, n_ffn = Norm(0), Norm(1), Norm(2), Norm(3)

    act_chain, dve_chain = sem("act_chain"), sem("dve_chain")
    counts = {"a": 0, "v": 0}

    def link_a(ins, n=1):
        ins.then_inc(act_chain, 1)
        counts["a"] += 1
        nc.scalar.wait_ge(act_chain, counts["a"])

    def link_v(ins):
        ins.then_inc(dve_chain, 1)
        counts["v"] += 1
        nc.vector.wait_ge(dve_chain, counts["v"])

    tile_ready, lora_in, lora_ready = sem("tile_ready"), sem("lora_in"), sem("lora_ready")
    lora_mm, lora_taken, xs_ready = sem("lora_mm"), sem("lora_taken"), sem("xs_ready")
    kk_squares, kk_max, kk_rsqrt, rk_ready = sem("kk_squares"), sem("kk_max"), sem("kk_rsqrt"), sem("rk_ready")
    cum_ready, decays_ready, fm_ready, glu_gate = sem("cum_ready"), sem("decays_ready"), sem("fm_ready"), sem("glu_gate")
    bonus_taken = sem("bonus_taken")
    step_mm, step_v, step_a = sem("step_mm"), sem("step_v"), sem("step_a")

    def prm_col(name, i):
        at = 0
        for n, rows in VECTORS:
            if n == name:
                return prm[:, 1, at + i:at + i + 1]
            at += rows

    def mu_col(tile):
        return prm[:, 2, tile:tile + 1]

    def two(ap):
        return ap.rearrange("p (a b) -> p a b", a=2)

    def out_view(s):
        return ps[:, 2 * s:2 * s + 2, 0:HALF]

    def dense(pe, b, s, x_hi, x_lo, kts=KT, k0=0, x0=0, width=HALF, parts=2, first=True, last=True,
              taken=None, x_ready=None, more=0):
        pe.wait_ge(w_lo_ready, b + 1 + more)
        if taken is not None:
            pe.wait_ge(out_taken[s], taken)
        for k in range(k0, k0 + kts):
            if x_ready is not None:
                pe.wait_ge(x_ready[0], x_ready[1] + k + 1)
            for n, (w, x) in enumerate(((w_hi, x_hi), (w_hi, x_lo), (w_lo, x_hi))):
                for a in range(parts):
                    mm = nc.tensor.matmul(ps[:, 2 * s + a, 0:width], w[:, b % 2, k, :],
                                          x[:, x0 + k, a * width:(a + 1) * width],
                                          start=(first and k == 0 and n == 0),
                                          stop=(last and k == block_kts(b) - 1 and n == 2))
        if k0 + kts == block_kts(b):
            mm.then_inc(block_done, 1)

    def block_kts(b):
        if B_MIX <= b < B_OUT:
            return KT // 2
        return DOWN_KT[(b - B_DOWN) % 3] if b >= B_DOWN else KT

    def split_hi(b, more=0, more4=0):
        nc.scalar.wait_ge(w_landed[b % RAW_SLOTS], 16 * (b // RAW_SLOTS + 1) + 16 * more4)
        if b >= 2:
            nc.scalar.wait_ge(block_done, b - 1 + more)
        nc.scalar.activation(w_hi[:, b % 2], w_raw[:, b % RAW_SLOTS], ACT.Copy).then_inc(w_hi_ready, 1)

    def pe_stats(norm, src, mean, tiles, width=HALF, parts=2):
        for k in range(tiles):
            nc.tensor.wait_ge(norm.squares, norm.tiles + k + 1)
            for a in range(parts):
                mm = nc.tensor.matmul(ps[:, 6 + a, 0:width], mean[:, :], src(k)[:, a * width:(a + 1) * width],
                                      start=(k == 0), stop=(k == tiles - 1))
            if k == tiles - 1:
                mm.then_inc(norm.stats, 1)

    def act_rsqrt(norm, out, src, eps_col):
        nc.scalar.wait_ge(norm.stats, norm.turn + 1)
        link_a(nc.scalar.activation(out, src, ACT.Ln, bias=eps_col))
        nc.scalar.activation(out, out, ACT.Exp, scale=-0.5).then_inc(norm.rsqrt, 1)

    def act_split(norm, src, hi, tiles=KT):
        for k in range(tiles):
            nc.scalar.wait_ge(norm.scaled, norm.tiles + k + 1)
            nc.scalar.activation(hi[:, k], src[:, k], ACT.Copy).then_inc(norm.hi, 1)

    def dve_scale_split(norm, x, scale, gain, tmp, lo, hi, tiles=KT):
        nc.vector.wait_ge(norm.rsqrt, norm.turn + 1)
        for k in range(tiles + 1):
            if k < tiles:
                nc.vector.scalar_tensor_tensor(tmp[:, k], x[:, k], prm_col(gain, k), scale, ALU.mult, ALU.mult
                                               ).then_inc(norm.scaled, 1)
            if k:
                nc.vector.wait_ge(norm.hi, norm.tiles + k)
                nc.vector.tensor_tensor(lo[:, k - 1], tmp[:, k - 1], hi[:, k - 1].bitcast(F32), ALU.subtract
                                        ).then_inc(norm.lo, 1)

    def first_block(p):
        return 5 + 7 * p

    w_in_v = A["w_in"][0].rearrange("(k p) c -> p k c", p=P)

    def in_column(b):
        if b < 5:
            return P * (12, 13, 0, 4, 8)[b]
        p, j = divmod(b - 5, 7)
        return (W_RWKV + C + P * p, W_RWKV + P * p, W_RWKV + 2 * C + 2 * P * p, W_RWKV + 2 * C + 2 * P * p + P,
                P * (p + 1), P * (p + 5), P * (p + 9))[j]

    def weight_view(name):
        return A[name][0].rearrange("(k p) c -> p k c", p=P)


    post_squares, post_added, post_stats_mm = sem("post_squares"), sem("post_added"), sem("post_stats_mm")
    post_rsqrt, post_x_ready = sem("post_rsqrt"), sem("post_x_ready")

    class Post:
        squares, added, stats, rsqrt, x_ready = post_squares, post_added, post_stats_mm, post_rsqrt, post_x_ready

        def __init__(self, turn, taken):
            self.turn, self.tiles, self.taken = turn, KT * turn, taken

    p_mix, p_x, p_ffn = Post(0, B_Q // 2), Post(1, B_UP // 2), Post(2, (B_DOWN + KT) // 2)
    attn_exp, attn_max, conv_hi, conv_lo = sem("attn_exp"), sem("attn_max"), sem("conv_hi"), sem("conv_lo")
    conv_ready, conv_scaled, conv_silu, f_hi_ready = sem("conv_ready"), sem("conv_scaled"), sem("conv_silu"), sem("f_hi_ready")
    f_lo_ready, gn_centred, gn_mean_mm = sem("f_lo_ready"), sem("gn_centred"), sem("gn_mean_mm")
    gn_rsqrt, gn_scaled, gn_squares, gn_var_mm = sem("gn_rsqrt"), sem("gn_scaled"), sem("gn_squares"), sem("gn_var_mm")
    k_tok_ready, k_used, ln_centred, ln_mean = sem("k_tok_ready"), sem("k_used"), sem("ln_centred"), sem("ln_mean")
    ln_rsqrt, ln_squares, ln_var, mem_back = sem("ln_rsqrt"), sem("ln_squares"), sem("ln_var"), sem("mem_back")
    mem_landed, mem_stored, mem_taken, mem_turned = sem("mem_landed"), sem("mem_stored"), sem("mem_taken"), sem("mem_turned")
    merged, mixed_hi, mixed_lo, o_hi = sem("merged"), sem("mixed_hi"), sem("mixed_lo"), sem("o_hi")
    o_lo, o_picked, o_turned, prob_ready = sem("o_lo"), sem("o_picked"), sem("o_turned"), sem("prob_ready")
    prob_s_ready, prob_s_turned, prob_t_ready, prob_turned = sem("prob_s_ready"), sem("prob_s_turned"), sem("prob_t_ready"), sem("prob_turned")
    prob_z_ready, q_stored, q_taken, q_turned = sem("prob_z_ready"), sem("q_stored"), sem("q_taken"), sem("q_turned")
    rwkv_hi, rwkv_lo, rwkv_made, sc_exp = sem("rwkv_hi"), sem("rwkv_lo"), sem("rwkv_made"), sem("sc_exp")
    sc_max, sc_turned, score_mm, shift_taken = sem("sc_max"), sem("sc_turned"), sem("score_mm"), sem("shift_taken")
    ss_landed, ss_stored, state_stored, state_taken = sem("ss_landed"), sem("ss_stored"), sem("state_stored"), sem("state_taken")
    state_turned, stored, v_tok_ready, v_used = sem("state_turned"), sem("stored"), sem("v_tok_ready"), sem("v_used")
    val_taken, vec_ready, vec_stored, vec_taken = sem("val_taken"), sem("vec_ready"), sem("vec_stored"), sem("vec_taken")
    vec_turned, weighed, win_landed, win_turned = sem("vec_turned"), sem("weighed"), sem("win_landed"), sem("win_turned")
    x2_landed, x2_taken_a, x2_taken_v, x2_turned = sem("x2_landed"), sem("x2_taken_a"), sem("x2_taken_v"), sem("x2_turned")
    y_landed, y_ready, y_turn_a, y_turn_v = sem("y_landed"), sem("y_ready"), sem("y_turn_a"), sem("y_turn_v")
    y_turned, y_turns, ys_made, ys_stored = sem("y_turned"), sem("y_turns"), sem("ys_made"), sem("ys_stored")
    cache_landed = [sem(f"cache_landed{i}") for i in range(CACHE_SLOTS)]
    q_landed = [sem("q_landed0"), sem("q_landed1")]
    N_CONSTS = 25

    def ln_buf(j):
        return (ln_tmp, ln_mu)[j % 2][:, :]

    with nc.Block() as block:
        @block.sync
        def _(sp):
            def load(b, src, more=0, kts=KT):
                if not (isinstance(b, int) and b < RAW_SLOTS):
                    sp.wait_ge(w_lo_ready, b - RAW_SLOTS + 1 + more)
                sp.dma_start(w_raw[:, b % RAW_SLOTS, 0:kts], src).then_inc(w_landed[b % RAW_SLOTS], 16)

            for b in range(B_GB):
                load(b, w_in_v[:, :, in_column(b):in_column(b) + P])
            with sp.Fori(0, KT // 4) as i:
                for u in range(4):
                    load(B_GB + u, w_in_v[:, :, bass.ds(i * (4 * P) + (W_RWKV + 2 * C + D + P * u), P)], more=4 * i)
            for b0, name in ((B_K, "w_k"), (B_V, "w_v")):
                with sp.Fori(0, KT // 4) as i:
                    for u in range(4):
                        load(b0 + u, weight_view(name)[:, :, bass.ds(i * (4 * P) + P * u, P)], more=4 * i)
            with sp.Fori(0, KT // 2) as i:
                for u in range(4):
                    name = ("w_pw", "w_out_rwkv")[u % 2]
                    load(B_MIX + u, weight_view(name)[:, :, bass.ds(i * (2 * P) + P * (u // 2), P)],
                         more=4 * i, kts=KT // 2)
            with sp.Fori(0, KT // 4) as i:
                for u in range(4):
                    load(B_OUT + u, weight_view("w_out")[:, :, bass.ds(i * (4 * P) + P * u, P)], more=4 * i)

            def load_cache(t):
                name, j = ("cache_mem_k", t) if t < 2 * B else ("cache_mem_v", t - 2 * B)
                if t == 0:
                    sp.wait_ge(x2_turned, 9)
                    sp.wait_ge(mem_stored, 32)
                if t >= CACHE_SLOTS:
                    old = t - CACHE_SLOTS
                    if old < 2 * B:
                        sp.wait_ge(k_used, old + 1)
                    else:
                        sp.wait_ge(v_used, old - 2 * B + 1)
                src = A[name][0][j // 2].rearrange("(m p) h d -> m p (h d)", p=P)[j % 2]
                sp.dma_start(cache[:, t % CACHE_SLOTS], src).then_inc(cache_landed[t % CACHE_SLOTS], 16)

            for m in range(KT):
                load(B_Q + m, weight_view("w_q")[:, :, P * m:P * m + P])
                if m >= 4:
                    load_cache(2 * (m - 4))
                    load_cache(2 * (m - 4) + 1)
            for t in range(8, CACHE_SLOTS):
                load_cache(t)
            for m in range(4):
                load(B_O + m, weight_view("w_o_x")[:, :, P * m:P * m + P])
            sp.wait_ge(q_taken, 1)
            sp.dma_start(q_scratch, q_tok[:, :]).then_inc(q_stored, 16)
            sp.wait_ge(q_stored, 16)
            t = CACHE_SLOTS
            for b in range(B):
                if b >= 2:
                    sp.wait_ge(k_used, 2 * (b - 1))
                sp.dma_start(q_bc[:, b % 2], q_scratch[b].partition_broadcast(P)).then_inc(q_landed[b % 2], 16)
                while t < 4 * B and t - CACHE_SLOTS < 2 * (b - 1):
                    load_cache(t)
                    t += 1
            while t < 4 * B:
                load_cache(t)
                t += 1
            for m in range(4, KT):
                load(B_O + m, weight_view("w_o_x")[:, :, P * m:P * m + P])
            with sp.Fori(0, FT // 2) as i:
                for u in range(4):
                    load(B_UP + u, weight_view("w_gate_up")[:, :, bass.ds(
                        i * (2 * P) + (FF * (u % 2) + P * (u // 2)), P)], more=4 * i)
            with sp.Fori(0, KT // 4) as i:
                for u in range(12):
                    kts, k0 = DOWN_KT[u % 3], sum(DOWN_KT[:u % 3])
                    load(B_DOWN + u, weight_view("w_down")[:, k0:k0 + kts, bass.ds(i * (4 * P) + P * (u // 3), P)],
                         more=12 * i, kts=kts)
            for j in range(4):
                (sp.wait_ge(y_turn_a, j // 2 + 1) if j % 2 == 0 else sp.wait_ge(y_turn_v, j // 2 + 1))
                sp.dma_start(y_prompt[0, P * j:P * j + P, :], y_tok[:, j]).then_inc(stored, 16)
            sp.wait_ge(y_turn_a, 3)
            sp.dma_start(y_sample[:, 0, :], ys_tok[:, :]).then_inc(stored, 16)
            sp.wait_ge(stored, 5 * 16)
            sp.wait_ge(state_stored, 6 * 16)
            sp.wait_ge(mem_stored, 32)
            sp.wait_ge(ss_stored, 16)

        @block.gpsimd
        def _(pool):
            for t, v in ((ident, 0.0), (stack_id, 0.0), (head_ones, 1.0), (head_mean, 1.0 / HS),
                         (model_mean, 1.0 / D), (conv_mean, 1.0 / C), (mask_s, 1.0), (mask_t, 1.0)):
                pool.memset(t[:], v).then_inc(consts_made, 1)
            for j, v in enumerate((NORM_EPS, GN_EPS, LN_EPS, LN_HALF)):
                pool.memset(eps[:, j:j + 1], v).then_inc(consts_made, 1)
            pool.wait_ge(consts_made, 12)
            pool.affine_select(out=ident[:, :], in_=ident[:, :], compare_op=ALU.not_equal, fill=1.0, base=0,
                               pattern=[[-1, P]], channel_multiplier=1).then_inc(consts_made, 1)
            pool.affine_select(out=stack_id[:, :], in_=stack_id[:, :], compare_op=ALU.not_equal, fill=1.0, base=0,
                               pattern=[[-1, HS]], channel_multiplier=1).then_inc(consts_made, 1)
            pool.wait_ge(consts_made, 14)
            pool.affine_select(out=stack_id[:, :], in_=stack_id[:, :], compare_op=ALU.not_equal, fill=1.0, base=-HS,
                               pattern=[[-1, HS]], channel_multiplier=1).then_inc(consts_made, 1)
            for t in (head_ones, head_mean):
                pool.affine_select(out=t[:, 0:HS], in_=t[:, 0:HS], compare_op=ALU.is_gt, fill=0.0, base=HS,
                                   pattern=[[0, HS]], channel_multiplier=-1).then_inc(consts_made, 1)
                pool.affine_select(out=t[:, HS:P], in_=t[:, HS:P], compare_op=ALU.is_ge, fill=0.0, base=-HS,
                                   pattern=[[0, HS]], channel_multiplier=1).then_inc(consts_made, 1)
            for h in range(2):
                r = slice(HS * h, HS * h + HS)
                pool.wait_ge(consts_made, 19 + 3 * h)
                pool.affine_select(out=mask_s[r, 0, :], in_=mask_s[r, 0, :], compare_op=ALU.is_gt, fill=0.0, base=0,
                                   pattern=[[1, HS]], channel_multiplier=-1).then_inc(consts_made, 1)
                pool.affine_select(out=mask_s[r, 1, :], in_=mask_s[r, 1, :], compare_op=ALU.is_ge, fill=0.0, base=0,
                                   pattern=[[1, HS]], channel_multiplier=-1).then_inc(consts_made, 1)
                pool.affine_select(out=mask_t[r, 0, :], in_=mask_t[r, 0, :], compare_op=ALU.is_gt, fill=0.0, base=0,
                                   pattern=[[-1, HS]], channel_multiplier=1).then_inc(consts_made, 1)

            def split_lo(b, more=0):
                pool.wait_ge(w_hi_ready, b + 1 + more)
                pool.tensor_tensor(w_lo[:, b % 2], w_raw[:, b % RAW_SLOTS], w_hi[:, b % 2].bitcast(F32),
                                   ALU.subtract).then_inc(w_lo_ready, 1)

            split_lo(0)
            split_lo(1)
            with pool.Fori(0, (N_BLOCKS - 2) // RAW_SLOTS) as i:
                for u in range(RAW_SLOTS):
                    split_lo(2 + u, more=RAW_SLOTS * i)

        @block.tensor
        def _(pe):
            tr = nc.tensor.transpose

            def turn_rows(rows, extra, bank_of, landed, waits, done):
                for j in range(KT + 1):
                    waits(j)
                    if j == 0:
                        pe.wait_ge(landed, 32)
                    if j < KT:
                        for t in range(T // P):
                            mm = tr(ps[:, bank_of(j), P * t:P * t + P], rows[:, t, P * j:P * j + P], ident[:, :])
                    else:
                        for k in range(KT):
                            mm = tr(ps[:, bank_of(j), B * k:B * k + B], extra[:, P * k:P * k + P], ident[0:B, 0:B])
                    mm.then_inc(done, 1)

            def x_waits(taken_a, taken_v):
                def waits(j):
                    if j >= 4:
                        pe.wait_ge(taken_a if j % 2 == 0 else taken_v, (j - 4) // 2 + 1)
                return waits

            pe.wait_ge(consts_made, N_CONSTS)
            pe.wait_ge(prm_landed, 16 * (len(VECTORS) + 2))
            for j, n in enumerate((TAPS * NP, P, N_SHIFT)):
                mm = tr(ps[:, 4, P * j:P * j + n], p_rows[0:n, j, :], ident[0:n, 0:n])
            mm.then_inc(prm_turned, 1)
            pe.wait_ge(shift_landed, 16)
            for j in range(N_SHIFT):
                mm = tr(ps[:, 5, B * j:B * j + B], shift_rows[:, P * j:P * j + P], ident[0:B, 0:B])
            mm.then_inc(shift_turned, 1)
            turn_rows(x_tok, xs_tok, lambda j: j % 4, x_landed, x_waits(x_taken_a, x_taken_v), x_turned)
            pe_stats(n_mix, lambda k: h_fm[:, k], model_mean, KT)

            for b in range(5):
                dense(pe, b, b % 2, h_hi, h_lo, taken=b // 2 if b >= 2 else None, x_ready=(n_mix.lo, n_mix.tiles) if b == 0 else None)

            def small(out, lhsT, rhs, start=True, stop=True):
                return nc.tensor.matmul(out, lhsT, rhs, start=start, stop=stop)

            def lora_product(bank, w, x):
                for a in range(2):
                    mm = small(ps[:, bank + a, 0:HALF], w, x[:, a * HALF:(a + 1) * HALF])
                mm.then_inc(lora_mm, 1)

            def step(p, k):
                name, q, _ = STEPS[k]
                if k < 2:
                    pe.wait_ge(fm_ready, p + 1)
                    pe.wait_ge(bonus_taken, p + 1)
                else:
                    upto = k - 1 if k < N_LOCKSTEP else min(k, N_STEPS - 2)
                    pe.wait_ge(step_v, emptied("v", p, upto))
                    pe.wait_ge(step_a, emptied("a", p, upto))
                base = 4 + 2 * q if k < N_LOCKSTEP else 0
                if name == "chain":
                    bank, c = (4, 6)[q % 2], q
                    for h in range(2):
                        r = slice(HS * h, HS * h + HS)
                        mm = small(ps[r, bank, 0:HS], wg[r, c, HS:2 * HS], s_all[r, c, :])
                    mm.then_inc(step_mm, 1)
                    return
                for j in range(4):
                    c = 4 * q + j
                    for h in range(2):
                        r = slice(HS * h, HS * h + HS)
                        wide = ps[r, base, 2 * HS * j:2 * HS * (j + 1)]
                        one = ps[r, base, HS * j:HS * (j + 1)]
                        if name == "gram_b":
                            mm = small(wide, bi[r, c, 0, :], ar[r, c, :, :])
                        elif name == "gram_k":
                            mm = small(wide, kt_fm[r, c, :], ar[r, c, :, :])
                        elif name == "gram_a":
                            mm = small(wide, ar[r, c, 0, :], bi[r, c, :, :])
                        elif name == "tok_kv":
                            small(wide[:, 0:HS], kh_fm[r, c, :], stack_id[r, :])
                            mm = small(wide[:, HS:2 * HS], xs[r, 2, HS * c:HS * (c + 1)], stack_id[r, :])
                        elif name == "tok_b":
                            mm = small(one, bh_fm[r, c, :], stack_id[r, :])
                        elif name == "akv":
                            mm = small(one, g2[r, c, 0:HS], kv_tok[r, c, HS:2 * HS])
                        elif name == "dbl5":
                            mm = small(wide, g1[r, c, 0:HS], axb[r, c, HS:3 * HS])
                        elif name.startswith("dbl"):
                            small(wide, g1[r, c, 0:HS], axb[r, c, HS:3 * HS])
                            other = ps[r, base + 1, 2 * HS * j:2 * HS * (j + 1)]
                            small(other[:, 0:HS], g1[r, c, 0:HS], axb[r, c, 0:HS])
                            mm = small(other[:, HS:2 * HS], axb[r, c, 0:HS], g1[r, c, 0:HS])
                        elif name == "pw":
                            mm = small(wide, axb[r, c, HS:2 * HS], g1[r, c, HS:3 * HS])
                        elif name == "h":
                            small(one, g1[r, c, 2 * HS:3 * HS], axb[r, c, 2 * HS:3 * HS], stop=False)
                            mm = small(one, kv_tok[r, c, 0:HS], kv_tok[r, c, HS:2 * HS], start=False)
                        elif name == "y":
                            out = ps[r, 5 + 2 * q, HS * j:HS * (j + 1)]
                            if c:
                                small(out, s_all[r, c, :], wg[r, c, 0:HS], stop=False)
                            small(out, kv_tok[r, c, HS:2 * HS], g2[r, c, HS:2 * HS], start=(c == 0), stop=False)
                            mm = small(out, axb[r, c, 2 * HS:3 * HS], g1[r, c, HS:2 * HS], start=False)
                mm.then_inc(step_mm, 1)

            pe.wait_ge(lora_landed, 48)
            pe.wait_ge(lora_ready, 2)
            for p in range(NP):
                b0, cols = first_block(p), slice(P * p, P * p + P)
                if p:
                    pe.wait_ge(step_v, emptied("v", p, 0))
                    pe.wait_ge(step_a, emptied("a", p, 0))
                lora_product(4, lora_w[0:HS, cols], lora[0:HS, 0, :])
                lora_product(6, lora_w[HS:P, cols], lora[HS:P, 0, :])
                dense(pe, b0, b0 % 2, h_hi, h_lo, taken=b0 // 2)
                pe.wait_ge(lora_taken, 3 * p + 1)
                lora_product(4, gate_w[:, cols], lora[:, 1, :])
                pe.wait_ge(lora_taken, 3 * p + 2)
                pe.wait_ge(kk_squares, p + 1)
                lora_product(6, head_ones[:, :], tmp1)
                dense(pe, b0 + 1, (b0 + 1) % 2, h_hi, h_lo, taken=(b0 + 1) // 2)
                pe.wait_ge(lora_taken, 3 * p + 3)
                pe.wait_ge(rk_ready, p + 1)
                lora_product(4, head_ones[:, :], tmp2)
                for b in (b0 + 2, b0 + 3):
                    dense(pe, b, b % 2, h_hi, h_lo, taken=b // 2)
                for k in range(N_LOCKSTEP):
                    step(p, k)
                parts = [(b, k) for b in range(b0 + 4, b0 + 7) for k in range(KT)] if p < NP - 1 else []
                for n in range(NC - 1):
                    step(p, N_LOCKSTEP + n)
                    take = parts[len(parts) * n // (NC - 1):len(parts) * (n + 1) // (NC - 1)]
                    for b, k in take:
                        dense(pe, b, b % 2, h_hi, h_lo, kts=1, k0=k, taken=b // 2 if k == 0 else None)
                step(p, N_STEPS - 2)
                step(p, N_STEPS - 1)

            def gate_block(m):
                b = B_GB + m
                dense(pe, b, b % 2, h_hi, h_lo, taken=b // 2)

            gate_block(0)
            pe.wait_ge(step_a, emptied("a", NP, 0))
            pe.wait_ge(step_v, emptied("v", NP, 0))
            pe.wait_ge(mem_landed, 16)
            for k in range(KT):
                for m in range(2):
                    mm = tr(ps[:, 4 + k // 2, MEM * (k % 2) + P * m:MEM * (k % 2) + P * m + P],
                            mem_tok[:, m, P * k:P * k + P], ident[:, :])
            mm.then_inc(mem_turned, 1)
            gate_block(1)
            pe.wait_ge(mem_taken, 1)
            pe.wait_ge(vec_ready, 1)
            for v in range(4):
                for p in range(NP):
                    mm = tr(ps[0:B, 4 + v, P * p:P * p + P], s_vec[:, v, p, :], ident[:, :])
            mm.then_inc(vec_turned, 1)
            gate_block(2)
            pe.wait_ge(vec_taken, 1)
            for v in range(2):
                for p in range(NP):
                    mm = tr(ps[0:B, 4 + v, P * p:P * p + P], s_vec[:, 4 + v, p, :], ident[:, :])
            mm.then_inc(vec_turned, 1)
            pe_stats(n_mem, lambda k: v_fm[:, k], model_mean, KT, width=MEM, parts=1)
            gate_block(3)
            pe.wait_ge(win_landed, 32)
            for j in range(2):
                if j == 1:
                    pe.wait_ge(n_mem.rsqrt, n_mem.turn + 1)
                for c in range(NP):
                    mm = tr(ps[:, 7 - j, 120 * c:120 * c + 120], win_rows[:, j, P * c:P * c + P], ident[0:120, 0:120])
            mm.then_inc(win_turned, 1)
            for m in range(4, 7):
                gate_block(m)
            pe.wait_ge(vec_taken, 2)
            pe.wait_ge(conv_ready, 1)
            for c in range(NP):
                for a in range(2):
                    mm = small(ps[:, 4 + a, 0:HALF], conv_mean[:, :], conv_y[:, c, a * HALF:(a + 1) * HALF],
                               start=(c == 0), stop=(c == NP - 1))
            mm.then_inc(ln_mean, 1)
            gate_block(7)
            for c in range(NP):
                pe.wait_ge(ln_squares, c + 1)
                for a in range(2):
                    mm = small(ps[:, 6 + a, 0:HALF], conv_mean[:, :], ln_buf(c)[:, a * HALF:(a + 1) * HALF],
                               start=(c == 0), stop=(c == NP - 1))
                mm.then_inc(ln_var, 1)

            def head_stat(j, src, matrix, done):
                for a in range(2):
                    mm = small(ps[:, 4 + 2 * (j % 2) + a, 0:HALF], matrix, src[:, a * HALF:(a + 1) * HALF])
                mm.then_inc(done, 1)

            def gn_mean(j):
                if j == 0:
                    pe.wait_ge(y_ready, 1)
                    pe.wait_ge(ln_rsqrt, 1)
                if j >= 2:
                    pe.wait_ge(gn_rsqrt, j - 1)
                head_stat(j, y_fm[:, j], head_mean[:, :], gn_mean_mm)

            def gn_var(j):
                pe.wait_ge(gn_squares, j + 1)
                head_stat(j, ln_buf(j), head_mean[:, :], gn_var_mm)

            def key_block(m):
                b = B_K + m
                dense(pe, b, b % 2, m_hi, m_lo, width=MEM, parts=1, taken=b // 2, x_ready=(n_mem.lo, n_mem.tiles) if m == 0 else None)

            key_block(0)
            key_block(1)
            pe.wait_ge(y_landed, 16)
            for p in range(NP):
                mm = tr(ps[:, 4, B * p:B * p + B], y_rows[:, P * p:P * p + P], ident[0:B, 0:B])
            mm.then_inc(y_turned, 1)
            key_block(2)
            gn_mean(0)
            gn_mean(1)
            key_block(3)
            gn_var(0)
            key_block(4)
            gn_mean(2)
            gn_var(1)
            key_block(5)
            gn_mean(3)
            gn_var(2)
            key_block(6)
            gn_var(3)
            key_block(7)
            with pe.Fori(0, KT // 4) as i:
                for u in range(4):
                    b = B_V + u
                    dense(pe, b, b % 2, m_hi, m_lo, width=MEM, parts=1, taken=b // 2 + 2 * i, more=4 * i)
            pe.wait_ge(out_taken[1], B_MIX // 2)
            pe.wait_ge(out_taken[0], B_MIX // 2)
            pe.wait_ge(gn_rsqrt, NP)
            for src, which in ((kt, 0), (v_fm, 1)):
                if which:
                    pe.wait_ge(k_tok_ready, 1)
                for m in range(2):
                    for k in range(KT):
                        at = KT * m + k
                        mm = tr(ps[:, 4 + at // 4, P * (at % 4):P * (at % 4) + P], src[:, k, P * m:P * m + P],
                                ident[:, :])
                mm.then_inc(mem_back, 1)

            pe.wait_ge(conv_lo, NP)
            pe.wait_ge(rwkv_lo, NP)
            with pe.Fori(0, KT // 2) as i:
                for u in range(4):
                    b = B_MIX + u
                    dense(pe, b, b % 2, h_hi, h_lo, kts=KT // 2, x0=NP * (u % 2), taken=b // 2 + 2 * i, more=4 * i)

            def post_stats(post):
                pe.wait_ge(post.added, post.tiles + KT)
                for a in range(2):
                    mm = small(ps[:, 6 + a, 0:HALF], model_mean[:, :], sq_acc[:, a * HALF:(a + 1) * HALF])
                mm.then_inc(post.stats, 1)

            def next_stats(post, norm):
                pe.wait_ge(post.rsqrt, post.turn + 1)
                pe_stats(norm, lambda k: y_buf[:, k], model_mean, KT)

            for m in range(KT):
                b = B_OUT + m
                dense(pe, b, b % 2, h_hi, h_lo, taken=b // 2, x_ready=(mixed_lo, 0) if m == 0 else None)
                if m == 3:
                    pe.wait_ge(v_tok_ready, 1)
                    turn_rows(x_tok2, xs_tok2, lambda j: 4 + j % 4, x2_landed, x_waits(x2_taken_a, x2_taken_v),
                              x2_turned)
            pe.wait_ge(x2_taken_v, 4)
            post_stats(p_mix)
            next_stats(p_mix, n_x)
            for m in range(KT):
                b = B_Q + m
                dense(pe, b, b % 2, h_hi, h_lo, taken=b // 2, x_ready=(n_x.lo, n_x.tiles) if m == 0 else None)

            pe.wait_ge(out_taken[0], B_O // 2)
            pe.wait_ge(out_taken[1], B_O // 2)
            for k in range(KT):
                mm = tr(ps[0:B, k // 4, P * (k % 4):P * (k % 4) + P], y_buf[:, k, T:NT], ident[:, :])
            mm.then_inc(q_turned, 1)
            pe.wait_ge(n_x.rsqrt, n_x.turn + 1)

            def scores(h):
                if h >= 2:
                    pe.wait_ge(attn_exp, 4 * (h - 1))
                for t in range(T // P):
                    for d in range(2):
                        mm = small(ps[:, 4 + 2 * (h % 2) + t // 2, MEM * (t % 2):MEM * (t % 2 + 1)],
                                   y_buf[:, 2 * h + d, P * t:P * t + P], kt[:, 2 * h + d, :],
                                   start=(d == 0), stop=(d == 1))
                    mm.then_inc(score_mm, 1)

            def turn_probs(h):
                pe.wait_ge(prob_ready, h + 1)
                (pe.wait_ge(prob_t_ready, h) if h else pe.wait_ge(q_taken, 1))
                for t in range(T // P):
                    for m in range(2):
                        mm = tr(ps[:, m, P * t:P * t + P], prob[:, t, P * m:P * m + P], ident[:, :])
                mm.then_inc(prob_turned, 1)

            def weigh(h):
                pe.wait_ge(prob_t_ready, h + 1)
                if h:
                    pe.wait_ge(o_lo, h)
                for d in range(2):
                    for m in range(2):
                        mm = small(ps[:, 2 + d, :], v_tok[:, m, XHD * h + P * d:XHD * h + P * d + P], prob_t[:, m, :],
                                   start=(m == 0), stop=(m == 1))
                mm.then_inc(weighed, 1)

            scores(0)
            scores(1)
            for h in range(XH):
                turn_probs(h)
                weigh(h)
                if h + 2 < XH:
                    scores(h + 2)
            pe.wait_ge(k_used, 2 * B)
            pe.wait_ge(attn_exp, 4 * XH)
            for m in range(2):
                mm = tr(ps[0:B * XH, 4, P * m:P * m + P], sc[:, m, :], ident[:, :])
            mm.then_inc(sc_turned, 1)
            pe.wait_ge(prob_s_ready, 1)
            for m in range(2):
                mm = tr(ps[:, 5, B * XH * m:B * XH * (m + 1)], prob_s[:, P * m:P * m + P], ident[0:B * XH, 0:B * XH])
            mm.then_inc(prob_s_turned, 1)
            pe.wait_ge(prob_z_ready, 1)
            for b in range(B):
                for m in range(2):
                    t = 2 * B + 2 * b + m
                    pe.wait_ge(cache_landed[t % CACHE_SLOTS], 16 * (t // CACHE_SLOTS + 1))
                    for a in range(2):
                        mm = small(ps[0:B * XH, 6 + a, :], prob_z[:, m, B * XH * b:B * XH * (b + 1)],
                                   cache[:, t % CACHE_SLOTS, 512 * a:512 * (a + 1)],
                                   start=(b == 0 and m == 0), stop=(b == B - 1 and m == 1))
                    mm.then_inc(v_used, 1)
            pe.wait_ge(o_picked, 1)
            for d in range(2):
                mm = tr(ps[:, 4, B * XH * d:B * XH * (d + 1)], o_pick[:, P * d:P * d + P], ident[0:B * XH, 0:B * XH])
            mm.then_inc(o_turned, 1)

            pe.wait_ge(o_lo, XH + 1)
            for m in range(KT):
                b = B_O + m
                dense(pe, b, b % 2, h_hi, h_lo, taken=b // 2)
                if m == 0:
                    for j in range(N_SHIFT):
                        mm = tr(ps[0:1 + B, 4 + j // 4, P * (j % 4):P * (j % 4) + P], p_last[:, j, :], ident[:, :])
                    mm.then_inc(state_turned, 1)
                if m == 1:
                    pe.wait_ge(shift_taken, 1)
                    for c in range(NP):
                        tr(ps[0:TAPS - 1, 4, P * c:P * c + P], glu_last[:, c, :], ident[:, :])
                        tr(ps[0:B, 5, P * c:P * c + P], glu_s[:, c, :], ident[:, :])
                        mm = tr(ps[0:HS, 6, P * c:P * c + P], s_final[:, c, :], ident[:, :])
                    mm.then_inc(state_turned, 1)
            pe.wait_ge(state_taken, 1)
            post_stats(p_x)
            next_stats(p_x, n_ffn)

            pe.wait_ge(n_ffn.lo, n_ffn.tiles + KT)
            with pe.Fori(0, FT // 2) as i:
                for u in range(4):
                    b = B_UP + u
                    dense(pe, b, b % 2, h_hi, h_lo, taken=b // 2 + 2 * i, more=4 * i)
            pe.wait_ge(f_lo_ready, FT)
            with pe.Fori(0, KT // 4) as i:
                for u in range(12):
                    b, o = B_DOWN + u, B_DOWN + u // 3
                    dense(pe, b, o % 2, f_hi, f_lo, kts=DOWN_KT[u % 3], x0=sum(DOWN_KT[:u % 3]), first=(u % 3 == 0),
                          last=(u % 3 == 2), taken=o // 2 + 2 * i if u % 3 == 0 else None, more=12 * i)
            post_stats(p_ffn)
            pe.wait_ge(p_ffn.x_ready, p_ffn.tiles + KT)
            for j in range(T // P + 1):
                for k in range(KT):
                    if j < T // P:
                        bank = 2 * j + k // 4
                        mm = tr(ps[:, bank, P * (k % 4):P * (k % 4) + P], x_res[:, k, P * j:P * j + P], ident[:, :])
                    else:
                        if k == 0:
                            pe.wait_ge(y_turn_a, 1)
                        mm = tr(ps[0:B, k // 4, P * (k % 4):P * (k % 4) + P], x_res[:, k, T:NT], ident[:, :])
                mm.then_inc(y_turns, 1)

        @block.scalar
        def _(act):
            go = nc.scalar.activation
            act.dma_start(x_tok[:, :, :], A["x_prompt"][0].rearrange("(t p) d -> p t d", p=P)).then_inc(x_landed, 16)
            act.dma_start(xs_tok[:, :], A["x_sample"][:, 0, :]).then_inc(x_landed, 16)
            at = 0
            for name, rows in VECTORS:
                src = A[name][0]
                src = src if name == "r_k" else src.rearrange("(r p) -> r p", p=P)
                src = src.rearrange("(r h) n -> r (h n)", h=2) if name == "r_k" else src
                act.dma_start(p_rows[at:at + rows, 1, :], src).then_inc(prm_landed, 16)
                at += rows
            assert at == P
            act.dma_start(p_rows[0:N_SHIFT, 2, :], A["tshift_mu"][0].rearrange("(r p) -> r p", p=P)
                          ).then_inc(prm_landed, 16)
            act.dma_start(p_rows[0:TAPS * NP, 0, :], A["conv_w"][0].rearrange("t (c p) -> (t c) p", p=P)
                          ).then_inc(prm_landed, 16)
            act.dma_start(shift_rows[:, :], A["state_shift"][0]).then_inc(shift_landed, 16)
            act.dma_start(o_conv_s[0][:, 0:TAPS - 2, :], A["state_conv"][0][:, 1:TAPS - 1, :]).then_inc(state_stored, 16)
            for j in range(0, KT, 2):
                act.wait_ge(x_turned, j + 1)
                go(x_fm[:, j, 0:T], ps[:, j % 4, :], ACT.Copy).then_inc(x_taken_a, 1)
            act.wait_ge(x_turned, KT + 1)
            go(x_fm[:, :, T:NT], ps[:, 0, 0:KT * B].rearrange("p (k b) -> p k b", b=B), ACT.Copy).then_inc(x_taken_a, 1)
            act.wait_ge(x_taken_a, KT // 2 + 1)
            act.wait_ge(x_taken_v, KT // 2)
            for k in range(KT):
                go(h_fm[:, k], x_fm[:, k], ACT.Square).then_inc(n_mix.squares, 1)
            split_hi(0)
            act_rsqrt(n_mix, two(rs[:, :]), ps[:, 6:8, 0:HALF], eps[:, 0:1])
            act_split(n_mix, h_fm, h_hi)
            act.wait_ge(n_mix.lo, n_mix.tiles + KT)
            act.dma_start(lora_w[0:HS, :], A["decay_w2"][0]).then_inc(lora_landed, 16)
            act.dma_start(lora_w[HS:P, :], A["iclr_a2"][0]).then_inc(lora_landed, 16)
            act.dma_start(gate_w[:, :], A["gate_g2"][0]).then_inc(lora_landed, 16)
            act.wait_ge(pair_consts, 1)
            act.wait_ge(prm_ready, 1)

            def tile_out(b, j, tile):
                act.wait_ge(block_done, b + 1)
                go(two(p_ext[:, j, 1:1 + NT]), out_view(b % 2), ACT.Copy).then_inc(out_taken[b % 2], 1)
                act.wait_ge(out_taken[b % 2], b // 2 + 1)
                go(p_last[:, tile, :], p_ext[:, j, T:1 + NT], ACT.Copy).then_inc(tile_ready, 1)

            for b in range(5):
                split_hi(b + 1)
                if b == 2:
                    act.wait_ge(lora_in, 1)
                tile_out(b, (0, 1, 0, 1, 2)[b], (12, 13, 0, 4, 8)[b])
                if b == 2:
                    go(lora[0:HS, 0], lora[0:HS, 0], ACT.Tanh).then_inc(lora_ready, 1)
                    go(lora[:, 1], lora[:, 1], ACT.Sigmoid).then_inc(lora_ready, 1)

            def gate_out(b, dst, col):
                act.wait_ge(block_done, b + 1)
                go(two(dst), out_view(b % 2), ACT.Sigmoid, bias=col).then_inc(out_taken[b % 2], 1)

            def step_out(p, k):
                name, q, engines = STEPS[k]
                if "a" not in engines:
                    return
                act.wait_ge(step_mm, N_STEPS * p + k + 1)
                cs, base = slice(4 * q, 4 * q + 4), 4 + 2 * q
                wide = ps[:, base, :].rearrange("p (c n) -> p c n", c=4)
                one = ps[:, base, 0:4 * HS].rearrange("p (c n) -> p c n", c=4)
                if name == "tok_kv":
                    ins = go(kv_tok[:, cs, :], wide, ACT.Copy)
                elif name == "tok_b":
                    ins = go(g1[:, cs, 2 * HS:3 * HS], one, ACT.Copy)
                elif name == "akv":
                    ins = go(axb[:, cs, 2 * HS:3 * HS], one, ACT.Copy)
                elif name.startswith("dbl"):
                    other = ps[:, base + 1, :].rearrange("p (c n) -> p c n", c=4)
                    go(axb[:, cs, 0:HS], other[:, :, 0:HS], ACT.Copy)
                    ins = go(g1[:, cs, 0:HS], other[:, :, HS:2 * HS], ACT.Copy)
                elif name == "h":
                    if q == 0:
                        go(s_all[:, 1, :], ps[:, base, 0:HS], ACT.Copy)
                    ins = go(h_add[:, cs, :], one, ACT.Copy)
                elif name == "y":
                    ins = go(y_fm[:, p, 4 * HS * q:4 * HS * (q + 1)], ps[:, 5 + 2 * q, 0:4 * HS], ACT.Copy)
                ins.then_inc(step_a, 1)

            for p in range(NP):
                b0 = first_block(p)
                act.wait_ge(lora_mm, 5 * p + 1)
                if p:
                    act.wait_ge(fm_ready, p)
                go(two(sig[:, :]), ps[:, 4:6, 0:HALF], ACT.Sigmoid, bias=prm_col("decay_w0", p)).then_inc(lora_taken, 1)
                act.wait_ge(lora_mm, 5 * p + 2)
                go(two(iclr[:, :]), ps[:, 6:8, 0:HALF], ACT.Sigmoid, bias=prm_col("iclr_a0", p)).then_inc(lora_taken, 1)
                split_hi(b0 + 1)
                act.wait_ge(xs_ready, p + 1)
                go(tmp1[:, :], xs[:, 1], ACT.Square, scale=prm_col("k_k", p)).then_inc(kk_squares, 1)
                act.wait_ge(lora_mm, 5 * p + 3)
                go(two(g_fm[:, p]), ps[:, 4:6, 0:HALF], ACT.Copy).then_inc(lora_taken, 1)
                if p:
                    act.wait_ge(val_taken, p)
                gate_out(b0, glu_sig[:, :], prm_col("glu_b", NP + p))
                act.wait_ge(out_taken[b0 % 2], b0 // 2 + 1)
                split_hi(b0 + 2)
                act.wait_ge(kk_max, p + 1)
                link_a(go(kkn[:, :], kkn[:, :], ACT.Ln, scale=LN_SCALE))
                go(kkn[:, :], kkn[:, :], ACT.Exp, scale=-0.5, bias=eps[:, 3:4]).then_inc(kk_rsqrt, 1)
                act.wait_ge(cum_ready, p + 1)
                go(e_dec[:, :], cum[:, :], ACT.Exp, scale=DECAY)
                go(sig[:, 0:T], sig[:, 0:T], ACT.Exp, scale=DECAY)
                link_a(go(s_vec[:, 4, p, :], sig[:, T:NT], ACT.Exp, scale=DECAY))
                go(cum[:, :], cum[:, :], ACT.Exp, scale=-DECAY).then_inc(decays_ready, 1)
                split_hi(b0 + 3)
                gate_out(b0 + 2, gate_a[:, 2 * p], prm_col("merge_gate_b", 2 * p))
                split_hi(b0 + 4)
                gate_out(b0 + 3, gate_a[:, 2 * p + 1], prm_col("merge_gate_b", 2 * p + 1))
                if p < NP - 1:
                    split_hi(b0 + 5)
                for k in range(N_LOCKSTEP):
                    step_out(p, k)
                if p < NP - 1:
                    for j in range(3):
                        tile_out(b0 + 4 + j, j, NP * j + p + 1)
                        if j < 2:
                            split_hi(b0 + 6 + j)
                for k in range(N_LOCKSTEP, N_STEPS):
                    step_out(p, k)

            def gate_b_out(m):
                gate_out(B_GB + m, gate_b[:, m], prm_col("merge_gate_b", KT + m))

            act.wait_ge(block_done, B_GB)
            act.wait_ge(step_mm, NP * N_STEPS)
            act.wait_ge(step_v, emptied("v", NP, 0))
            act.wait_ge(step_a, emptied("a", NP, 0))
            act.dma_start(mem_tok[:, :, :], A["mem_prompt"][0].rearrange("(m p) d -> p m d", p=P)
                          ).then_inc(mem_landed, 16)
            for j in range(2):
                act.dma_start(win_rows[:, j, :], A["state_conv"][0][4 * j:4 * j + 4].rearrange("b t c -> (b t) c")
                              ).then_inc(win_landed, 16)
            split_hi(B_GB + 1)
            gate_b_out(0)
            split_hi(B_GB + 2)
            act.wait_ge(mem_turned, 1)
            go(mem_fm[:, :, :], ps[:, 4:8, :].rearrange("p b (k n) -> p (b k) n", k=2), ACT.Copy).then_inc(mem_taken, 1)
            act.wait_ge(mem_taken, 1)
            for k in range(KT):
                go(v_fm[:, k], mem_fm[:, k], ACT.Square).then_inc(n_mem.squares, 1)
            gate_b_out(1)
            split_hi(B_GB + 3)
            act.wait_ge(vec_turned, 1)
            go(vt1[:, :, :], ps[0:B, 4:8, :], ACT.Copy).then_inc(vec_taken, 1)
            act.wait_ge(vec_taken, 1)
            act.dma_start(vec_scratch[0:4].rearrange("v b c -> b v c"), vt1[:, :, :]).then_inc(vec_stored, 16)
            gate_b_out(2)
            split_hi(B_GB + 4)
            act.wait_ge(vec_turned, 2)
            go(vt2[:, :, :], ps[0:B, 4:6, :], ACT.Copy).then_inc(vec_taken, 1)
            act.wait_ge(vec_taken, 2)
            act.dma_start(vec_scratch[4:6].rearrange("v b c -> b v c"), vt2[:, :, :]).then_inc(vec_stored, 16)
            act_rsqrt(n_mem, rs[:, 0:MEM], ps[:, 6, 0:MEM], eps[:, 0:1])
            act.wait_ge(vec_stored, 32)
            act.dma_start(ss[:, :, :], A["state_rwkv"][0].rearrange("b h (g i) j -> (b h g) i j", g=2)
                          ).then_inc(ss_landed, 16)
            for g in range(2):
                act.dma_start(vs[g:P:2, :, :], vec_scratch[0:5].rearrange("v b (h j) -> (b h) v j", j=HS)
                              ).then_inc(ss_landed, 16)
            act.dma_start(vs_v[:, :], vec_scratch[5].rearrange("b (h i) -> (b h) i", i=HS // 2)).then_inc(ss_landed, 16)
            act_split(n_mem, v_fm, m_hi)
            for m in range(3, 6):
                gate_b_out(m)
                split_hi(B_GB + m + 2)
            gate_b_out(6)
            split_hi(B_GB + 8)
            gate_b_out(7)
            split_hi(B_GB + 9)
            for c in range(NP):
                act.wait_ge(ln_centred, c + 1)
                if c >= 2:
                    act.wait_ge(ln_var, c - 1)
                go(ln_buf(c), conv_y[:, c], ACT.Square).then_inc(ln_squares, 1)
            act.wait_ge(ln_var, NP)
            act.wait_ge(n_mem.lo, n_mem.tiles + KT)
            link_a(go(two(rs[:, :]), ps[:, 6:8, 0:HALF], ACT.Ln, bias=eps[:, 2:3]))
            go(rs[:, :], rs[:, :], ACT.Exp, scale=-0.5).then_inc(ln_rsqrt, 1)

            def key_out(m):
                b = B_K + m
                act.wait_ge(block_done, b + 1)
                go(kt[:, m], ps[:, 2 * (b % 2), 0:MEM], ACT.Copy).then_inc(out_taken[b % 2], 1)

            key_out(0)
            split_hi(B_K + 2)
            for c in range(NP):
                act.wait_ge(conv_scaled, c + 1)
                go(conv_y[:, c], conv_y[:, c], ACT.Silu, bias=prm_col("conv_ln_b", c)).then_inc(conv_silu, 1)
            act.wait_ge(conv_silu, NP)
            for c in range(NP):
                go(h_hi[:, c], conv_y[:, c], ACT.Copy).then_inc(conv_hi, 1)
            key_out(1)
            split_hi(B_K + 3)
            act.wait_ge(ys_made, 1)
            act.dma_start(y_scratch.rearrange("b (h i) -> (b h) i", i=HS // 2), vs_y[:, :]).then_inc(ys_stored, 16)
            act.dma_start(o_rwkv_s[0].rearrange("b h (g i) j -> (b h g) i j", g=2), ss[:, :, :]).then_inc(ss_stored, 16)
            act.wait_ge(ys_stored, 16)
            act.dma_start(y_rows[:, :], y_scratch).then_inc(y_landed, 16)

            def gn_square(j):
                act.wait_ge(gn_centred, j + 1)
                go(ln_buf(j), y_fm[:, j], ACT.Square).then_inc(gn_squares, 1)

            def gn_root(j):
                act.wait_ge(gn_var_mm, j + 1)
                link_a(go(two(ln_buf(j)), ps[:, 4 + 2 * (j % 2):6 + 2 * (j % 2), 0:HALF], ACT.Ln, bias=eps[:, 1:2]))
                go(ln_buf(j), ln_buf(j), ACT.Exp, scale=-0.5).then_inc(gn_rsqrt, 1)

            key_out(2)
            split_hi(B_K + 4)
            gn_square(0)
            gn_square(1)
            key_out(3)
            split_hi(B_K + 5)
            gn_root(0)
            key_out(4)
            split_hi(B_K + 6)
            gn_root(1)
            act.wait_ge(gn_scaled, 1)
            gn_square(2)
            key_out(5)
            split_hi(B_K + 7)
            act.wait_ge(gn_scaled, 2)
            gn_root(2)
            gn_square(3)
            key_out(6)
            split_hi(B_K + 8)
            gn_root(3)
            for j in range(NP):
                act.wait_ge(rwkv_made, j + 1)
                go(h_hi[:, NP + j], y_fm[:, j], ACT.Copy).then_inc(rwkv_hi, 1)
            key_out(7)
            with act.Fori(0, KT // 4) as i:
                for u in range(4):
                    b = B_V + u
                    split_hi(b + 1, more=4 * i, more4=i)
                    act.wait_ge(block_done, b + 1 + 4 * i)
                    go(v_fm[:, bass.ds(4 * i + u, 1)], ps[:, 2 * (b % 2), 0:MEM], ACT.Copy).then_inc(out_taken[b % 2], 1)
            act.wait_ge(ss_stored, 16)
            act.wait_ge(mem_back, 1)
            go(k_tok[:, :, :].rearrange("p m d -> p (m d)"), ps[:, 4:8, :].rearrange("p b n -> p (b n)"), ACT.Copy
               ).then_inc(k_tok_ready, 1)
            act.wait_ge(k_tok_ready, 1)
            act.dma_start(o_memk[0, 0].rearrange("(m p) h d -> p m (h d)", p=P), k_tok[:, :, :]).then_inc(mem_stored, 16)
            with act.Fori(0, KT // 2) as i:
                for u in range(4):
                    split_hi(B_MIX + 1 + u, more=4 * i, more4=i)
            act.wait_ge(v_tok_ready, 1)
            act.dma_start(o_memv[0, 0].rearrange("(m p) h d -> p m (h d)", p=P), v_tok[:, :, :]).then_inc(mem_stored, 16)
            act.wait_ge(block_done, B_OUT)
            for m in range(KT):
                act.wait_ge(merged, m + 1)
                go(h_hi[:, m], gate_b[:, m], ACT.Copy).then_inc(mixed_hi, 1)
            act.wait_ge(mixed_lo, KT)
            act.dma_start(x_tok2[:, :, :], A["x_prompt"][0].rearrange("(t p) d -> p t d", p=P)).then_inc(x2_landed, 16)
            act.dma_start(xs_tok2[:, :], A["x_sample"][:, 0, :]).then_inc(x2_landed, 16)

            def post_square(post, o, done, m):
                act.wait_ge(block_done, done)
                if m >= 2:
                    act.wait_ge(post.added, post.tiles + m - 1)
                go(two(sq_tmp[:, m % 2]), out_view(o % 2), ACT.Square).then_inc(post.squares, 1)

            def x_squares(post, norm):
                for k in range(KT):
                    act.wait_ge(post.x_ready, post.tiles + k + 1)
                    go(y_buf[:, k], x_res[:, k], ACT.Square).then_inc(norm.squares, 1)

            for m in range(KT):
                split_hi(B_OUT + m + 1)
                post_square(p_mix, B_OUT + m, B_OUT + m + 1, m)
                if m == 3:
                    for j in range(0, KT + 1, 2):
                        act.wait_ge(x2_turned, j + 1)
                        if j < KT:
                            ins = go(x_res[:, j, 0:T], ps[:, 4 + j % 4, :], ACT.Copy)
                        else:
                            ins = go(x_res[:, :, T:NT], ps[:, 4, 0:KT * B].rearrange("p (k b) -> p k b", b=B), ACT.Copy)
                        ins.then_inc(x2_taken_a, 1)
            act_rsqrt(p_mix, two(rs[:, :]), ps[:, 6:8, 0:HALF], eps[:, 0:1])
            x_squares(p_mix, n_x)
            act_rsqrt(n_x, two(rs[:, :]), ps[:, 6:8, 0:HALF], eps[:, 0:1])
            act_split(n_x, y_buf, h_hi)
            with act.Fori(0, KT // 4) as i:
                for u in range(4):
                    b = B_Q + u
                    split_hi(b + 1, more=4 * i, more4=i)
                    act.wait_ge(block_done, b + 1 + 4 * i)
                    go(y_buf[:, bass.ds(4 * i + u, 1)].rearrange("p o (a b) -> p (o a) b", a=2), out_view(b % 2), ACT.Copy
                       ).then_inc(out_taken[b % 2], 1)

            act.wait_ge(q_turned, 1)
            go(q_tok[:, :], ps[0:B, 0:2, :].rearrange("p a n -> p (a n)"), ACT.Copy).then_inc(q_taken, 1)

            def exps(h):
                act.wait_ge(attn_max, h + 1)
                if h:
                    act.wait_ge(prob_turned, h)
                for t in range(T // P):
                    j = 4 * h + t
                    go(prob[:, t], ps[:, 4 + 2 * (h % 2) + t // 2, MEM * (t % 2):MEM * (t % 2 + 1)], ACT.Exp,
                       scale=XHD ** -0.5, bias=stat[:, 0, j:j + 1], accum_out=stat[:, 1, j:j + 1]).then_inc(attn_exp, 1)

            def take_prob_t(h):
                act.wait_ge(prob_turned, h + 1)
                if h:
                    act.wait_ge(weighed, h)
                go(prob_t[:, :, :], ps[:, 0:2, :], ACT.Copy).then_inc(prob_t_ready, 1)

            def o_high(h):
                act.wait_ge(weighed, h + 1)
                go(h_hi[:, 2 * h:2 * h + 2, 0:T], ps[:, 2:4, :], ACT.Copy).then_inc(o_hi, 1)

            exps(0)
            take_prob_t(0)
            for h in range(1, XH):
                exps(h)
                o_high(h - 1)
                take_prob_t(h)
            o_high(XH - 1)
            act.wait_ge(sc_max, 1)
            go(prob_s[:, :], ps[0:B * XH, 4, 0:MEM], ACT.Exp, scale=XHD ** -0.5, bias=stat_s[:, 0:1],
               accum_out=stat_s[:, 1:2]).then_inc(sc_exp, 1)
            act.wait_ge(o_turned, 1)
            for d in range(2):
                ins = go(h_hi[:, d:KT:2, T:NT],
                         ps[:, 4, B * XH * d:B * XH * (d + 1)].rearrange("p (b h) -> p h b", b=B), ACT.Copy)
            ins.then_inc(o_hi, 1)

            for m in range(KT):
                split_hi(B_O + m + 1)
                if m == 1:
                    act.wait_ge(state_turned, 1)
                    go(shift_out[:, :, :], ps[0:1 + B, 4:8, :].rearrange("p b (j n) -> p (b j) n", n=P)[:, 0:N_SHIFT],
                       ACT.Copy).then_inc(shift_taken, 1)
                post_square(p_x, B_O + m, B_O + m + 1, m)
                if m == 2:
                    act.wait_ge(state_turned, 2)
                    go(conv_out[:, :], ps[0:TAPS - 1, 4, :], ACT.Copy)
                    go(glu_out[:, :], ps[0:B, 5, :], ACT.Copy)
                    go(rwkv_out[:, :, :], ps[0:HS, 6, :].rearrange("p (j n) -> p j n", j=NP), ACT.Copy
                       ).then_inc(state_taken, 1)
                    act.wait_ge(state_taken, 1)
                    act.wait_ge(shift_taken, 1)
                    act.dma_start(o_shift_p[0], shift_out[0:1].rearrange("p j n -> p (j n)")).then_inc(state_stored, 16)
                    act.dma_start(o_shift_s[0], shift_out[1:1 + B].rearrange("p j n -> p (j n)")).then_inc(state_stored, 16)
                    act.dma_start(o_conv_p[0, 0], conv_out[:, :]).then_inc(state_stored, 16)
                    act.dma_start(o_conv_s[0][:, TAPS - 2, :], glu_out[:, :]).then_inc(state_stored, 16)
                    act.dma_start(o_rwkv_p[0, 0].rearrange("(p g) i j -> i p g j", g=2),
                                  rwkv_out[:, :, :].rearrange("i p (g j) -> i p g j", g=2)).then_inc(state_stored, 16)
            act_rsqrt(p_x, two(rs[:, :]), ps[:, 6:8, 0:HALF], eps[:, 0:1])
            x_squares(p_x, n_ffn)
            act_rsqrt(n_ffn, two(rs[:, :]), ps[:, 6:8, 0:HALF], eps[:, 0:1])
            act_split(n_ffn, y_buf, h_hi)
            act.wait_ge(state_stored, 6 * 16)
            with act.Fori(0, FT // 2) as i:
                for u in range(4):
                    b, j = B_UP + u, u // 2
                    split_hi(b + 1, more=4 * i, more4=i)
                    if u % 2 == 0:
                        act.wait_ge(block_done, b + 1 + 4 * i)
                        go(two(silu[:, :]), out_view(0), ACT.Silu).then_inc(out_taken[0], 1)
                    else:
                        act.wait_ge(out_taken[1], B_UP // 2 + j + 1 + 2 * i)
                        go(f_hi[:, bass.ds(2 * i + j, 1)].rearrange("p o n -> p (o n)"), f_tmp[:, j], ACT.Copy
                           ).then_inc(f_hi_ready, 1)
            for m in range(KT):
                for j in range(3):
                    if B_DOWN + 3 * m + j + 1 < N_BLOCKS:
                        split_hi(B_DOWN + 3 * m + j + 1)
                post_square(p_ffn, B_DOWN + m, B_DOWN + 3 * m + 3, m)
            act_rsqrt(p_ffn, two(rs[:, :]), ps[:, 6:8, 0:HALF], eps[:, 0:1])
            for j in (0, 2):
                act.wait_ge(y_turns, j + 1)
                go(y_tok[:, j].rearrange("p (a n) -> p a n", a=2), ps[:, 2 * j:2 * j + 2, :], ACT.Copy).then_inc(y_turn_a, 1)
            act.wait_ge(y_turns, 5)
            go(ys_tok[:, :].rearrange("p (a n) -> p a n", a=2), ps[0:B, 0:2, :], ACT.Copy).then_inc(y_turn_a, 1)

        @block.vector
        def _(dve):
            V = nc.vector
            stt, tt, ts = V.scalar_tensor_tensor, V.tensor_tensor, V.tensor_scalar
            dve.wait_ge(prm_turned, 1)
            V.tensor_copy(prm[:, 0, 0:TAPS * NP], ps[:, 4, 0:TAPS * NP])
            V.tensor_copy(prm[:, 1, :], ps[:, 4, P:2 * P])
            V.tensor_copy(prm[:, 2, 0:N_SHIFT], ps[:, 4, 2 * P:2 * P + N_SHIFT]).then_inc(prm_ready, 1)
            for j in range(1, KT, 2):
                dve.wait_ge(x_turned, j + 1)
                V.tensor_copy(x_fm[:, j, 0:T], ps[:, j % 4, :]).then_inc(x_taken_v, 1)
            dve.wait_ge(prm_ready, 1)
            dve.wait_ge(x_taken_a, KT // 2 + 1)
            dve.wait_ge(x_taken_v, KT // 2)
            dve_scale_split(n_mix, x_fm, rs[:, :], "g_mix_pre", h_fm, h_lo, h_hi)
            dve.wait_ge(n_mix.lo, n_mix.tiles + KT)
            dve.wait_ge(shift_turned, 1)
            dve.wait_ge(consts_made, N_CONSTS)
            V.tensor_copy(shift_t[:, :, :], ps[:, 5, 0:N_SHIFT * B].rearrange("p (j b) -> p j b", b=B))
            V.memset(p_ext[:, :, 0:1], 0.0)
            V.memset(glu[:, 0:TAPS - 1], 0.0)
            link_v(V.memset(scan_mask[:, :], 1.0))
            V.memset(scan_mask[:, :].rearrange("p (c t) -> p c t", t=HS)[:, :, 0:1], 0.0)
            link_v(V.tensor_copy(bi[:, :, 1, :], stack_id[:, :].unsqueeze(1).to_broadcast([P, NC, HS])))
            V.tensor_copy(eps_copy[:, :], eps[:, :]).then_inc(pair_consts, 1)

            def shift_mix(dst, tiles, prev_s):
                n = len(tiles)
                tt(dst[:, 0:n, 0:T], p_ext[:, 0:n, 0:T], p_ext[:, 0:n, 1:1 + T], ALU.subtract)
                link_v(tt(dst[:, 0:n, T:NT], prev_s, p_ext[:, 0:n, 1 + T:1 + NT], ALU.subtract))
                for j, tile in enumerate(tiles):
                    ins = stt(dst[:, j], dst[:, j], mu_col(tile), p_ext[:, j, 1:1 + NT], ALU.mult, ALU.add)
                return ins

            dve.wait_ge(tile_ready, 2)
            shift_mix(lora, (12, 13), shift_t[:, 12:14, :]).then_inc(lora_in, 1)

            def conv_tap(p, t):
                src, w = glu[:, t:t + T], prm[:, 0, NP * t + p:NP * t + p + 1]
                if t == 0:
                    link_v(ts(conv_y[:, p, 0:T], src, w, prm_col("conv_b", p), ALU.mult, ALU.add))
                else:
                    link_v(stt(conv_y[:, p, 0:T], src, w, conv_y[:, p, 0:T], ALU.mult, ALU.add))

            def step_out(p, k):
                name, q, engines = STEPS[k]
                if "v" not in engines:
                    return
                dve.wait_ge(step_mm, N_STEPS * p + k + 1)
                if name == "chain":
                    tt(s_all[:, q + 1, :], ps[:, (4, 6)[q % 2], 0:HS], h_add[:, q, :], ALU.add).then_inc(step_v, 1)
                    return
                cs, base = slice(4 * q, 4 * q + 4), 4 + 2 * q
                wide = ps[:, base, :].rearrange("p (c n) -> p c n", c=4)
                mask = {"gram_b": mask_s, "gram_k": mask_s, "gram_a": mask_t}.get(name)
                dst = {"gram_b": g1, "gram_k": g2, "gram_a": axb}.get(name)
                if mask is not None:
                    m = mask[:, :, :].rearrange("p a n -> p (a n)").unsqueeze(1).to_broadcast([P, 4, 2 * HS])
                    ins = tt(dst[:, cs, 0:2 * HS], wide, m, ALU.mult)
                elif name.startswith("dbl"):
                    ins = tt(axb[:, cs, HS:3 * HS], wide, axb[:, cs, HS:3 * HS], ALU.add)
                elif name == "pw":
                    tt(wg[:, cs, 0:HS], wide[:, :, 0:HS], ar[:, cs, 1, :], ALU.add)
                    for j in range(4):
                        c = 4 * q + j
                        last = e_dec[:, HS * c + HS - 1:HS * c + HS]
                        ins = stt(wg[:, c, HS:2 * HS], stack_id[:, :], last, wide[:, j, HS:2 * HS], ALU.mult, ALU.add)
                ins.then_inc(step_v, 1)

            def chunks(ap):
                return ap.rearrange("p (c t) -> p c t", t=HS)

            for p in range(NP):
                b0 = first_block(p)
                dve.wait_ge(tile_ready, 2 + 3 * (p + 1))
                if p:
                    dve.wait_ge(step_mm, N_STEPS * p)
                r, k, v = xs[:, 0], xs[:, 1], xs[:, 2]
                shift_mix(xs, (p, NP + p, 2 * NP + p), shift_t[:, p:3 * NP:NP, :]).then_inc(xs_ready, 1)
                dve.wait_ge(lora_taken, 3 * p + 1)
                link_v(V.tensor_tensor_scan(cum[:, :], scan_mask[:, :], sig[:, 0:T], 0.0, ALU.mult, ALU.add))
                tt(sig[:, 0:T], cum[:, :], sig[:, 0:T], ALU.subtract).then_inc(cum_ready, 1)
                dve.wait_ge(lora_taken, 3 * p + 2)
                dve.wait_ge(xs_ready, p + 1)
                link_v(ts(kh[:, :], iclr[:, :], 1.0, prm_col("k_a", p), ALU.subtract, ALU.mult))
                link_v(stt(kh[:, :], kh[:, :], 1.0, k, ALU.add, ALU.mult))
                stt(tmp2[:, :], r, prm_col("r_k", p), kh[:, :], ALU.mult, ALU.mult).then_inc(rk_ready, 1)
                dve.wait_ge(lora_mm, 5 * p + 4)
                ts(two(kkn[:, :]), ps[:, 6:8, 0:HALF], 1e-24, None, ALU.max).then_inc(kk_max, 1)
                dve.wait_ge(kk_rsqrt, p + 1)
                link_v(stt(kkn[:, :], k, prm_col("k_k", p), kkn[:, :], ALU.mult, ALU.mult))
                link_v(tt(tmp1[:, :], kkn[:, :], iclr[:, :], ALU.mult))
                dve.wait_ge(lora_mm, 5 * p + 5)
                tt(two(bonus[:, p]), ps[:, 4:6, 0:HALF], two(v), ALU.mult).then_inc(bonus_taken, 1)
                dve.wait_ge(decays_ready, p + 1)
                stt(ar[:, :, 0, :], chunks(kkn[:, 0:T]), -1.0, chunks(sig[:, 0:T]), ALU.mult, ALU.mult)
                tt(ar[:, :, 1, :], chunks(xs[:, 0, 0:T]), chunks(e_dec[:, :]), ALU.mult)
                tt(bi[:, :, 0, :], chunks(tmp1[:, 0:T]), chunks(cum[:, :]), ALU.mult)
                link_v(tt(kt_fm[:, :, :], chunks(kh[:, 0:T]), chunks(cum[:, :]), ALU.mult))
                whole = chunks(e_dec[:, :])[:, :, HS - 1:HS].to_broadcast([P, NC, HS])
                tt(bh_fm[:, :, :], bi[:, :, 0, :], whole, ALU.mult)
                tt(kh_fm[:, :, :], kt_fm[:, :, :], whole, ALU.mult)
                V.tensor_copy(s_vec[:, 0, p, :], xs[:, 0, T:NT])
                V.tensor_copy(s_vec[:, 1, p, :], kh[:, T:NT])
                ts(s_vec[:, 2, p, :], kkn[:, T:NT], -1.0, None, ALU.mult)
                V.tensor_copy(s_vec[:, 3, p, :], tmp1[:, T:NT])
                V.tensor_copy(s_vec[:, 5, p, :], xs[:, 2, T:NT]).then_inc(fm_ready, 1)
                dve.wait_ge(block_done, b0 + 2)
                dve.wait_ge(out_taken[b0 % 2], b0 // 2 + 1)
                stt(two(glu[:, TAPS - 1:TAPS - 1 + NT]), out_view((b0 + 1) % 2), prm_col("glu_b", p), two(glu_sig[:, :]),
                    ALU.add, ALU.mult).then_inc(out_taken[(b0 + 1) % 2], 1)
                dve.wait_ge(out_taken[(b0 + 1) % 2], (b0 + 1) // 2 + 1)
                V.tensor_copy(glu_last[:, p, :], glu[:, T:T + TAPS - 1])
                link_v(V.tensor_copy(glu_s[:, p, :], glu[:, T + TAPS - 1:]))
                V.tensor_copy(eps_copy[:, :], eps[:, :]).then_inc(val_taken, 1)
                tap = 0
                for n in range(N_LOCKSTEP):
                    step_out(p, n)
                    take = 3 if STEPS[n][0] in ("dbl0", "dbl1", "dbl2", "dbl3", "dbl4") else 1 if n == 0 else 0
                    for t in range(tap, tap + take):
                        conv_tap(p, t)
                    tap += take
                assert tap == TAPS
                for n in range(N_LOCKSTEP, N_STEPS):
                    step_out(p, n)
                dve.wait_ge(step_v, emptied("v", p, N_STEPS))
                link_v(V.tensor_copy(s_final[:, p, :], s_all[:, NC, :]))
            V.tensor_copy(eps_copy[:, :], eps[:, :]).then_inc(vec_ready, 1)

            dve.wait_ge(win_turned, 1)
            for j in range(2):
                V.tensor_copy(win[:, :, 4 * j:4 * j + 4, 0:TAPS - 1],
                              ps[:, 7 - j, 0:480].rearrange("p (c b t) -> p c b t", c=NP, b=4))
            link_v(V.tensor_copy(win[:, :, :, TAPS - 1], glu_s[:, :, :]))
            for c in range(NP):
                w = prm[:, 0, c:NP * TAPS:NP].unsqueeze(1).to_broadcast([P, B, TAPS])
                ins = tt(win[:, c], win[:, c], w, ALU.mult)
            link_v(ins)
            link_v(V.tensor_reduce(conv_y[:, :, T:NT], win[:, :, :, :], AX.X, ALU.add))
            for c in range(NP):
                ins = ts(conv_y[:, c, T:NT], conv_y[:, c, T:NT], prm_col("conv_b", c), None, ALU.add)
            ins.then_inc(conv_ready, 1)
            dve_scale_split(n_mem, mem_fm, rs[:, 0:MEM], "g_mem", v_fm, m_lo, m_hi)
            dve.wait_ge(n_mem.lo, n_mem.tiles + KT)

            def over_i(ap):
                return ap.unsqueeze(1).to_broadcast([P, HS // 2, HS])

            def over_j(ap):
                return ap.unsqueeze(2).to_broadcast([P, HS // 2, HS])

            dve.wait_ge(ss_landed, 64)
            link_v(tt(ss_tmp[:, :, :], ss[:, :, :], over_i(vs[:, 2, :]), ALU.mult))
            link_v(V.tensor_reduce(vs_sa[:, :], ss_tmp[:, :, :], AX.X, ALU.add))
            tt(ss[:, :, :], ss[:, :, :], over_i(vs[:, 4, :]), ALU.mult)
            link_v(tt(ss_tmp[:, :, :], over_j(vs_sa[:, :]), over_i(vs[:, 3, :]), ALU.mult))
            link_v(tt(ss[:, :, :], ss[:, :, :], ss_tmp[:, :, :], ALU.add))
            link_v(tt(ss_tmp[:, :, :], over_j(vs_v[:, :]), over_i(vs[:, 1, :]), ALU.mult))
            link_v(tt(ss[:, :, :], ss[:, :, :], ss_tmp[:, :, :], ALU.add))
            link_v(tt(ss_tmp[:, :, :], ss[:, :, :], over_i(vs[:, 0, :]), ALU.mult))
            V.tensor_reduce(vs_y[:, :], ss_tmp[:, :, :], AX.X, ALU.add).then_inc(ys_made, 1)

            dve.wait_ge(ln_mean, 1)
            for c in range(NP):
                tt(two(conv_y[:, c]), two(conv_y[:, c]), ps[:, 4:6, 0:HALF], ALU.subtract).then_inc(ln_centred, 1)
            dve.wait_ge(ln_rsqrt, 1)
            dve.wait_ge(ln_centred, NP)
            for c in range(NP):
                stt(conv_y[:, c], conv_y[:, c], prm_col("conv_ln_g", c), rs[:, :], ALU.mult, ALU.mult
                    ).then_inc(conv_scaled, 1)
            for c in range(NP):
                dve.wait_ge(conv_hi, c + 1)
                tt(h_lo[:, c], conv_y[:, c], h_hi[:, c].bitcast(F32), ALU.subtract).then_inc(conv_lo, 1)
            dve.wait_ge(y_turned, 1)
            V.tensor_copy(y_fm[:, :, T:NT], ps[:, 4, 0:NP * B].rearrange("p (c b) -> p c b", b=B)).then_inc(y_ready, 1)

            def gn_centre(j):
                dve.wait_ge(gn_mean_mm, j + 1)
                if j == 0:
                    dve.wait_ge(y_ready, 1)
                tt(two(y_fm[:, j]), two(y_fm[:, j]), ps[:, 4 + 2 * (j % 2):6 + 2 * (j % 2), 0:HALF], ALU.subtract
                   ).then_inc(gn_centred, 1)

            def gn_scale(j):
                dve.wait_ge(gn_rsqrt, j + 1)
                dve.wait_ge(gn_centred, j + 1)
                stt(y_fm[:, j], y_fm[:, j], prm_col("lnx_g", j), ln_buf(j), ALU.mult, ALU.mult).then_inc(gn_scaled, 1)
                dve.wait_ge(gn_scaled, j + 1)
                link_v(stt(y_fm[:, j], y_fm[:, j], prm_col("lnx_b", j), bonus[:, j], ALU.add, ALU.add))
                tt(y_fm[:, j], y_fm[:, j], g_fm[:, j], ALU.mult).then_inc(rwkv_made, 1)

            gn_centre(0)
            gn_centre(1)
            gn_scale(0)
            gn_centre(2)
            gn_scale(1)
            gn_centre(3)
            gn_scale(2)
            gn_scale(3)
            for j in range(NP):
                dve.wait_ge(rwkv_hi, j + 1)
                tt(h_lo[:, NP + j], y_fm[:, j], h_hi[:, NP + j].bitcast(F32), ALU.subtract).then_inc(rwkv_lo, 1)
            dve.wait_ge(mem_back, 2)
            V.tensor_copy(v_tok[:, :, :].rearrange("p m d -> p (m d)"), ps[:, 4:8, :].rearrange("p b n -> p (b n)")
                          ).then_inc(v_tok_ready, 1)

            b_pw0 = sum(n for _, n in VECTORS[:[n for n, _ in VECTORS].index("b_pw")])
            with dve.Fori(0, KT // 2) as i:
                for j in range(2):
                    ga = gate_a[:, bass.ds(2 * i + j, 1)].rearrange("p o (a b) -> p (o a) b", a=2)
                    gb = gate_b[:, bass.ds(2 * i + j, 1)].rearrange("p o (a b) -> p (o a) b", a=2)
                    m_no, taken = B_MIX + 2 * j, B_MIX // 2 + j + 1
                    dve.wait_ge(block_done, m_no + 1 + 4 * i)
                    stt(gb, out_view(0), prm[:, 1, bass.ds(2 * i + (b_pw0 + j), 1)], gb, ALU.add, ALU.mult
                        ).then_inc(out_taken[0], 1)
                    dve.wait_ge(block_done, m_no + 2 + 4 * i)
                    tt(ga, out_view(1), ga, ALU.mult).then_inc(out_taken[1], 1)
                    dve.wait_ge(out_taken[0], taken + 2 * i)
                    dve.wait_ge(out_taken[1], taken + 2 * i)
                    tt(gb, ga, gb, ALU.add).then_inc(merged, 1)
            dve.wait_ge(merged, KT)
            for m in range(KT):
                dve.wait_ge(mixed_hi, m + 1)
                tt(h_lo[:, m], gate_b[:, m], h_hi[:, m].bitcast(F32), ALU.subtract).then_inc(mixed_lo, 1)

            def post_take(post, o, m):
                dve.wait_ge(post.squares, post.tiles + m + 1)
                V.tensor_copy(two(y_buf[:, m]), out_view(o % 2)).then_inc(out_taken[o % 2], 1)
                if m:
                    dve.wait_ge(post.added, post.tiles + m)
                    ins = tt(sq_acc[:, :], sq_acc[:, :], sq_tmp[:, m % 2], ALU.add)
                else:
                    ins = V.tensor_copy(sq_acc[:, :], sq_tmp[:, 0])
                ins.then_inc(post.added, 1)

            def post_add(post, gain):
                dve.wait_ge(post.rsqrt, post.turn + 1)
                dve.wait_ge(out_taken[0], post.taken)
                dve.wait_ge(out_taken[1], post.taken)
                for k in range(KT):
                    link_v(stt(y_buf[:, k], y_buf[:, k], prm_col(gain, k), rs[:, :], ALU.mult, ALU.mult))
                    tt(x_res[:, k], x_res[:, k], y_buf[:, k], ALU.add).then_inc(post.x_ready, 1)

            for m in range(KT):
                post_take(p_mix, B_OUT + m, m)
                if m == 3:
                    for j in range(1, KT, 2):
                        dve.wait_ge(x2_turned, j + 1)
                        V.tensor_copy(x_res[:, j, 0:T], ps[:, 4 + j % 4, :]).then_inc(x2_taken_v, 1)
            dve.wait_ge(x2_taken_a, KT // 2 + 1)
            dve.wait_ge(x2_taken_v, KT // 2)
            post_add(p_mix, "g_mix_post")
            dve.wait_ge(p_mix.x_ready, p_mix.tiles + KT)
            dve_scale_split(n_x, x_res, rs[:, :], "g_x_pre", y_buf, h_lo, h_hi)

            V.memset(prob_z[:, :, :], 0.0)
            link_v(V.tensor_reduce(head_pick[:, :], ident[0:B * XH, 0:B * XH].rearrange("p (b h) -> p h b", b=B),
                                   AX.X, ALU.add))

            def head_max(h):
                for t in range(0, T // P, 2):
                    dve.wait_ge(score_mm, 4 * h + t + 2)
                    ins = V.tensor_reduce(stat[:, 0, 4 * h + t:4 * h + t + 2],
                                          ps[:, 4 + 2 * (h % 2) + t // 2, :].rearrange("p (t m) -> p t m", m=MEM),
                                          AX.X, ALU.max, negate=True)
                link_v(ins)
                ts(stat[:, 0, 4 * h:4 * h + 4], stat[:, 0, 4 * h:4 * h + 4], XHD ** -0.5, None, ALU.mult
                   ).then_inc(attn_max, 1)

            def head_norm(h):
                dve.wait_ge(attn_exp, 4 * h + 4)
                link_v(V.reciprocal(stat[:, 1, 4 * h:4 * h + 4], stat[:, 1, 4 * h:4 * h + 4]))
                for t in range(T // P):
                    ins = ts(prob[:, t], prob[:, t], stat[:, 1, 4 * h + t:4 * h + t + 1], None, ALU.mult)
                ins.then_inc(prob_ready, 1)

            def o_low(h):
                dve.wait_ge(o_hi, h + 1)
                tt(h_lo[:, 2 * h:2 * h + 2, 0:T], ps[:, 2:4, :], h_hi[:, 2 * h:2 * h + 2, 0:T].bitcast(F32), ALU.subtract
                   ).then_inc(o_lo, 1)

            def sample_scores(b):
                dve.wait_ge(q_landed[b % 2], 16 * (b // 2 + 1))
                for m in range(2):
                    t = 2 * b + m
                    dve.wait_ge(cache_landed[t % CACHE_SLOTS], 16 * (t // CACHE_SLOTS + 1))
                    for h in range(XH):
                        keys = cache[:, t % CACHE_SLOTS, XHD * h:XHD * (h + 1)]
                        ins = V.tensor_tensor_reduce(keys, keys, q_bc[:, b % 2, XHD * h:XHD * (h + 1)], 1.0, 0.0,
                                                     ALU.mult, ALU.add, sc[:, m, XH * b + h:XH * b + h + 1])
                    ins.then_inc(k_used, 1)

            head_max(0)
            head_norm(0)
            head_max(1)
            sample_scores(0)
            sample_scores(1)
            for h in range(1, XH):
                head_norm(h)
                o_low(h - 1)
                if h + 1 < XH:
                    head_max(h + 1)
                sample_scores(2 * h)
                sample_scores(2 * h + 1)
            o_low(XH - 1)
            dve.wait_ge(sc_turned, 1)
            link_v(V.tensor_reduce(stat_s[:, 0:1], ps[0:B * XH, 4, 0:MEM], AX.X, ALU.max, negate=True))
            ts(stat_s[:, 0:1], stat_s[:, 0:1], XHD ** -0.5, None, ALU.mult).then_inc(sc_max, 1)
            dve.wait_ge(sc_exp, 1)
            link_v(V.reciprocal(stat_s[:, 1:2], stat_s[:, 1:2]))
            ts(prob_s[:, :], prob_s[:, :], stat_s[:, 1:2], None, ALU.mult).then_inc(prob_s_ready, 1)
            dve.wait_ge(prob_s_turned, 1)
            back = ps[:, 5, 0:2 * B * XH].rearrange("p (m n) -> p m n", m=2)
            for b in range(B):
                ins = V.tensor_copy(prob_z[:, :, (B + 1) * XH * b:(B + 1) * XH * b + XH], back[:, :, XH * b:XH * (b + 1)])
            ins.then_inc(prob_z_ready, 1)
            dve.wait_ge(v_used, 2 * B)
            for h in range(XH):
                src = ps[0:B * XH, 6 + h // 2, XHD * (h % 2):XHD * (h % 2 + 1)]
                if h == 0:
                    link_v(ts(o_pick[:, :], src, head_pick[:, 0:1], None, ALU.mult))
                else:
                    ins = stt(o_pick[:, :], src, head_pick[:, h:h + 1], o_pick[:, :], ALU.mult, ALU.add)
                    (link_v(ins) if h < XH - 1 else ins.then_inc(o_picked, 1))
            dve.wait_ge(o_hi, XH + 1)
            for d in range(2):
                ins = tt(h_lo[:, d:KT:2, T:NT], ps[:, 4, B * XH * d:B * XH * (d + 1)].rearrange("p (b h) -> p h b", b=B),
                         h_hi[:, d:KT:2, T:NT].bitcast(F32), ALU.subtract)
            ins.then_inc(o_lo, 1)

            for m in range(KT):
                post_take(p_x, B_O + m, m)
            post_add(p_x, "g_x_post")
            dve.wait_ge(p_x.x_ready, p_x.tiles + KT)
            dve_scale_split(n_ffn, x_res, rs[:, :], "g_ffn_pre", y_buf, h_lo, h_hi)

            with dve.Fori(0, FT // 2) as i:
                for j in range(2):
                    b = B_UP + 2 * j + 1
                    dve.wait_ge(block_done, b + 1 + 4 * i)
                    dve.wait_ge(out_taken[0], B_UP // 2 + j + 1 + 2 * i)
                    if j == 1:
                        dve.wait_ge(f_lo_ready, 2 * i + 1)
                    tt(two(f_tmp[:, j]), out_view(1), two(silu[:, :]), ALU.mult).then_inc(out_taken[1], 1)
                    dve.wait_ge(out_taken[1], B_UP // 2 + j + 1 + 2 * i)
                    dve.wait_ge(f_hi_ready, 2 * i + j + 1)
                    at = bass.ds(2 * i + j, 1)
                    tt(f_lo[:, at].rearrange("p o n -> p (o n)"), f_tmp[:, j],
                       f_hi[:, at].rearrange("p o n -> p (o n)").bitcast(F32), ALU.subtract).then_inc(f_lo_ready, 1)
            for m in range(KT):
                post_take(p_ffn, B_DOWN + m, m)
            post_add(p_ffn, "g_ffn_post")
            for j in (1, 3):
                dve.wait_ge(y_turns, j + 1)
                V.tensor_copy(y_tok[:, j].rearrange("p (a n) -> p a n", a=2), ps[:, 2 * j:2 * j + 2, :]
                              ).then_inc(y_turn_v, 1)


_OUTS = [(1, T, D), (B, 1, D), (1, 1, C // HS, HS, HS), (1, 1, W_RWKV), (1, 1, TAPS - 1, C), (1, 1, MEM, XH, XHD),
         (1, 1, MEM, XH, XHD), (1, B, C // HS, HS, HS), (1, B, W_RWKV), (1, B, TAPS - 1, C)]


def kernel(**inputs):
    import numpy as _np
    import concourse.bacc as _bacc
    from concourse import mybir as _mybir
    from concourse.bass_utils import run_bass_kernel_spmd as _run

    nc = _bacc.Bacc("TRN2", target_bir_lowering=False, num_devices=1)
    arrays, args, outs = {}, {}, []
    for name, a in inputs.items():
        a = _np.ascontiguousarray(a)
        arrays[f"in_{name}_dram"] = a
        args[name] = nc.dram_tensor(f"in_{name}_dram", a.shape, _mybir.dt.from_np(a.dtype), kind="ExternalInput").ap()
    for i, shape in enumerate(_OUTS):
        outs.append(nc.dram_tensor(f"out_{i}_dram", shape, _mybir.dt.float32, kind="ExternalOutput").ap())
    hybrid_step_kernel(nc, args, outs)
    r = _run(nc, [arrays], core_ids=[0])
    return tuple(r.results[0][f"out_{i}_dram"] for i in range(len(_OUTS)))
```

```python
import concourse.bass as bass
from concourse import mybir

F32 = mybir.dt.float32
F32R = mybir.dt.float32r
ALU = mybir.AluOpType
ACT = mybir.ActivationFunctionType
AX = mybir.AxisListType

P = 128
D = 1024
KT = D // P
T = 512
B = 8
NT = T + B
HALF = NT // 2
C = 512
NP = C // P
HS = 64
NC = T // HS
W_RWKV = 3 * C + 256
N_SHIFT = W_RWKV // P
TAPS = 31
MEM = 256
CACHE_SLOTS = 11
XH, XHD = 4, D // 4
FF = 2816
FT = FF // P
NORM_EPS, LN_EPS, GN_EPS = 1e-6, 1e-5, 64e-5
DECAY = -0.6065306597126334
LN_SCALE = 2.0 ** 30
LN_HALF = 10.397207708399179

VECTORS = [("decay_w0", 4), ("iclr_a0", 4), ("k_k", 4), ("k_a", 4), ("r_k", 4), ("lnx_g", 4), ("lnx_b", 4),
           ("glu_b", 8), ("conv_b", 4), ("conv_ln_g", 4), ("conv_ln_b", 4), ("b_pw", 8), ("merge_gate_b", 16),
           ("g_mix_pre", 8), ("g_mix_post", 8), ("g_mem", 8), ("g_x_pre", 8), ("g_x_post", 8),
           ("g_ffn_pre", 8), ("g_ffn_post", 8)]

B_PAIR = 0
B_GB = 30
B_K = 38
B_V = 46
B_MIX = 54
B_OUT = 70
B_Q = 78
B_O = 86
B_UP = 94
B_DOWN = 138
N_BLOCKS = B_DOWN + 3 * KT
DOWN_KT = (8, 8, 6)
RAW_SLOTS = 4

STEP_ENGINES = [("gram_b", "v"), ("gram_k", "v"), ("gram_a", "v"), ("tok_kv", "a"), ("tok_b", "a"), ("akv", "a"),
                ("dbl0", "va"), ("dbl1", "va"), ("dbl2", "va"), ("dbl3", "va"), ("dbl4", "va"), ("dbl5", "v"),
                ("apply", "a"), ("pw", "v"), ("h", "a")]
STEPS = [(name, q, e) for name, e in STEP_ENGINES for q in range(2)]
N_LOCKSTEP = len(STEPS)
STEPS += [("chain", c, "v") for c in range(1, NC)] + [("y", q, "a") for q in range(2)]
N_STEPS = len(STEPS)


def emptied(engine, pair, upto):
    per_pair = sum(engine in e for _, _, e in STEPS)
    return pair * per_pair + sum(engine in e for _, _, e in STEPS[:upto])


def hybrid_step_kernel(nc, A, O):
    (y_prompt, y_sample, o_rwkv_p, o_shift_p, o_conv_p, o_memk, o_memv, o_rwkv_s, o_shift_s, o_conv_s) = O
    vec_scratch = nc.dram_tensor("vec_scratch", [6, B, C], F32, kind="Internal").ap()
    y_scratch = nc.dram_tensor("y_scratch", [B, C], F32, kind="Internal").ap()
    q_scratch = nc.dram_tensor("q_scratch", [B, D], F32, kind="Internal").ap()

    cursor = [(nc.sbuf_base + 63) // 64 * 64]

    def buf(name, shape, dt=F32):
        size = 4
        for n in shape[1:]:
            size *= n
        t = nc.alloc_sbuf_tensor_at(name, shape, dt, offset=cursor[0])
        cursor[0] += (size + 31) // 32 * 32
        assert cursor[0] <= nc.sbuf_usable_end, (name, cursor[0])
        return t

    ident = buf("ident", [P, P])
    stack_id = buf("stack_id", [P, HS])
    head_ones = buf("head_ones", [P, P])
    head_mean = buf("head_mean", [P, P])
    model_mean = buf("model_mean", [P, P])
    conv_mean = buf("conv_mean", [P, P])
    mask_s = buf("mask_s", [P, 2, HS])
    mask_t = buf("mask_t", [P, 2, HS])
    eps = buf("eps", [P, 4])
    eps_copy = buf("eps_copy", [P, 4])
    prm = buf("prm", [P, 3, P])
    rs = buf("rs", [P, NT])
    w_raw = buf("w_raw", [P, RAW_SLOTS, KT, P])
    w_hi = buf("w_hi", [P, 2, KT, P], F32R)
    w_lo = buf("w_lo", [P, 2, KT, P], F32R)
    h_hi = buf("h_hi", [P, KT, NT], F32R)
    h_lo = buf("h_lo", [P, KT, NT], F32R)
    shared = cursor[0]

    gate_a = buf("gate_a", [P, KT, NT])
    y_fm = buf("y_fm", [P, NP, NT])
    bonus = buf("bonus", [P, NP, NT])
    g_fm = buf("g_fm", [P, NP, NT])
    conv_y = buf("conv_y", [P, NP, NT])
    small_base = cursor[0]
    s_vec = buf("s_vec", [P, 6, NP, B])
    s_final = buf("s_final", [P, NP, HS])
    p_last = buf("p_last", [P, N_SHIFT, 1 + B])
    glu_last = buf("glu_last", [P, NP, TAPS - 1])
    glu_s = buf("glu_s", [P, NP, B])
    pair_base = cursor[0]
    p_ext = buf("p_ext", [P, 3, 1 + NT])
    lora = buf("lora", [P, 2, NT])
    lora_w = buf("lora_w", [P, C])
    gate_w = buf("gate_w", [P, C])
    shift_t = buf("shift_t", [P, N_SHIFT, B])
    scan_mask = buf("scan_mask", [P, T])
    xs = buf("xs", [P, 3, NT])
    sig = buf("sig", [P, NT])
    cum = buf("cum", [P, T])
    e_dec = buf("e_dec", [P, T])
    iclr = buf("iclr", [P, NT])
    kkn = buf("kkn", [P, NT])
    tmp1 = buf("tmp1", [P, NT])
    tmp2 = buf("tmp2", [P, NT])
    kh = buf("kh", [P, NT])
    glu_sig = rs
    glu = buf("glu", [P, TAPS - 1 + NT])
    ar = buf("ar", [P, NC, 2, HS])
    bi = buf("bi", [P, NC, 2, HS])
    kt_fm = buf("kt_fm", [P, NC, HS])
    bh_fm = buf("bh_fm", [P, NC, HS])
    kh_fm = tmp2[:, 0:T].rearrange("p (c n) -> p c n", n=HS)
    g1 = buf("g1", [P, NC, 4 * HS])
    g2 = buf("g2", [P, NC, 2 * HS])
    axb = buf("axb", [P, NC, 3 * HS])
    kv_tok = buf("kv_tok", [P, NC, 2 * HS])
    wg = buf("wg", [P, NC, 2 * HS])
    h_add = buf("h_add", [P, NC, HS])
    s_all = buf("s_all", [P, NC + 1, HS])
    pair_end = cursor[0]
    cursor[0] = shared
    x_tok = buf("x_tok", [P, T // P, D])
    xs_tok = buf("xs_tok", [B, D])
    x_squares_out = buf("x_squares_out", [P, D])
    x_stat = buf("x_stat", [P, T // P + 1])
    h_fm = buf("h_fm", [P, KT, NT])
    p_rows = buf("p_rows", [P, 3, P])
    shift_rows = buf("shift_rows", [B, W_RWKV])
    pro_end = cursor[0]
    cursor[0] = pair_base
    kt = buf("kt", [P, KT, MEM])
    v_tok = buf("v_tok", [P, 2, D])
    attn_base = cursor[0]
    gate_b = buf("gate_b", [P, KT, NT])
    m_hi = buf("m_hi", [P, KT, MEM], F32R)
    m_lo = buf("m_lo", [P, KT, MEM], F32R)
    kv_base = cursor[0]
    ss = buf("ss", [P, HS // 2, HS])
    ss_tmp = buf("ss_tmp", [P, HS // 2, HS])
    vs = buf("vs", [P, 5, HS])
    vs_v = buf("vs_v", [P, HS // 2])
    vs_sa = buf("vs_sa", [P, HS // 2])
    vs_y = buf("vs_y", [P, HS // 2])
    win = buf("win", [P, NP, B, TAPS])
    win_rows = buf("win_rows", [120, 2, C])
    y_rows = buf("y_rows", [B, C])
    ln_base = cursor[0]
    ln_tmp = buf("ln_tmp", [P, NT])
    ln_mu = buf("ln_mu", [P, NT])
    cursor[0] = pair_base
    mem_tok = buf("mem_tok", [P, 2, D])
    mem_fm = buf("mem_fm", [P, KT, MEM])
    cursor[0] = kv_base
    k_tok = buf("k_tok", [P, 2, D])
    v_fm = buf("v_fm", [P, KT, MEM])
    cursor[0] = kv_base
    vt1 = buf("vt1", [B, 4, C])
    cursor[0] = ln_base
    vt2 = buf("vt2", [B, 2, C])
    cursor[0] = shared
    x_res = buf("x_res", [P, KT, NT])
    y_buf = buf("y_buf", [P, KT, NT])
    sq_acc = buf("sq_acc", [P, NT])
    sq_tmp = buf("sq_tmp", [P, 2, NT])
    stream_end = cursor[0]
    sc = buf("sc", [P, 2, B * XH])
    prob_s = buf("prob_s", [B * XH, MEM])
    head_pick = buf("head_pick", [B * XH, XH])
    o_pick = buf("o_pick", [B * XH, XHD])
    stat = buf("stat", [P, 2, 16])
    stat_s = buf("stat_s", [B * XH, 4])
    q_tok = buf("q_tok", [B, D])
    assert cursor[0] <= small_base
    cursor[0] = attn_base
    cache = buf("cache", [P, CACHE_SLOTS, D])
    q_bc = buf("q_bc", [P, 2, D])
    prob = buf("prob", [P, 4, MEM])
    prob_t = buf("prob_t", [P, 2, T])
    prob_z = buf("prob_z", [P, 2, B * B * XH])
    cursor[0] = attn_base
    x_tok2 = buf("x_tok2", [P, T // P, D])
    xs_tok2 = buf("xs_tok2", [B, D])
    cursor[0] = attn_base
    shift_out = buf("shift_out", [1 + B, N_SHIFT, P])
    conv_out = buf("conv_out", [TAPS - 1, C])
    glu_out = buf("glu_out", [B, C])
    rwkv_out = buf("rwkv_out", [HS, NP, P])
    cursor[0] = stream_end
    f_hi = buf("f_hi", [P, FT, NT], F32R)
    f_lo = buf("f_lo", [P, FT, NT], F32R)
    silu = buf("silu", [P, NT])
    f_tmp = buf("f_tmp", [P, 2, NT])
    cursor[0] = stream_end
    y_tok = buf("y_tok", [P, T // P, D])
    ys_tok = buf("ys_tok", [B, D])

    ps = nc.alloc_psum_tensor("ps", [P, 8, 512], F32)

    def sem(name):
        return nc.alloc_semaphore(name)

    w_landed = [sem(f"w_landed{i}") for i in range(RAW_SLOTS)]
    w_hi_ready, w_lo_ready, block_done = sem("w_hi_ready"), sem("w_lo_ready"), sem("block_done")
    out_taken = [sem("out_taken0"), sem("out_taken1")]
    ident_made, consts_made = sem("ident_made"), sem("consts_made")
    x_landed = [sem(f"x_landed{t}") for t in range(T // P + 1)]
    x_squared, x_rsqrt, x_scaled = sem("x_squared"), sem("x_rsqrt"), sem("x_scaled")
    prm_landed, shift_landed = sem("prm_landed"), sem("shift_landed")
    prm_turned, shift_turned, x_turned = sem("prm_turned"), sem("shift_turned"), sem("x_turned")
    prm_ready, xs_turned, xs_taken = sem("prm_ready"), sem("xs_turned"), sem("xs_taken")
    x_taken_v, x_taken_a = sem("x_taken_v"), sem("x_taken_a")
    pair_consts, lora_landed = sem("pair_consts"), sem("lora_landed")

    norm_squares, norm_stats, norm_rsqrt = sem("norm_squares"), sem("norm_stats"), sem("norm_rsqrt")
    norm_scaled, norm_hi, norm_lo = sem("norm_scaled"), sem("norm_hi"), sem("norm_lo")

    class Norm:
        squares, stats, rsqrt, scaled, hi, lo = (norm_squares, norm_stats, norm_rsqrt, norm_scaled, norm_hi, norm_lo)

        def __init__(self, turn):
            self.turn, self.tiles, self.split = turn - 1, KT * (turn - 1), KT * turn

    n_mix, n_mem, n_x, n_ffn = Norm(0), Norm(1), Norm(2), Norm(3)

    act_chain, dve_chain = sem("act_chain"), sem("dve_chain")
    counts = {"a": 0, "v": 0}

    def link_a(ins, n=1):
        ins.then_inc(act_chain, 1)
        counts["a"] += 1
        nc.scalar.wait_ge(act_chain, counts["a"])

    def link_v(ins):
        ins.then_inc(dve_chain, 1)
        counts["v"] += 1
        nc.vector.wait_ge(dve_chain, counts["v"])

    tile_ready, lora_in, lora_ready = sem("tile_ready"), sem("lora_in"), sem("lora_ready")
    lora_mm, lora_taken, xs_ready = sem("lora_mm"), sem("lora_taken"), sem("xs_ready")
    kk_squares, kk_max, kk_rsqrt, rk_ready = sem("kk_squares"), sem("kk_max"), sem("kk_rsqrt"), sem("rk_ready")
    cum_ready, decays_ready, fm_ready, glu_gate = sem("cum_ready"), sem("decays_ready"), sem("fm_ready"), sem("glu_gate")
    bonus_taken = sem("bonus_taken")
    step_mm, step_v, step_a = sem("step_mm"), sem("step_v"), sem("step_a")

    def prm_col(name, i):
        at = 0
        for n, rows in VECTORS:
            if n == name:
                return prm[:, 1, at + i:at + i + 1]
            at += rows

    def mu_col(tile):
        return prm[:, 2, tile:tile + 1]

    def two(ap):
        return ap.rearrange("p (a b) -> p a b", a=2)

    def out_view(s):
        return ps[:, 2 * s:2 * s + 2, 0:HALF]

    def dense(pe, b, s, x_hi, x_lo, kts=KT, k0=0, x0=0, width=HALF, parts=2, first=True, last=True,
              taken=None, x_ready=None, more=0):
        pe.wait_ge(w_lo_ready, b + 1 + more)
        if taken is not None:
            pe.wait_ge(out_taken[s], taken)
        for k in range(k0, k0 + kts):
            if x_ready is not None:
                pe.wait_ge(x_ready[0], x_ready[1] + k + 1)
            for n, (w, x) in enumerate(((w_hi, x_hi), (w_hi, x_lo), (w_lo, x_hi))):
                for a in range(parts):
                    mm = nc.tensor.matmul(ps[:, 2 * s + a, 0:width], w[:, b % 2, k, :],
                                          x[:, x0 + k, a * width:(a + 1) * width],
                                          start=(first and k == 0 and n == 0),
                                          stop=(last and k == block_kts(b) - 1 and n == 2))
        if k0 + kts == block_kts(b):
            mm.then_inc(block_done, 1)

    def block_kts(b):
        if B_MIX <= b < B_OUT:
            return KT // 2
        return DOWN_KT[(b - B_DOWN) % 3] if b >= B_DOWN else KT

    def split_hi(b, more=0, more4=0):
        nc.scalar.wait_ge(w_landed[b % RAW_SLOTS], 16 * (b // RAW_SLOTS + 1) + 16 * more4)
        if b >= 2:
            nc.scalar.wait_ge(block_done, b - 1 + more)
        kts = block_kts(b)
        nc.scalar.activation(w_hi[:, b % 2, 0:kts], w_raw[:, b % RAW_SLOTS, 0:kts], ACT.Copy).then_inc(w_hi_ready, 1)

    def pe_stats(norm, src, mean, tiles, width=HALF, parts=2):
        for k in range(tiles):
            nc.tensor.wait_ge(norm.squares, norm.tiles + k + 1)
            for a in range(parts):
                mm = nc.tensor.matmul(ps[:, 6 + a, 0:width], mean[:, :], src(k)[:, a * width:(a + 1) * width],
                                      start=(k == 0), stop=(k == tiles - 1))
            if k == tiles - 1:
                mm.then_inc(norm.stats, 1)

    def log_exp_table():
        nc.scalar.preload_act_table_set("natural_log_exp_and_others")

    def act_rsqrt(norm, out, src, eps_col):
        log_exp_table()
        nc.scalar.wait_ge(norm.stats, norm.turn + 1)
        link_a(nc.scalar.activation(out, src, ACT.Ln, bias=eps_col))
        nc.scalar.activation(out, out, ACT.Exp, scale=-0.5).then_inc(norm.rsqrt, 1)

    def act_split(norm, src, hi, tiles=KT):
        for k in range(tiles):
            nc.scalar.wait_ge(norm.scaled, norm.tiles + k + 1)
            nc.scalar.activation(hi[:, k], src[:, k], ACT.Copy).then_inc(norm.hi, 1)

    def dve_scale_split(norm, x, scale, gain, tmp, lo, hi, tiles=KT):
        nc.vector.wait_ge(norm.rsqrt, norm.turn + 1)
        for k in range(tiles + 1):
            if k < tiles:
                nc.vector.scalar_tensor_tensor(tmp[:, k], x[:, k], prm_col(gain, k), scale, ALU.mult, ALU.mult
                                               ).then_inc(norm.scaled, 1)
            if k:
                nc.vector.wait_ge(norm.hi, norm.split + k)
                nc.vector.tensor_tensor(lo[:, k - 1], tmp[:, k - 1], hi[:, k - 1].bitcast(F32), ALU.subtract
                                        ).then_inc(norm.lo, 1)

    def first_block(p):
        return 5 + 7 * p

    w_in_v = A["w_in"][0].rearrange("(k p) c -> p k c", p=P)

    def in_column(b):
        if b < 5:
            return P * (12, 13, 0, 4, 8)[b]
        p, j = divmod(b - 5, 7)
        return (W_RWKV + C + P * p, W_RWKV + P * p, W_RWKV + 2 * C + 2 * P * p, W_RWKV + 2 * C + 2 * P * p + P,
                P * (p + 1), P * (p + 5), P * (p + 9))[j]

    def weight_view(name):
        return A[name][0].rearrange("(k p) c -> p k c", p=P)


    post_squares, post_added, post_stats_mm = sem("post_squares"), sem("post_added"), sem("post_stats_mm")
    post_rsqrt, post_x_ready = sem("post_rsqrt"), sem("post_x_ready")
    branch_scaled, x_even_ready = sem("branch_scaled"), sem("x_even_ready")

    class Post:
        squares, added, stats, rsqrt, x_ready = post_squares, post_added, post_stats_mm, post_rsqrt, post_x_ready

        def __init__(self, turn, taken):
            self.turn, self.tiles, self.taken = turn, KT * turn, taken

        def wait_x(self, engine, k):
            engine.wait_ge(self.x_ready if k % 2 else x_even_ready, KT // 2 * self.turn + k // 2 + 1)

    p_mix, p_x, p_ffn = Post(0, B_Q // 2), Post(1, B_UP // 2), Post(2, (B_DOWN + KT) // 2)
    attn_exp, attn_max, conv_hi, conv_lo = sem("attn_exp"), sem("attn_max"), sem("conv_hi"), sem("conv_lo")
    conv_ready, conv_scaled, conv_silu, f_hi_ready = sem("conv_ready"), sem("conv_scaled"), sem("conv_silu"), sem("f_hi_ready")
    f_lo_ready, gn_centred, gn_mean_mm = sem("f_lo_ready"), sem("gn_centred"), sem("gn_mean_mm")
    gn_rsqrt, gn_scaled, gn_squares, gn_var_mm = sem("gn_rsqrt"), sem("gn_scaled"), sem("gn_squares"), sem("gn_var_mm")
    k_tok_ready, k_used, ln_centred, ln_mean = sem("k_tok_ready"), sem("k_used"), sem("ln_centred"), sem("ln_mean")
    ln_rsqrt, ln_squares, ln_var, mem_back = sem("ln_rsqrt"), sem("ln_squares"), sem("ln_var"), sem("mem_back")
    mem_landed, mem_stored, mem_taken, mem_turned = sem("mem_landed"), sem("mem_stored"), sem("mem_taken"), sem("mem_turned")
    merged, mixed_hi, mixed_lo, o_hi = sem("merged"), sem("mixed_hi"), sem("mixed_lo"), sem("o_hi")
    o_lo, o_picked, o_turned, prob_ready = sem("o_lo"), sem("o_picked"), sem("o_turned"), sem("prob_ready")
    prob_s_ready, prob_s_turned, prob_t_ready, prob_turned = sem("prob_s_ready"), sem("prob_s_turned"), sem("prob_t_ready"), sem("prob_turned")
    prob_z_ready, q_stored, q_taken, q_turned = sem("prob_z_ready"), sem("q_stored"), sem("q_taken"), sem("q_turned")
    rwkv_hi, rwkv_lo, rwkv_made, sc_exp = sem("rwkv_hi"), sem("rwkv_lo"), sem("rwkv_made"), sem("sc_exp")
    sc_max, sc_turned, score_mm, shift_taken = sem("sc_max"), sem("sc_turned"), sem("score_mm"), sem("shift_taken")
    ss_landed, ss_stored, state_stored, state_taken = sem("ss_landed"), sem("ss_stored"), sem("state_stored"), sem("state_taken")
    state_turned, stored, v_tok_ready, v_used = sem("state_turned"), sem("stored"), sem("v_tok_ready"), sem("v_used")
    val_taken, vec_ready, vec_stored, vec_taken = sem("val_taken"), sem("vec_ready"), sem("vec_stored"), sem("vec_taken")
    vec_turned, weighed, win_landed, win_turned = sem("vec_turned"), sem("weighed"), sem("win_landed"), sem("win_turned")
    x2_landed, x2_taken_a, x2_taken_v, x2_turned = sem("x2_landed"), sem("x2_taken_a"), sem("x2_taken_v"), sem("x2_turned")
    y_landed, y_ready, y_turn_a, y_turn_v = sem("y_landed"), sem("y_ready"), sem("y_turn_a"), sem("y_turn_v")
    y_turned, y_turns, ys_made, ys_stored = sem("y_turned"), sem("y_turns"), sem("ys_made"), sem("ys_stored")
    cache_landed = [sem(f"cache_landed{i}") for i in range(CACHE_SLOTS)]
    q_landed = [sem("q_landed0"), sem("q_landed1")]
    N_CONSTS = 23

    def ln_buf(j):
        return (ln_tmp, ln_mu)[j % 2][:, :]

    with nc.Block() as block:
        @block.sync
        def _(sp):
            def load(b, src, more=0, kts=KT):
                if not (isinstance(b, int) and b < RAW_SLOTS):
                    sp.wait_ge(w_lo_ready, b - RAW_SLOTS + 1 + more)
                sp.dma_start(w_raw[:, b % RAW_SLOTS, 0:kts], src).then_inc(w_landed[b % RAW_SLOTS], 16)

            def load_parameters():
                at = 0
                for name, rows in VECTORS:
                    src = A[name][0]
                    src = src if name == "r_k" else src.rearrange("(r p) -> r p", p=P)
                    src = src.rearrange("(r h) n -> r (h n)", h=2) if name == "r_k" else src
                    sp.dma_start(p_rows[at:at + rows, 1, :], src).then_inc(prm_landed, 16)
                    at += rows
                assert at == P
                sp.dma_start(p_rows[0:N_SHIFT, 2, :], A["tshift_mu"][0].rearrange("(r p) -> r p", p=P)
                              ).then_inc(prm_landed, 16)
                sp.dma_start(p_rows[0:TAPS * NP, 0, :], A["conv_w"][0].rearrange("t (c p) -> (t c) p", p=P)
                              ).then_inc(prm_landed, 16)
                sp.dma_start(shift_rows[:, :], A["state_shift"][0]).then_inc(shift_landed, 16)
                sp.dma_start(o_conv_s[0][:, 0:TAPS - 2, :], A["state_conv"][0][:, 1:TAPS - 1, :]).then_inc(state_stored, 16)

            for b in range(B_GB):
                if b == 2:
                    load_parameters()
                load(b, w_in_v[:, :, in_column(b):in_column(b) + P])
            with sp.Fori(0, KT // 4) as i:
                for u in range(4):
                    load(B_GB + u, w_in_v[:, :, bass.ds(i * (4 * P) + (W_RWKV + 2 * C + D + P * u), P)], more=4 * i)
            for b0, name in ((B_K, "w_k"), (B_V, "w_v")):
                with sp.Fori(0, KT // 4) as i:
                    for u in range(4):
                        load(b0 + u, weight_view(name)[:, :, bass.ds(i * (4 * P) + P * u, P)], more=4 * i)
            with sp.Fori(0, KT // 2) as i:
                for u in range(4):
                    name = ("w_pw", "w_out_rwkv")[u % 2]
                    load(B_MIX + u, weight_view(name)[:, :, bass.ds(i * (2 * P) + P * (u // 2), P)],
                         more=4 * i, kts=KT // 2)
            with sp.Fori(0, KT // 4) as i:
                for u in range(4):
                    load(B_OUT + u, weight_view("w_out")[:, :, bass.ds(i * (4 * P) + P * u, P)], more=4 * i)

            def load_cache(t):
                name, j = ("cache_mem_k", t) if t < 2 * B else ("cache_mem_v", t - 2 * B)
                if t == 0:
                    sp.wait_ge(x2_turned, 9)
                    sp.wait_ge(mem_stored, 32)
                if t >= CACHE_SLOTS:
                    old = t - CACHE_SLOTS
                    if old < 2 * B:
                        sp.wait_ge(k_used, old + 1)
                    else:
                        sp.wait_ge(v_used, old - 2 * B + 1)
                src = A[name][0][j // 2].rearrange("(m p) h d -> m p (h d)", p=P)[j % 2]
                sp.dma_start(cache[:, t % CACHE_SLOTS], src).then_inc(cache_landed[t % CACHE_SLOTS], 16)

            for m in range(KT):
                load(B_Q + m, weight_view("w_q")[:, :, P * m:P * m + P])
                if m >= 4:
                    load_cache(2 * (m - 4))
                    load_cache(2 * (m - 4) + 1)
            for t in range(8, CACHE_SLOTS):
                load_cache(t)
            for m in range(4):
                load(B_O + m, weight_view("w_o_x")[:, :, P * m:P * m + P])
            sp.wait_ge(q_taken, 1)
            sp.dma_start(q_scratch, q_tok[:, :]).then_inc(q_stored, 16)
            sp.wait_ge(q_stored, 16)
            t = CACHE_SLOTS
            for b in range(B):
                if b >= 2:
                    sp.wait_ge(k_used, 2 * (b - 1))
                sp.dma_start(q_bc[:, b % 2], q_scratch[b].partition_broadcast(P)).then_inc(q_landed[b % 2], 16)
                while t < 4 * B and t - CACHE_SLOTS < 2 * (b - 1):
                    load_cache(t)
                    t += 1
            while t < 4 * B:
                load_cache(t)
                t += 1
            for m in range(4, KT):
                load(B_O + m, weight_view("w_o_x")[:, :, P * m:P * m + P])
            sp.wait_ge(shift_taken, 1)
            sp.dma_start(o_shift_p[0], shift_out[0:1].rearrange("p j n -> p (j n)")).then_inc(state_stored, 16)
            sp.dma_start(o_shift_s[0], shift_out[1:1 + B].rearrange("p j n -> p (j n)")).then_inc(state_stored, 16)
            sp.wait_ge(state_taken, 1)
            sp.dma_start(o_conv_p[0, 0], conv_out[:, :]).then_inc(state_stored, 16)
            sp.dma_start(o_conv_s[0][:, TAPS - 2, :], glu_out[:, :]).then_inc(state_stored, 16)
            sp.dma_start(o_rwkv_p[0, 0].rearrange("(p g) i j -> i p g j", g=2),
                         rwkv_out[:, :, :].rearrange("i p (g j) -> i p g j", g=2)).then_inc(state_stored, 16)
            with sp.Fori(0, FT // 2) as i:
                for u in range(4):
                    load(B_UP + u, weight_view("w_gate_up")[:, :, bass.ds(
                        i * (2 * P) + (FF * (u % 2) + P * (u // 2)), P)], more=4 * i)
            with sp.Fori(0, KT // 4) as i:
                for u in range(12):
                    kts, k0 = DOWN_KT[u % 3], sum(DOWN_KT[:u % 3])
                    load(B_DOWN + u, weight_view("w_down")[:, k0:k0 + kts, bass.ds(i * (4 * P) + P * (u // 3), P)],
                         more=12 * i, kts=kts)
            for j in range(4):
                (sp.wait_ge(y_turn_a, j // 2 + 1) if j % 2 == 0 else sp.wait_ge(y_turn_v, j // 2 + 1))
                sp.dma_start(y_prompt[0, P * j:P * j + P, :], y_tok[:, j]).then_inc(stored, 16)
            sp.wait_ge(y_turn_a, 3)
            sp.dma_start(y_sample[:, 0, :], ys_tok[:, :]).then_inc(stored, 16)
            sp.wait_ge(stored, 5 * 16)
            sp.wait_ge(state_stored, 6 * 16)
            sp.wait_ge(mem_stored, 32)
            sp.wait_ge(ss_stored, 16)

        @block.gpsimd
        def _(pool):
            pool.memset(ident[:], 0.0).then_inc(ident_made, 1)
            pool.wait_ge(ident_made, 1)
            pool.affine_select(out=ident[:, :], in_=ident[:, :], compare_op=ALU.not_equal, fill=1.0, base=0,
                               pattern=[[-1, P]], channel_multiplier=1).then_inc(ident_made, 1)
            for t, v in ((stack_id, 0.0), (head_ones, 1.0), (head_mean, 1.0 / HS),
                         (model_mean, 1.0 / D), (conv_mean, 1.0 / C), (mask_s, 1.0), (mask_t, 1.0)):
                pool.memset(t[:], v).then_inc(consts_made, 1)
            for j, v in enumerate((NORM_EPS, GN_EPS, LN_EPS, LN_HALF)):
                pool.memset(eps[:, j:j + 1], v).then_inc(consts_made, 1)
            pool.wait_ge(consts_made, 11)
            pool.affine_select(out=stack_id[:, :], in_=stack_id[:, :], compare_op=ALU.not_equal, fill=1.0, base=0,
                               pattern=[[-1, HS]], channel_multiplier=1).then_inc(consts_made, 1)
            pool.wait_ge(consts_made, 12)
            pool.affine_select(out=stack_id[:, :], in_=stack_id[:, :], compare_op=ALU.not_equal, fill=1.0, base=-HS,
                               pattern=[[-1, HS]], channel_multiplier=1).then_inc(consts_made, 1)
            for t in (head_ones, head_mean):
                pool.affine_select(out=t[:, 0:HS], in_=t[:, 0:HS], compare_op=ALU.is_gt, fill=0.0, base=HS,
                                   pattern=[[0, HS]], channel_multiplier=-1).then_inc(consts_made, 1)
                pool.affine_select(out=t[:, HS:P], in_=t[:, HS:P], compare_op=ALU.is_ge, fill=0.0, base=-HS,
                                   pattern=[[0, HS]], channel_multiplier=1).then_inc(consts_made, 1)
            for h in range(2):
                r = slice(HS * h, HS * h + HS)
                pool.wait_ge(consts_made, 17 + 3 * h)
                pool.affine_select(out=mask_s[r, 0, :], in_=mask_s[r, 0, :], compare_op=ALU.is_gt, fill=0.0, base=0,
                                   pattern=[[1, HS]], channel_multiplier=-1).then_inc(consts_made, 1)
                pool.affine_select(out=mask_s[r, 1, :], in_=mask_s[r, 1, :], compare_op=ALU.is_ge, fill=0.0, base=0,
                                   pattern=[[1, HS]], channel_multiplier=-1).then_inc(consts_made, 1)
                pool.affine_select(out=mask_t[r, 0, :], in_=mask_t[r, 0, :], compare_op=ALU.is_gt, fill=0.0, base=0,
                                   pattern=[[-1, HS]], channel_multiplier=1).then_inc(consts_made, 1)

            def split_lo(b, more=0):
                pool.wait_ge(w_hi_ready, b + 1 + more)
                kts = block_kts(b)
                pool.tensor_tensor(w_lo[:, b % 2, 0:kts], w_raw[:, b % RAW_SLOTS, 0:kts], w_hi[:, b % 2, 0:kts].bitcast(F32),
                                   ALU.subtract).then_inc(w_lo_ready, 1)

            pool.wait_ge(consts_made, N_CONSTS)
            split_lo(0)
            split_lo(1)

            def split_lows(b0, end):
                with pool.Fori(0, (end - b0) // RAW_SLOTS) as i:
                    for u in range(RAW_SLOTS):
                        split_lo(b0 + u, more=RAW_SLOTS * i)
                for b in range(end - (end - b0) % RAW_SLOTS, end):
                    split_lo(b)

            def add_branch(post):
                for k in range(0, KT, 2):
                    pool.wait_ge(branch_scaled, KT // 2 * post.turn + k // 2 + 1)
                    pool.tensor_tensor(x_res[:, k], x_res[:, k], y_buf[:, k], ALU.add).then_inc(x_even_ready, 1)

            split_lows(2, B_MIX)
            split_lows(B_MIX, B_OUT)
            split_lows(B_OUT, B_Q + 2)
            add_branch(p_mix)
            split_lows(B_Q + 2, B_UP + 2)
            add_branch(p_x)
            split_lows(B_UP + 2, B_DOWN - 2)
            for b in range(B_DOWN - 2, N_BLOCKS):
                split_lo(b)
            add_branch(p_ffn)

        @block.tensor
        def _(pe):
            tr = nc.tensor.transpose

            def turn_rows(rows, extra, bank_of, landed, waits, done):
                for j in range(KT + 1):
                    waits(j)
                    if j == 0:
                        pe.wait_ge(landed, 32)
                    if j < KT:
                        for t in range(T // P):
                            mm = tr(ps[:, bank_of(j), P * t:P * t + P], rows[:, t, P * j:P * j + P], ident[:, :])
                    else:
                        for k in range(KT):
                            mm = tr(ps[:, bank_of(j), B * k:B * k + B], extra[:, P * k:P * k + P], ident[0:B, 0:B])
                    mm.then_inc(done, 1)

            def x_waits(taken_a, taken_v):
                def waits(j):
                    if j >= 4:
                        pe.wait_ge(taken_a if j % 2 == 0 else taken_v, (j - 4) // 2 + 1)
                return waits

            pe.wait_ge(ident_made, 2)
            pe.wait_ge(prm_landed, 16 * (len(VECTORS) + 2))
            for j, n in enumerate((TAPS * NP, P, N_SHIFT)):
                mm = tr(ps[:, 2, P * j:P * j + n], p_rows[0:n, j, :], ident[0:n, 0:n])
            mm.then_inc(prm_turned, 1)
            pe.wait_ge(shift_landed, 16)
            for j in range(N_SHIFT):
                mm = tr(ps[:, 3, B * j:B * j + B], shift_rows[:, P * j:P * j + P], ident[0:B, 0:B])
            mm.then_inc(shift_turned, 1)
            pe.wait_ge(x_scaled, T // P + 1)
            for k in range(KT):
                mm = tr(ps[:, 4, B * k:B * k + B], xs_tok[:, P * k:P * k + P], ident[0:B, 0:B])
            mm.then_inc(x_turned, 1)
            for i in range(1, KT + 1):
                if i >= 4:
                    pe.wait_ge(x_taken_a if i % 2 else x_taken_v, (i - 3) // 2 if i % 2 else (i - 4) // 2 + 1)
                for t in range(T // P):
                    mm = tr(ps[:, 4 + i % 4, P * t:P * t + P], x_tok[:, t, P * (i - 1):P * i], ident[:, :])
                mm.then_inc(x_turned, 1)
            pe.wait_ge(consts_made, N_CONSTS)

            for b in range(5):
                if b == 1:
                    pe.wait_ge(pair_consts, 1)
                dense(pe, b, b % 2, h_hi, h_lo, taken=b // 2 if b >= 2 else None, x_ready=(n_mix.lo, n_mix.split) if b == 0 else None)

            def small(out, lhsT, rhs, start=True, stop=True):
                return nc.tensor.matmul(out, lhsT, rhs, start=start, stop=stop)

            def lora_product(bank, w, x):
                for a in range(2):
                    mm = small(ps[:, bank + a, 0:HALF], w, x[:, a * HALF:(a + 1) * HALF])
                mm.then_inc(lora_mm, 1)

            def step(p, k):
                name, q, _ = STEPS[k]
                if k < 2:
                    pe.wait_ge(fm_ready, p + 1)
                    pe.wait_ge(bonus_taken, p + 1)
                else:
                    upto = k - 1 if k < N_LOCKSTEP else min(k, N_STEPS - 2)
                    pe.wait_ge(step_v, emptied("v", p, upto))
                    pe.wait_ge(step_a, emptied("a", p, upto))
                base = 4 + 2 * q if k < N_LOCKSTEP else 0
                if name == "chain":
                    bank, c = (4, 6)[q % 2], q
                    for h in range(2):
                        r = slice(HS * h, HS * h + HS)
                        mm = small(ps[r, bank, 0:HS], wg[r, c, HS:2 * HS], s_all[r, c, :])
                    mm.then_inc(step_mm, 1)
                    return
                for j in range(4):
                    c = 4 * q + j
                    for h in range(2):
                        r = slice(HS * h, HS * h + HS)
                        wide = ps[r, base, 2 * HS * j:2 * HS * (j + 1)]
                        one = ps[r, base, HS * j:HS * (j + 1)]
                        if name == "gram_b":
                            mm = small(wide, bi[r, c, 0, :], ar[r, c, :, :])
                        elif name == "gram_k":
                            mm = small(wide, kt_fm[r, c, :], ar[r, c, :, :])
                        elif name == "gram_a":
                            mm = small(wide, ar[r, c, 0, :], bi[r, c, :, :])
                        elif name == "tok_kv":
                            small(wide[:, 0:HS], kh_fm[r, c, :], stack_id[r, :])
                            mm = small(wide[:, HS:2 * HS], xs[r, 2, HS * c:HS * (c + 1)], stack_id[r, :])
                        elif name == "tok_b":
                            mm = small(one, bh_fm[r, c, :], stack_id[r, :])
                        elif name == "akv":
                            mm = small(one, g2[r, c, 0:HS], kv_tok[r, c, HS:2 * HS])
                        elif name == "dbl5":
                            mm = small(wide[:, 0:HS], axb[r, c, 0:HS], g1[r, c, 0:HS])
                        elif name.startswith("dbl"):
                            if name == "dbl0":
                                small(wide[:, HS:2 * HS], axb[r, c, 0:HS], g1[r, c, HS:2 * HS])
                            else:
                                small(wide, axb[r, c, 0:HS], g1[r, c, 0:2 * HS])
                            mm = small(ps[r, base + 1, HS * j:HS * (j + 1)], g1[r, c, HS:2 * HS], axb[r, c, 0:HS])
                        elif name == "apply":
                            mm = small(wide, g1[r, c, 0:HS], axb[r, c, HS:3 * HS])
                        elif name == "pw":
                            mm = small(wide, axb[r, c, HS:2 * HS], g1[r, c, 2 * HS:4 * HS])
                        elif name == "h":
                            small(one, g1[r, c, 3 * HS:4 * HS], axb[r, c, 2 * HS:3 * HS], stop=False)
                            mm = small(one, kv_tok[r, c, 0:HS], kv_tok[r, c, HS:2 * HS], start=False)
                        elif name == "y":
                            out = ps[r, 5 + 2 * q, HS * j:HS * (j + 1)]
                            if c:
                                small(out, s_all[r, c, :], wg[r, c, 0:HS], stop=False)
                            small(out, kv_tok[r, c, HS:2 * HS], g2[r, c, HS:2 * HS], start=(c == 0), stop=False)
                            mm = small(out, axb[r, c, 2 * HS:3 * HS], g1[r, c, 2 * HS:3 * HS], start=False)
                mm.then_inc(step_mm, 1)

            pe.wait_ge(lora_landed, 48)
            pe.wait_ge(lora_ready, 2)
            for p in range(NP):
                b0, cols = first_block(p), slice(P * p, P * p + P)
                if p:
                    pe.wait_ge(step_v, emptied("v", p, 0))
                    pe.wait_ge(step_a, emptied("a", p, 0))
                lora_product(4, lora_w[0:HS, cols], lora[0:HS, 0, :])
                lora_product(6, lora_w[HS:P, cols], lora[HS:P, 0, :])
                dense(pe, b0, b0 % 2, h_hi, h_lo, taken=b0 // 2)
                pe.wait_ge(lora_taken, 3 * p + 1)
                lora_product(4, gate_w[:, cols], lora[:, 1, :])
                pe.wait_ge(lora_taken, 3 * p + 2)
                pe.wait_ge(kk_squares, p + 1)
                lora_product(6, head_ones[:, :], tmp1)
                dense(pe, b0 + 1, (b0 + 1) % 2, h_hi, h_lo, taken=(b0 + 1) // 2)
                pe.wait_ge(lora_taken, 3 * p + 3)
                pe.wait_ge(rk_ready, p + 1)
                lora_product(4, head_ones[:, :], tmp2)
                for b in (b0 + 2, b0 + 3):
                    dense(pe, b, b % 2, h_hi, h_lo, taken=b // 2)
                for k in range(N_LOCKSTEP):
                    step(p, k)
                parts = [(b, k) for b in range(b0 + 4, b0 + 7) for k in range(KT)] if p < NP - 1 else []
                for n in range(NC - 1):
                    step(p, N_LOCKSTEP + n)
                    take = parts[len(parts) * n // (NC - 1):len(parts) * (n + 1) // (NC - 1)]
                    for b, k in take:
                        dense(pe, b, b % 2, h_hi, h_lo, kts=1, k0=k, taken=b // 2 if k == 0 else None)
                step(p, N_STEPS - 2)
                step(p, N_STEPS - 1)

            def gate_block(m):
                b = B_GB + m
                dense(pe, b, b % 2, h_hi, h_lo, taken=b // 2)

            gate_block(0)
            pe.wait_ge(step_a, emptied("a", NP, 0))
            pe.wait_ge(step_v, emptied("v", NP, 0))
            pe.wait_ge(mem_landed, 16)
            for k in range(KT):
                for m in range(2):
                    mm = tr(ps[:, 4 + k // 2, MEM * (k % 2) + P * m:MEM * (k % 2) + P * m + P],
                            mem_tok[:, m, P * k:P * k + P], ident[:, :])
            mm.then_inc(mem_turned, 1)
            gate_block(1)
            pe.wait_ge(mem_taken, 1)
            pe.wait_ge(vec_ready, 1)
            for v in range(4):
                for p in range(NP):
                    mm = tr(ps[0:B, 4 + v, P * p:P * p + P], s_vec[:, v, p, :], ident[:, :])
            mm.then_inc(vec_turned, 1)
            gate_block(2)
            pe.wait_ge(vec_taken, 1)
            for v in range(2):
                for p in range(NP):
                    mm = tr(ps[0:B, 4 + v, P * p:P * p + P], s_vec[:, 4 + v, p, :], ident[:, :])
            mm.then_inc(vec_turned, 1)
            pe_stats(n_mem, lambda k: v_fm[:, k], model_mean, KT, width=MEM, parts=1)
            gate_block(3)
            pe.wait_ge(win_landed, 32)
            for j in range(2):
                if j == 1:
                    pe.wait_ge(n_mem.rsqrt, n_mem.turn + 1)
                for c in range(NP):
                    mm = tr(ps[:, 7 - j, 120 * c:120 * c + 120], win_rows[:, j, P * c:P * c + P], ident[0:120, 0:120])
            mm.then_inc(win_turned, 1)
            for m in range(4, 7):
                gate_block(m)
            pe.wait_ge(vec_taken, 2)
            pe.wait_ge(conv_ready, 1)
            for c in range(NP):
                for a in range(2):
                    mm = small(ps[:, 4 + a, 0:HALF], conv_mean[:, :], conv_y[:, c, a * HALF:(a + 1) * HALF],
                               start=(c == 0), stop=(c == NP - 1))
            mm.then_inc(ln_mean, 1)
            gate_block(7)
            for c in range(NP):
                pe.wait_ge(ln_squares, c + 1)
                for a in range(2):
                    mm = small(ps[:, 6 + a, 0:HALF], conv_mean[:, :], ln_buf(c)[:, a * HALF:(a + 1) * HALF],
                               start=(c == 0), stop=(c == NP - 1))
                mm.then_inc(ln_var, 1)

            def head_stat(j, src, matrix, done):
                for a in range(2):
                    mm = small(ps[:, 4 + 2 * (j % 2) + a, 0:HALF], matrix, src[:, a * HALF:(a + 1) * HALF])
                mm.then_inc(done, 1)

            def gn_mean(j):
                if j == 0:
                    pe.wait_ge(y_ready, 1)
                    pe.wait_ge(ln_rsqrt, 1)
                if j >= 2:
                    pe.wait_ge(gn_rsqrt, j - 1)
                head_stat(j, y_fm[:, j], head_mean[:, :], gn_mean_mm)

            def gn_var(j):
                pe.wait_ge(gn_squares, j + 1)
                head_stat(j, ln_buf(j), head_mean[:, :], gn_var_mm)

            def key_block(m):
                b = B_K + m
                dense(pe, b, b % 2, m_hi, m_lo, width=MEM, parts=1, taken=b // 2, x_ready=(n_mem.lo, n_mem.split) if m == 0 else None)

            key_block(0)
            key_block(1)
            pe.wait_ge(y_landed, 16)
            for p in range(NP):
                mm = tr(ps[:, 4, B * p:B * p + B], y_rows[:, P * p:P * p + P], ident[0:B, 0:B])
            mm.then_inc(y_turned, 1)
            key_block(2)
            gn_mean(0)
            gn_mean(1)
            key_block(3)
            gn_var(0)
            key_block(4)
            gn_mean(2)
            gn_var(1)
            key_block(5)
            gn_mean(3)
            gn_var(2)
            key_block(6)
            gn_var(3)
            key_block(7)
            with pe.Fori(0, KT // 4) as i:
                for u in range(4):
                    b = B_V + u
                    dense(pe, b, b % 2, m_hi, m_lo, width=MEM, parts=1, taken=b // 2 + 2 * i, more=4 * i)
            pe.wait_ge(out_taken[1], B_MIX // 2)
            pe.wait_ge(out_taken[0], B_MIX // 2)
            pe.wait_ge(gn_rsqrt, NP)
            for src, which in ((kt, 0), (v_fm, 1)):
                if which:
                    pe.wait_ge(k_tok_ready, 1)
                for m in range(2):
                    for k in range(KT):
                        at = KT * m + k
                        mm = tr(ps[:, 4 + at // 4, P * (at % 4):P * (at % 4) + P], src[:, k, P * m:P * m + P],
                                ident[:, :])
                mm.then_inc(mem_back, 1)

            pe.wait_ge(conv_lo, NP)
            pe.wait_ge(rwkv_lo, NP)
            with pe.Fori(0, KT // 2) as i:
                for u in range(4):
                    b = B_MIX + u
                    dense(pe, b, b % 2, h_hi, h_lo, kts=KT // 2, x0=NP * (u % 2), taken=b // 2 + 2 * i, more=4 * i)

            def post_stats(post):
                pe.wait_ge(post.added, post.tiles + KT)
                for a in range(2):
                    mm = small(ps[:, 6 + a, 0:HALF], model_mean[:, :], sq_acc[:, a * HALF:(a + 1) * HALF])
                mm.then_inc(post.stats, 1)

            def next_stats(post, norm):
                pe.wait_ge(post.rsqrt, post.turn + 1)
                pe_stats(norm, lambda k: y_buf[:, k], model_mean, KT)

            for m in range(KT):
                b = B_OUT + m
                dense(pe, b, b % 2, h_hi, h_lo, taken=b // 2, x_ready=(mixed_lo, 0) if m == 0 else None)
                if m == 3:
                    pe.wait_ge(v_tok_ready, 1)
                    turn_rows(x_tok2, xs_tok2, lambda j: 4 + j % 4, x2_landed, x_waits(x2_taken_a, x2_taken_v),
                              x2_turned)
            pe.wait_ge(x2_taken_v, 4)
            post_stats(p_mix)
            next_stats(p_mix, n_x)
            for m in range(KT):
                b = B_Q + m
                dense(pe, b, b % 2, h_hi, h_lo, taken=b // 2, x_ready=(n_x.lo, n_x.split) if m == 0 else None)

            pe.wait_ge(out_taken[0], B_O // 2)
            pe.wait_ge(out_taken[1], B_O // 2)
            for k in range(KT):
                mm = tr(ps[0:B, k // 4, P * (k % 4):P * (k % 4) + P], y_buf[:, k, T:NT], ident[:, :])
            mm.then_inc(q_turned, 1)
            pe.wait_ge(n_x.rsqrt, n_x.turn + 1)

            def scores(h):
                if h >= 2:
                    pe.wait_ge(attn_exp, 4 * (h - 1))
                for t in range(T // P):
                    for d in range(2):
                        mm = small(ps[:, 4 + 2 * (h % 2) + t // 2, MEM * (t % 2):MEM * (t % 2 + 1)],
                                   y_buf[:, 2 * h + d, P * t:P * t + P], kt[:, 2 * h + d, :],
                                   start=(d == 0), stop=(d == 1))
                    mm.then_inc(score_mm, 1)

            def turn_probs(h):
                pe.wait_ge(prob_ready, h + 1)
                (pe.wait_ge(prob_t_ready, h) if h else pe.wait_ge(q_taken, 1))
                for t in range(T // P):
                    for m in range(2):
                        mm = tr(ps[:, m, P * t:P * t + P], prob[:, t, P * m:P * m + P], ident[:, :])
                mm.then_inc(prob_turned, 1)

            def weigh(h):
                pe.wait_ge(prob_t_ready, h + 1)
                if h:
                    pe.wait_ge(o_lo, h)
                for d in range(2):
                    for m in range(2):
                        mm = small(ps[:, 2 + d, :], v_tok[:, m, XHD * h + P * d:XHD * h + P * d + P], prob_t[:, m, :],
                                   start=(m == 0), stop=(m == 1))
                mm.then_inc(weighed, 1)

            scores(0)
            scores(1)
            for h in range(XH):
                turn_probs(h)
                weigh(h)
                if h + 2 < XH:
                    scores(h + 2)
            pe.wait_ge(k_used, 2 * B)
            pe.wait_ge(attn_exp, 4 * XH)
            for m in range(2):
                mm = tr(ps[0:B * XH, 4, P * m:P * m + P], sc[:, m, :], ident[:, :])
            mm.then_inc(sc_turned, 1)
            pe.wait_ge(prob_s_ready, 1)
            for m in range(2):
                mm = tr(ps[:, 5, B * XH * m:B * XH * (m + 1)], prob_s[:, P * m:P * m + P], ident[0:B * XH, 0:B * XH])
            mm.then_inc(prob_s_turned, 1)
            pe.wait_ge(prob_z_ready, 1)
            for b in range(B):
                for m in range(2):
                    t = 2 * B + 2 * b + m
                    pe.wait_ge(cache_landed[t % CACHE_SLOTS], 16 * (t // CACHE_SLOTS + 1))
                    for a in range(2):
                        mm = small(ps[0:B * XH, 6 + a, :], prob_z[:, m, B * XH * b:B * XH * (b + 1)],
                                   cache[:, t % CACHE_SLOTS, 512 * a:512 * (a + 1)],
                                   start=(b == 0 and m == 0), stop=(b == B - 1 and m == 1))
                    mm.then_inc(v_used, 1)
            pe.wait_ge(o_picked, 1)
            for d in range(2):
                mm = tr(ps[:, 4, B * XH * d:B * XH * (d + 1)], o_pick[:, P * d:P * d + P], ident[0:B * XH, 0:B * XH])
            mm.then_inc(o_turned, 1)

            pe.wait_ge(o_lo, XH + 1)
            for m in range(KT):
                b = B_O + m
                dense(pe, b, b % 2, h_hi, h_lo, taken=b // 2)
                if m == 0:
                    for j in range(N_SHIFT):
                        mm = tr(ps[0:1 + B, 4 + j // 4, P * (j % 4):P * (j % 4) + P], p_last[:, j, :], ident[:, :])
                    mm.then_inc(state_turned, 1)
                if m == 1:
                    pe.wait_ge(shift_taken, 1)
                    for c in range(NP):
                        tr(ps[0:TAPS - 1, 4, P * c:P * c + P], glu_last[:, c, :], ident[:, :])
                        tr(ps[0:B, 5, P * c:P * c + P], glu_s[:, c, :], ident[:, :])
                        mm = tr(ps[0:HS, 6, P * c:P * c + P], s_final[:, c, :], ident[:, :])
                    mm.then_inc(state_turned, 1)
            pe.wait_ge(state_taken, 1)
            post_stats(p_x)
            next_stats(p_x, n_ffn)

            with pe.Fori(0, FT // 2) as i:
                for u in range(4):
                    b = B_UP + u
                    dense(pe, b, b % 2, h_hi, h_lo, taken=b // 2 + 2 * i, more=4 * i,
                          x_ready=(n_ffn.lo, n_ffn.split) if u == 0 else None)
            pe.wait_ge(f_lo_ready, sum(DOWN_KT[:2]))
            with pe.Fori(0, KT // 4) as i:
                for u in range(12):
                    b, o = B_DOWN + u, B_DOWN + u // 3
                    if u == 2:
                        pe.wait_ge(f_lo_ready, FT)
                    dense(pe, b, o % 2, f_hi, f_lo, kts=DOWN_KT[u % 3], x0=sum(DOWN_KT[:u % 3]), first=(u % 3 == 0),
                          last=(u % 3 == 2), taken=o // 2 + 2 * i if u % 3 == 0 else None, more=12 * i)
            post_stats(p_ffn)
            pe.wait_ge(p_ffn.rsqrt, p_ffn.turn + 1)
            for k in range(KT):
                p_ffn.wait_x(pe, k)
                for j in range(T // P):
                    mm = tr(ps[:, 2 * j + k // 4, P * (k % 4):P * (k % 4) + P], x_res[:, k, P * j:P * j + P],
                            ident[:, :])
                    if k == KT - 1:
                        mm.then_inc(y_turns, 1)
            pe.wait_ge(y_turn_a, 1)
            for k in range(KT):
                mm = tr(ps[0:B, k // 4, P * (k % 4):P * (k % 4) + P], x_res[:, k, T:NT], ident[:, :])
            mm.then_inc(y_turns, 1)

        @block.scalar
        def _(act):
            go = nc.scalar.activation
            for t in range(T // P):
                act.dma_start(x_tok[:, t, :], A["x_prompt"][0, P * t:P * t + P, :]).then_inc(x_landed[t], 16)
            act.dma_start(xs_tok[:, :], A["x_sample"][:, 0, :]).then_inc(x_landed[T // P], 16)
            log_exp_table()
            act.wait_ge(x_squared, 1)
            for t in range(T // P):
                act.wait_ge(x_landed[t], 16)
                go(x_squares_out[:, :], x_tok[:, t], ACT.Square, accum_out=x_stat[:, t:t + 1]).then_inc(x_squared, 1)
                act.wait_ge(x_squared, t + 2)
            act.wait_ge(x_landed[T // P], 16)
            link_a(go(x_squares_out[0:B, :], xs_tok[:, :], ACT.Square, accum_out=x_stat[0:B, T // P:T // P + 1]))
            act.wait_ge(consts_made, 11)
            link_a(go(x_stat[:, :], x_stat[:, :], ACT.Ln, scale=1.0 / D, bias=eps[:, 0:1]))
            go(x_stat[:, :], x_stat[:, :], ACT.Exp, scale=-0.5).then_inc(x_rsqrt, 1)
            split_hi(0)
            act.wait_ge(prm_ready, 1)
            for k in range(KT):
                if k % 2 == 0:
                    act.wait_ge(x_turned, k + 2)
                    go(h_fm[:, k, 0:T], ps[:, 4 + (k + 1) % 4, :], ACT.Copy, scale=prm_col("g_mix_pre", k)
                       ).then_inc(x_taken_a, 1)
                act.wait_ge(x_taken_a, k // 2 + 1)
                act.wait_ge(x_taken_v, (k + 1) // 2 + 1)
                go(h_hi[:, k], h_fm[:, k], ACT.Copy).then_inc(n_mix.hi, 1)
                if k == 1:
                    split_hi(1)
            act.wait_ge(n_mix.lo, n_mix.split + KT)
            act.dma_start(lora_w[0:HS, :], A["decay_w2"][0]).then_inc(lora_landed, 16)
            act.dma_start(lora_w[HS:P, :], A["iclr_a2"][0]).then_inc(lora_landed, 16)
            act.dma_start(gate_w[:, :], A["gate_g2"][0]).then_inc(lora_landed, 16)
            act.wait_ge(pair_consts, 1)
            act.wait_ge(prm_ready, 1)

            def tile_out(b, j, tile):
                act.wait_ge(block_done, b + 1)
                go(two(p_ext[:, j, 1:1 + NT]), out_view(b % 2), ACT.Copy).then_inc(out_taken[b % 2], 1)
                act.wait_ge(out_taken[b % 2], b // 2 + 1)
                go(p_last[:, tile, :], p_ext[:, j, T:1 + NT], ACT.Copy).then_inc(tile_ready, 1)

            for b in range(5):
                if b:
                    split_hi(b + 1)
                if b == 2:
                    act.wait_ge(lora_in, 1)
                tile_out(b, (0, 1, 0, 1, 2)[b], (12, 13, 0, 4, 8)[b])
                if b == 2:
                    go(lora[0:HS, 0], lora[0:HS, 0], ACT.Tanh).then_inc(lora_ready, 1)
                    go(lora[:, 1], lora[:, 1], ACT.Sigmoid).then_inc(lora_ready, 1)

            def gate_out(b, dst, col):
                act.wait_ge(block_done, b + 1)
                go(two(dst), out_view(b % 2), ACT.Sigmoid, bias=col).then_inc(out_taken[b % 2], 1)

            def step_out(p, k):
                name, q, engines = STEPS[k]
                if "a" not in engines:
                    return
                act.wait_ge(step_mm, N_STEPS * p + k + 1)
                cs, base = slice(4 * q, 4 * q + 4), 4 + 2 * q
                wide = ps[:, base, :].rearrange("p (c n) -> p c n", c=4)
                one = ps[:, base, 0:4 * HS].rearrange("p (c n) -> p c n", c=4)
                if name == "tok_kv":
                    ins = go(kv_tok[:, cs, :], wide, ACT.Copy)
                elif name == "tok_b":
                    ins = go(g1[:, cs, 3 * HS:4 * HS], one, ACT.Copy)
                elif name == "akv":
                    ins = go(axb[:, cs, 2 * HS:3 * HS], one, ACT.Copy)
                elif name.startswith("dbl"):
                    ins = go(axb[:, cs, 0:HS], ps[:, base + 1, 0:4 * HS].rearrange("p (c n) -> p c n", c=4), ACT.Copy)
                elif name == "apply":
                    ins = go(axb[:, cs, HS:3 * HS], wide, ACT.Copy)
                elif name == "h":
                    if q == 0:
                        go(s_all[:, 1, :], ps[:, base, 0:HS], ACT.Copy)
                    ins = go(h_add[:, cs, :], one, ACT.Copy)
                elif name == "y":
                    ins = go(y_fm[:, p, 4 * HS * q:4 * HS * (q + 1)], ps[:, 5 + 2 * q, 0:4 * HS], ACT.Copy)
                ins.then_inc(step_a, 1)

            for p in range(NP):
                b0 = first_block(p)
                act.wait_ge(lora_mm, 5 * p + 1)
                if p:
                    act.wait_ge(fm_ready, p)
                go(two(sig[:, :]), ps[:, 4:6, 0:HALF], ACT.Sigmoid, bias=prm_col("decay_w0", p)).then_inc(lora_taken, 1)
                act.wait_ge(lora_mm, 5 * p + 2)
                go(two(iclr[:, :]), ps[:, 6:8, 0:HALF], ACT.Sigmoid, bias=prm_col("iclr_a0", p)).then_inc(lora_taken, 1)
                split_hi(b0 + 1)
                act.wait_ge(xs_ready, p + 1)
                go(tmp1[:, :], xs[:, 1], ACT.Square, scale=prm_col("k_k", p)).then_inc(kk_squares, 1)
                act.wait_ge(lora_mm, 5 * p + 3)
                go(two(g_fm[:, p]), ps[:, 4:6, 0:HALF], ACT.Copy).then_inc(lora_taken, 1)
                if p:
                    act.wait_ge(val_taken, p)
                gate_out(b0, glu_sig[:, :], prm_col("glu_b", NP + p))
                act.wait_ge(out_taken[b0 % 2], b0 // 2 + 1)
                split_hi(b0 + 2)
                act.wait_ge(kk_max, p + 1)
                link_a(go(kkn[:, :], kkn[:, :], ACT.Ln, scale=LN_SCALE))
                go(kkn[:, :], kkn[:, :], ACT.Exp, scale=-0.5, bias=eps[:, 3:4]).then_inc(kk_rsqrt, 1)
                act.wait_ge(cum_ready, p + 1)
                go(e_dec[:, :], cum[:, :], ACT.Exp, scale=DECAY)
                go(sig[:, 0:T], sig[:, 0:T], ACT.Exp, scale=DECAY)
                link_a(go(s_vec[:, 4, p, :], sig[:, T:NT], ACT.Exp, scale=DECAY))
                go(cum[:, :], cum[:, :], ACT.Exp, scale=-DECAY).then_inc(decays_ready, 1)
                split_hi(b0 + 3)
                gate_out(b0 + 2, gate_a[:, 2 * p], prm_col("merge_gate_b", 2 * p))
                split_hi(b0 + 4)
                gate_out(b0 + 3, gate_a[:, 2 * p + 1], prm_col("merge_gate_b", 2 * p + 1))
                if p < NP - 1:
                    split_hi(b0 + 5)
                for k in range(N_LOCKSTEP):
                    step_out(p, k)
                if p < NP - 1:
                    for j in range(3):
                        tile_out(b0 + 4 + j, j, NP * j + p + 1)
                        if j < 2:
                            split_hi(b0 + 6 + j)
                for k in range(N_LOCKSTEP, N_STEPS):
                    step_out(p, k)

            def gate_b_out(m):
                gate_out(B_GB + m, gate_b[:, m], prm_col("merge_gate_b", KT + m))

            act.wait_ge(block_done, B_GB)
            act.wait_ge(step_mm, NP * N_STEPS)
            act.wait_ge(step_v, emptied("v", NP, 0))
            act.wait_ge(step_a, emptied("a", NP, 0))
            act.dma_start(mem_tok[:, :, :], A["mem_prompt"][0].rearrange("(m p) d -> p m d", p=P)
                          ).then_inc(mem_landed, 16)
            for j in range(2):
                act.dma_start(win_rows[:, j, :], A["state_conv"][0][4 * j:4 * j + 4].rearrange("b t c -> (b t) c")
                              ).then_inc(win_landed, 16)
            split_hi(B_GB + 1)
            gate_b_out(0)
            split_hi(B_GB + 2)
            act.wait_ge(mem_turned, 1)
            go(mem_fm[:, :, :], ps[:, 4:8, :].rearrange("p b (k n) -> p (b k) n", k=2), ACT.Copy).then_inc(mem_taken, 1)
            act.wait_ge(mem_taken, 1)
            for k in range(KT):
                go(v_fm[:, k], mem_fm[:, k], ACT.Square).then_inc(n_mem.squares, 1)
            gate_b_out(1)
            split_hi(B_GB + 3)
            act.wait_ge(vec_turned, 1)
            go(vt1[:, :, :], ps[0:B, 4:8, :], ACT.Copy).then_inc(vec_taken, 1)
            act.wait_ge(vec_taken, 1)
            act.dma_start(vec_scratch[0:4].rearrange("v b c -> b v c"), vt1[:, :, :]).then_inc(vec_stored, 16)
            gate_b_out(2)
            split_hi(B_GB + 4)
            act.wait_ge(vec_turned, 2)
            go(vt2[:, :, :], ps[0:B, 4:6, :], ACT.Copy).then_inc(vec_taken, 1)
            act.wait_ge(vec_taken, 2)
            act.dma_start(vec_scratch[4:6].rearrange("v b c -> b v c"), vt2[:, :, :]).then_inc(vec_stored, 16)
            act_rsqrt(n_mem, rs[:, 0:MEM], ps[:, 6, 0:MEM], eps[:, 0:1])
            act.wait_ge(vec_stored, 32)
            act.dma_start(ss[:, :, :], A["state_rwkv"][0].rearrange("b h (g i) j -> (b h g) i j", g=2)
                          ).then_inc(ss_landed, 16)
            for g in range(2):
                act.dma_start(vs[g:P:2, :, :], vec_scratch[0:5].rearrange("v b (h j) -> (b h) v j", j=HS)
                              ).then_inc(ss_landed, 16)
            act.dma_start(vs_v[:, :], vec_scratch[5].rearrange("b (h i) -> (b h) i", i=HS // 2)).then_inc(ss_landed, 16)
            act_split(n_mem, v_fm, m_hi)
            for m in range(3, 6):
                gate_b_out(m)
                split_hi(B_GB + m + 2)
            gate_b_out(6)
            split_hi(B_GB + 8)
            act.wait_ge(ys_made, 1)
            act.dma_start(y_scratch.rearrange("b (h i) -> (b h) i", i=HS // 2), vs_y[:, :]).then_inc(ys_stored, 16)
            act.dma_start(o_rwkv_s[0].rearrange("b h (g i) j -> (b h g) i j", g=2), ss[:, :, :]).then_inc(ss_stored, 16)
            gate_b_out(7)
            split_hi(B_GB + 9)
            act.wait_ge(ys_stored, 16)
            act.dma_start(y_rows[:, :], y_scratch).then_inc(y_landed, 16)
            for c in range(NP):
                act.wait_ge(ln_centred, c + 1)
                if c >= 2:
                    act.wait_ge(ln_var, c - 1)
                go(ln_buf(c), conv_y[:, c], ACT.Square).then_inc(ln_squares, 1)
            log_exp_table()
            act.wait_ge(ln_var, NP)
            act.wait_ge(n_mem.lo, n_mem.split + KT)
            link_a(go(two(rs[:, :]), ps[:, 6:8, 0:HALF], ACT.Ln, bias=eps[:, 2:3]))
            go(rs[:, :], rs[:, :], ACT.Exp, scale=-0.5).then_inc(ln_rsqrt, 1)

            def key_out(m):
                b = B_K + m
                act.wait_ge(block_done, b + 1)
                go(kt[:, m], ps[:, 2 * (b % 2), 0:MEM], ACT.Copy).then_inc(out_taken[b % 2], 1)

            key_out(0)
            split_hi(B_K + 2)
            for c in range(NP):
                act.wait_ge(conv_scaled, c + 1)
                go(conv_y[:, c], conv_y[:, c], ACT.Silu, bias=prm_col("conv_ln_b", c)).then_inc(conv_silu, 1)
            act.wait_ge(conv_silu, NP)
            for c in range(NP):
                go(h_hi[:, c], conv_y[:, c], ACT.Copy).then_inc(conv_hi, 1)
            key_out(1)
            split_hi(B_K + 3)

            def gn_square(j):
                act.wait_ge(gn_centred, j + 1)
                go(ln_buf(j), y_fm[:, j], ACT.Square).then_inc(gn_squares, 1)

            def gn_root(j):
                if j == 0:
                    log_exp_table()
                act.wait_ge(gn_var_mm, j + 1)
                link_a(go(two(ln_buf(j)), ps[:, 4 + 2 * (j % 2):6 + 2 * (j % 2), 0:HALF], ACT.Ln, bias=eps[:, 1:2]))
                go(ln_buf(j), ln_buf(j), ACT.Exp, scale=-0.5).then_inc(gn_rsqrt, 1)

            key_out(2)
            split_hi(B_K + 4)
            gn_square(0)
            gn_square(1)
            key_out(3)
            split_hi(B_K + 5)
            gn_root(0)
            key_out(4)
            split_hi(B_K + 6)
            gn_root(1)
            act.wait_ge(gn_scaled, 1)
            gn_square(2)
            key_out(5)
            split_hi(B_K + 7)
            act.wait_ge(gn_scaled, 2)
            gn_root(2)
            gn_square(3)
            key_out(6)
            split_hi(B_K + 8)
            gn_root(3)
            for j in range(NP):
                act.wait_ge(rwkv_made, j + 1)
                go(h_hi[:, NP + j], y_fm[:, j], ACT.Copy).then_inc(rwkv_hi, 1)
            key_out(7)
            for m in range(KT):
                b = B_V + m
                split_hi(b + 1)
                act.wait_ge(block_done, b + 1)
                go(v_fm[:, m], ps[:, 2 * (b % 2), 0:MEM], ACT.Copy).then_inc(out_taken[b % 2], 1)
            act.wait_ge(ss_stored, 16)
            act.wait_ge(mem_back, 1)
            go(k_tok[:, :, :].rearrange("p m d -> p (m d)"), ps[:, 4:8, :].rearrange("p b n -> p (b n)"), ACT.Copy
               ).then_inc(k_tok_ready, 1)
            act.wait_ge(k_tok_ready, 1)
            act.dma_start(o_memk[0, 0].rearrange("(m p) h d -> p m (h d)", p=P), k_tok[:, :, :]).then_inc(mem_stored, 16)
            with act.Fori(0, KT // 2 - 1) as i:
                for u in range(4):
                    split_hi(B_MIX + 1 + u, more=4 * i, more4=i)
            for b in range(B_OUT - 3, B_OUT + 2):
                split_hi(b)
            act.wait_ge(v_tok_ready, 1)
            act.dma_start(o_memv[0, 0].rearrange("(m p) h d -> p m (h d)", p=P), v_tok[:, :, :]).then_inc(mem_stored, 16)
            act.wait_ge(block_done, B_OUT)
            for m in range(KT):
                act.wait_ge(merged, m + 1)
                go(h_hi[:, m], gate_b[:, m], ACT.Copy).then_inc(mixed_hi, 1)
            act.wait_ge(mixed_lo, KT)
            act.dma_start(x_tok2[:, :, :], A["x_prompt"][0].rearrange("(t p) d -> p t d", p=P)).then_inc(x2_landed, 16)
            act.dma_start(xs_tok2[:, :], A["x_sample"][:, 0, :]).then_inc(x2_landed, 16)

            def post_square(post, o, done, m):
                act.wait_ge(block_done, done)
                if m >= 2:
                    act.wait_ge(post.added, post.tiles + m - 1)
                go(two(sq_tmp[:, m % 2]), out_view(o % 2), ACT.Square).then_inc(post.squares, 1)

            def x_squares(post, norm):
                for k in range(KT):
                    post.wait_x(act, k)
                    go(y_buf[:, k], x_res[:, k], ACT.Square).then_inc(norm.squares, 1)

            for m in range(KT):
                if m:
                    split_hi(B_OUT + m + 1)
                post_square(p_mix, B_OUT + m, B_OUT + m + 1, m)
                if m == 3:
                    for j in range(0, KT + 1, 2):
                        act.wait_ge(x2_turned, j + 1)
                        if j < KT:
                            ins = go(x_res[:, j, 0:T], ps[:, 4 + j % 4, :], ACT.Copy)
                        else:
                            ins = go(x_res[:, :, T:NT], ps[:, 4, 0:KT * B].rearrange("p (k b) -> p k b", b=B), ACT.Copy)
                        ins.then_inc(x2_taken_a, 1)
            split_hi(B_Q + 1)
            act_rsqrt(p_mix, two(rs[:, :]), ps[:, 6:8, 0:HALF], eps[:, 0:1])
            x_squares(p_mix, n_x)
            act_rsqrt(n_x, two(rs[:, :]), ps[:, 6:8, 0:HALF], eps[:, 0:1])
            act_split(n_x, y_buf, h_hi)
            for m in range(KT):
                b = B_Q + m
                if m:
                    split_hi(b + 1)
                act.wait_ge(block_done, b + 1)
                go(two(y_buf[:, m]), out_view(b % 2), ACT.Copy).then_inc(out_taken[b % 2], 1)
            split_hi(B_O + 1)

            act.wait_ge(q_turned, 1)
            go(q_tok[:, :], ps[0:B, 0:2, :].rearrange("p a n -> p (a n)"), ACT.Copy).then_inc(q_taken, 1)

            def exps(h):
                act.wait_ge(attn_max, h + 1)
                if h:
                    act.wait_ge(prob_turned, h)
                for t in range(T // P):
                    j = 4 * h + t
                    go(prob[:, t], ps[:, 4 + 2 * (h % 2) + t // 2, MEM * (t % 2):MEM * (t % 2 + 1)], ACT.Exp,
                       scale=XHD ** -0.5, bias=stat[:, 0, j:j + 1], accum_out=stat[:, 1, j:j + 1]).then_inc(attn_exp, 1)

            def take_prob_t(h):
                act.wait_ge(prob_turned, h + 1)
                if h:
                    act.wait_ge(weighed, h)
                go(prob_t[:, :, :], ps[:, 0:2, :], ACT.Copy).then_inc(prob_t_ready, 1)

            def o_high(h):
                act.wait_ge(weighed, h + 1)
                go(h_hi[:, 2 * h:2 * h + 2, 0:T], ps[:, 2:4, :], ACT.Copy).then_inc(o_hi, 1)

            exps(0)
            take_prob_t(0)
            for h in range(1, XH):
                exps(h)
                o_high(h - 1)
                take_prob_t(h)
            o_high(XH - 1)
            act.wait_ge(sc_max, 1)
            go(prob_s[:, :], ps[0:B * XH, 4, 0:MEM], ACT.Exp, scale=XHD ** -0.5, bias=stat_s[:, 0:1],
               accum_out=stat_s[:, 1:2]).then_inc(sc_exp, 1)
            act.wait_ge(o_turned, 1)
            for d in range(2):
                ins = go(h_hi[:, d:KT:2, T:NT],
                         ps[:, 4, B * XH * d:B * XH * (d + 1)].rearrange("p (b h) -> p h b", b=B), ACT.Copy)
            ins.then_inc(o_hi, 1)

            for m in range(KT):
                if m:
                    split_hi(B_O + m + 1)
                if m == 1:
                    act.wait_ge(state_turned, 1)
                    go(shift_out[:, :, :], ps[0:1 + B, 4:8, :].rearrange("p b (j n) -> p (b j) n", n=P)[:, 0:N_SHIFT],
                       ACT.Copy).then_inc(shift_taken, 1)
                post_square(p_x, B_O + m, B_O + m + 1, m)
                if m == 2:
                    act.wait_ge(state_turned, 2)
                    go(conv_out[:, :], ps[0:TAPS - 1, 4, :], ACT.Copy)
                    go(glu_out[:, :], ps[0:B, 5, :], ACT.Copy)
                    go(rwkv_out[:, :, :], ps[0:HS, 6, :].rearrange("p (j n) -> p j n", j=NP), ACT.Copy
                       ).then_inc(state_taken, 1)
            split_hi(B_UP + 1)
            act_rsqrt(p_x, two(rs[:, :]), ps[:, 6:8, 0:HALF], eps[:, 0:1])
            x_squares(p_x, n_ffn)
            act_rsqrt(n_ffn, two(rs[:, :]), ps[:, 6:8, 0:HALF], eps[:, 0:1])
            act_split(n_ffn, y_buf, h_hi)
            act.wait_ge(state_stored, 6 * 16)
            nc.scalar.preload_act_table(ACT.Silu)
            for j in range(FT):
                b = B_UP + 2 * j
                if j:
                    split_hi(b + 1)
                    act.wait_ge(out_taken[1], B_UP // 2 + j)
                    go(f_hi[:, j - 1], f_tmp[:, (j - 1) % 2], ACT.Copy).then_inc(f_hi_ready, 1)
                act.wait_ge(block_done, b + 1)
                go(two(silu[:, :]), out_view(0), ACT.Silu).then_inc(out_taken[0], 1)
                split_hi(b + 2)
            act.wait_ge(out_taken[1], B_UP // 2 + FT)
            go(f_hi[:, FT - 1], f_tmp[:, (FT - 1) % 2], ACT.Copy).then_inc(f_hi_ready, 1)
            split_hi(B_DOWN + 1)
            for m in range(KT):
                for j in range(3):
                    if 1 < 3 * m + j + 1 and B_DOWN + 3 * m + j + 1 < N_BLOCKS:
                        split_hi(B_DOWN + 3 * m + j + 1)
                post_square(p_ffn, B_DOWN + m, B_DOWN + 3 * m + 3, m)
            act_rsqrt(p_ffn, two(rs[:, :]), ps[:, 6:8, 0:HALF], eps[:, 0:1])
            for j in (0, 2):
                act.wait_ge(y_turns, j + 1)
                go(y_tok[:, j].rearrange("p (a n) -> p a n", a=2), ps[:, 2 * j:2 * j + 2, :], ACT.Copy).then_inc(y_turn_a, 1)
            act.wait_ge(y_turns, 5)
            go(ys_tok[:, :].rearrange("p (a n) -> p a n", a=2), ps[0:B, 0:2, :], ACT.Copy).then_inc(y_turn_a, 1)

        @block.vector
        def _(dve):
            V = nc.vector
            stt, tt, ts = V.scalar_tensor_tensor, V.tensor_tensor, V.tensor_scalar
            V.memset(x_stat[:, :], 1.0).then_inc(x_squared, 1)
            dve.wait_ge(x_rsqrt, 1)
            for t in range(T // P):
                ts(x_tok[:, t], x_tok[:, t], x_stat[:, t:t + 1], None, ALU.mult).then_inc(x_scaled, 1)
            ts(xs_tok[:, :], xs_tok[:, :], x_stat[0:B, T // P:T // P + 1], None, ALU.mult).then_inc(x_scaled, 1)
            gain0 = sum(n for _, n in VECTORS[:[n for n, _ in VECTORS].index("g_mix_pre")])
            dve.wait_ge(prm_turned, 1)
            V.tensor_copy(prm[:, 0, 0:TAPS * NP], ps[:, 2, 0:TAPS * NP])
            V.tensor_copy(prm[:, 1, :], ps[:, 2, P:2 * P])
            V.tensor_copy(prm[:, 2, 0:N_SHIFT], ps[:, 2, 2 * P:2 * P + N_SHIFT]).then_inc(prm_ready, 1)
            dve.wait_ge(prm_ready, 1)
            dve.wait_ge(x_turned, 1)
            tt(h_fm[:, :, T:NT], ps[:, 4, 0:KT * B].rearrange("p (k b) -> p k b", b=B),
               prm[:, 1, gain0:gain0 + KT].unsqueeze(2).to_broadcast([P, KT, B]), ALU.mult).then_inc(x_taken_v, 1)
            for k in range(KT + 1):
                if k < KT and k % 2:
                    dve.wait_ge(x_turned, k + 2)
                    ts(h_fm[:, k, 0:T], ps[:, 4 + (k + 1) % 4, :], prm_col("g_mix_pre", k), None, ALU.mult
                       ).then_inc(x_taken_v, 1)
                if k:
                    dve.wait_ge(n_mix.hi, k)
                    tt(h_lo[:, k - 1], h_fm[:, k - 1], h_hi[:, k - 1].bitcast(F32), ALU.subtract).then_inc(n_mix.lo, 1)
            dve.wait_ge(n_mix.lo, n_mix.split + KT)
            dve.wait_ge(shift_turned, 1)
            dve.wait_ge(consts_made, N_CONSTS)
            V.tensor_copy(shift_t[:, :, :], ps[:, 3, 0:N_SHIFT * B].rearrange("p (j b) -> p j b", b=B))
            V.memset(p_ext[:, :, 0:1], 0.0)
            V.memset(glu[:, 0:TAPS - 1], 0.0)
            link_v(V.memset(scan_mask[:, :], 1.0))
            V.memset(scan_mask[:, :].rearrange("p (c t) -> p c t", t=HS)[:, :, 0:1], 0.0)
            link_v(V.tensor_copy(bi[:, :, 1, :], stack_id[:, :].unsqueeze(1).to_broadcast([P, NC, HS])))
            V.tensor_copy(eps_copy[:, :], eps[:, :]).then_inc(pair_consts, 1)

            def shift_mix(dst, tiles, prev_s):
                n = len(tiles)
                tt(dst[:, 0:n, 0:T], p_ext[:, 0:n, 0:T], p_ext[:, 0:n, 1:1 + T], ALU.subtract)
                link_v(tt(dst[:, 0:n, T:NT], prev_s, p_ext[:, 0:n, 1 + T:1 + NT], ALU.subtract))
                for j, tile in enumerate(tiles):
                    ins = stt(dst[:, j], dst[:, j], mu_col(tile), p_ext[:, j, 1:1 + NT], ALU.mult, ALU.add)
                return ins

            dve.wait_ge(tile_ready, 2)
            shift_mix(lora, (12, 13), shift_t[:, 12:14, :]).then_inc(lora_in, 1)

            def conv_tap(p, t):
                src, w = glu[:, t:t + T], prm[:, 0, NP * t + p:NP * t + p + 1]
                if t == 0:
                    link_v(ts(conv_y[:, p, 0:T], src, w, prm_col("conv_b", p), ALU.mult, ALU.add))
                else:
                    link_v(stt(conv_y[:, p, 0:T], src, w, conv_y[:, p, 0:T], ALU.mult, ALU.add))

            def step_out(p, k):
                name, q, engines = STEPS[k]
                if "v" not in engines:
                    return
                dve.wait_ge(step_mm, N_STEPS * p + k + 1)
                if name == "chain":
                    tt(s_all[:, q + 1, :], ps[:, (4, 6)[q % 2], 0:HS], h_add[:, q, :], ALU.add).then_inc(step_v, 1)
                    return
                cs, base = slice(4 * q, 4 * q + 4), 4 + 2 * q
                wide = ps[:, base, :].rearrange("p (c n) -> p c n", c=4)
                mask = {"gram_b": mask_s, "gram_k": mask_s, "gram_a": mask_t}.get(name)
                dst = {"gram_b": g1, "gram_k": g2, "gram_a": axb}.get(name)
                if mask is not None:
                    if name == "gram_a":
                        dve.wait_ge(step_v, emptied("v", p, q + 1))
                        tt(g1[:, cs, 0:HS], g1[:, cs, HS:2 * HS],
                           stack_id[:, :].unsqueeze(1).to_broadcast([P, 4, HS]), ALU.add)
                    m = mask[:, :, :].rearrange("p a n -> p (a n)").unsqueeze(1).to_broadcast([P, 4, 2 * HS])
                    at = HS if name == "gram_b" else 0
                    ins = tt(dst[:, cs, at:at + 2 * HS], wide, m, ALU.mult)
                elif name.startswith("dbl"):
                    if name != "dbl0":
                        ins = tt(g1[:, cs, 0:HS], wide[:, :, 0:HS], g1[:, cs, 0:HS], ALU.add)
                    if name != "dbl5":
                        ins = V.tensor_copy(g1[:, cs, HS:2 * HS], wide[:, :, HS:2 * HS])
                elif name == "pw":
                    tt(wg[:, cs, 0:HS], wide[:, :, 0:HS], ar[:, cs, 1, :], ALU.add)
                    for j in range(4):
                        c = 4 * q + j
                        last = e_dec[:, HS * c + HS - 1:HS * c + HS]
                        ins = stt(wg[:, c, HS:2 * HS], stack_id[:, :], last, wide[:, j, HS:2 * HS], ALU.mult, ALU.add)
                ins.then_inc(step_v, 1)

            def chunks(ap):
                return ap.rearrange("p (c t) -> p c t", t=HS)

            for p in range(NP):
                b0 = first_block(p)
                dve.wait_ge(tile_ready, 2 + 3 * (p + 1))
                if p:
                    dve.wait_ge(step_mm, N_STEPS * p)
                r, k, v = xs[:, 0], xs[:, 1], xs[:, 2]
                shift_mix(xs, (p, NP + p, 2 * NP + p), shift_t[:, p:3 * NP:NP, :]).then_inc(xs_ready, 1)
                dve.wait_ge(lora_taken, 3 * p + 1)
                link_v(V.tensor_tensor_scan(cum[:, :], scan_mask[:, :], sig[:, 0:T], 0.0, ALU.mult, ALU.add))
                tt(sig[:, 0:T], cum[:, :], sig[:, 0:T], ALU.subtract).then_inc(cum_ready, 1)
                dve.wait_ge(lora_taken, 3 * p + 2)
                dve.wait_ge(xs_ready, p + 1)
                link_v(ts(kh[:, :], iclr[:, :], 1.0, prm_col("k_a", p), ALU.subtract, ALU.mult))
                link_v(stt(kh[:, :], kh[:, :], 1.0, k, ALU.add, ALU.mult))
                stt(tmp2[:, :], r, prm_col("r_k", p), kh[:, :], ALU.mult, ALU.mult).then_inc(rk_ready, 1)
                dve.wait_ge(lora_mm, 5 * p + 4)
                ts(two(kkn[:, :]), ps[:, 6:8, 0:HALF], 1e-24, None, ALU.max).then_inc(kk_max, 1)
                dve.wait_ge(kk_rsqrt, p + 1)
                link_v(stt(kkn[:, :], k, prm_col("k_k", p), kkn[:, :], ALU.mult, ALU.mult))
                link_v(tt(tmp1[:, :], kkn[:, :], iclr[:, :], ALU.mult))
                dve.wait_ge(lora_mm, 5 * p + 5)
                tt(two(bonus[:, p]), ps[:, 4:6, 0:HALF], two(v), ALU.mult).then_inc(bonus_taken, 1)
                dve.wait_ge(decays_ready, p + 1)
                stt(ar[:, :, 0, :], chunks(kkn[:, 0:T]), -1.0, chunks(sig[:, 0:T]), ALU.mult, ALU.mult)
                tt(ar[:, :, 1, :], chunks(xs[:, 0, 0:T]), chunks(e_dec[:, :]), ALU.mult)
                tt(bi[:, :, 0, :], chunks(tmp1[:, 0:T]), chunks(cum[:, :]), ALU.mult)
                link_v(tt(kt_fm[:, :, :], chunks(kh[:, 0:T]), chunks(cum[:, :]), ALU.mult))
                whole = chunks(e_dec[:, :])[:, :, HS - 1:HS].to_broadcast([P, NC, HS])
                tt(bh_fm[:, :, :], bi[:, :, 0, :], whole, ALU.mult)
                tt(kh_fm, kt_fm[:, :, :], whole, ALU.mult)
                V.tensor_copy(s_vec[:, 0, p, :], xs[:, 0, T:NT])
                V.tensor_copy(s_vec[:, 1, p, :], kh[:, T:NT])
                ts(s_vec[:, 2, p, :], kkn[:, T:NT], -1.0, None, ALU.mult)
                V.tensor_copy(s_vec[:, 3, p, :], tmp1[:, T:NT])
                V.tensor_copy(s_vec[:, 5, p, :], xs[:, 2, T:NT]).then_inc(fm_ready, 1)
                dve.wait_ge(block_done, b0 + 2)
                dve.wait_ge(out_taken[b0 % 2], b0 // 2 + 1)
                stt(two(glu[:, TAPS - 1:TAPS - 1 + NT]), out_view((b0 + 1) % 2), prm_col("glu_b", p), two(glu_sig[:, :]),
                    ALU.add, ALU.mult).then_inc(out_taken[(b0 + 1) % 2], 1)
                dve.wait_ge(out_taken[(b0 + 1) % 2], (b0 + 1) // 2 + 1)
                V.tensor_copy(glu_last[:, p, :], glu[:, T:T + TAPS - 1])
                link_v(V.tensor_copy(glu_s[:, p, :], glu[:, T + TAPS - 1:]))
                V.tensor_copy(eps_copy[:, :], eps[:, :]).then_inc(val_taken, 1)
                tap = 0
                for n in range(N_LOCKSTEP):
                    step_out(p, n)
                    take = 2 if STEPS[n][0][:3] in ("dbl", "app") or STEPS[n] == ("gram_a", 1, "v") else int(n == 0)
                    for t in range(tap, tap + take):
                        conv_tap(p, t)
                    tap += take
                assert tap == TAPS
                for n in range(N_LOCKSTEP, N_STEPS):
                    step_out(p, n)
                dve.wait_ge(step_v, emptied("v", p, N_STEPS))
                link_v(V.tensor_copy(s_final[:, p, :], s_all[:, NC, :]))
            V.tensor_copy(eps_copy[:, :], eps[:, :]).then_inc(vec_ready, 1)

            dve_scale_split(n_mem, mem_fm, rs[:, 0:MEM], "g_mem", v_fm, m_lo, m_hi)
            dve.wait_ge(win_turned, 1)
            for j in range(2):
                V.tensor_copy(win[:, :, 4 * j:4 * j + 4, 0:TAPS - 1],
                              ps[:, 7 - j, 0:480].rearrange("p (c b t) -> p c b t", c=NP, b=4))
            link_v(V.tensor_copy(win[:, :, :, TAPS - 1], glu_s[:, :, :]))
            for c in range(NP):
                w = prm[:, 0, c:NP * TAPS:NP].unsqueeze(1).to_broadcast([P, B, TAPS])
                ins = tt(win[:, c], win[:, c], w, ALU.mult)
            link_v(ins)
            link_v(V.tensor_reduce(conv_y[:, :, T:NT], win[:, :, :, :], AX.X, ALU.add))
            for c in range(NP):
                ins = ts(conv_y[:, c, T:NT], conv_y[:, c, T:NT], prm_col("conv_b", c), None, ALU.add)
            ins.then_inc(conv_ready, 1)

            def over_i(ap):
                return ap.unsqueeze(1).to_broadcast([P, HS // 2, HS])

            def over_j(ap):
                return ap.unsqueeze(2).to_broadcast([P, HS // 2, HS])

            dve.wait_ge(ss_landed, 64)
            link_v(tt(ss_tmp[:, :, :], ss[:, :, :], over_i(vs[:, 2, :]), ALU.mult))
            link_v(V.tensor_reduce(vs_sa[:, :], ss_tmp[:, :, :], AX.X, ALU.add))
            tt(ss[:, :, :], ss[:, :, :], over_i(vs[:, 4, :]), ALU.mult)
            link_v(tt(ss_tmp[:, :, :], over_j(vs_sa[:, :]), over_i(vs[:, 3, :]), ALU.mult))
            link_v(tt(ss[:, :, :], ss[:, :, :], ss_tmp[:, :, :], ALU.add))
            link_v(tt(ss_tmp[:, :, :], over_j(vs_v[:, :]), over_i(vs[:, 1, :]), ALU.mult))
            link_v(tt(ss[:, :, :], ss[:, :, :], ss_tmp[:, :, :], ALU.add))
            link_v(tt(ss_tmp[:, :, :], ss[:, :, :], over_i(vs[:, 0, :]), ALU.mult))
            V.tensor_reduce(vs_y[:, :], ss_tmp[:, :, :], AX.X, ALU.add).then_inc(ys_made, 1)

            dve.wait_ge(ln_mean, 1)
            for c in range(NP):
                tt(two(conv_y[:, c]), two(conv_y[:, c]), ps[:, 4:6, 0:HALF], ALU.subtract).then_inc(ln_centred, 1)
            dve.wait_ge(ln_rsqrt, 1)
            dve.wait_ge(ln_centred, NP)
            for c in range(NP):
                stt(conv_y[:, c], conv_y[:, c], prm_col("conv_ln_g", c), rs[:, :], ALU.mult, ALU.mult
                    ).then_inc(conv_scaled, 1)
            for c in range(NP):
                dve.wait_ge(conv_hi, c + 1)
                tt(h_lo[:, c], conv_y[:, c], h_hi[:, c].bitcast(F32), ALU.subtract).then_inc(conv_lo, 1)
            dve.wait_ge(y_turned, 1)
            V.tensor_copy(y_fm[:, :, T:NT], ps[:, 4, 0:NP * B].rearrange("p (c b) -> p c b", b=B)).then_inc(y_ready, 1)

            def gn_centre(j):
                dve.wait_ge(gn_mean_mm, j + 1)
                if j == 0:
                    dve.wait_ge(y_ready, 1)
                tt(two(y_fm[:, j]), two(y_fm[:, j]), ps[:, 4 + 2 * (j % 2):6 + 2 * (j % 2), 0:HALF], ALU.subtract
                   ).then_inc(gn_centred, 1)

            def gn_scale(j):
                dve.wait_ge(gn_rsqrt, j + 1)
                dve.wait_ge(gn_centred, j + 1)
                stt(y_fm[:, j], y_fm[:, j], prm_col("lnx_g", j), ln_buf(j), ALU.mult, ALU.mult).then_inc(gn_scaled, 1)
                dve.wait_ge(gn_scaled, j + 1)
                link_v(stt(y_fm[:, j], y_fm[:, j], prm_col("lnx_b", j), bonus[:, j], ALU.add, ALU.add))
                tt(y_fm[:, j], y_fm[:, j], g_fm[:, j], ALU.mult).then_inc(rwkv_made, 1)

            gn_centre(0)
            gn_centre(1)
            gn_scale(0)
            gn_centre(2)
            gn_scale(1)
            gn_centre(3)
            gn_scale(2)
            gn_scale(3)
            for j in range(NP):
                dve.wait_ge(rwkv_hi, j + 1)
                tt(h_lo[:, NP + j], y_fm[:, j], h_hi[:, NP + j].bitcast(F32), ALU.subtract).then_inc(rwkv_lo, 1)
            dve.wait_ge(mem_back, 2)
            V.tensor_copy(v_tok[:, :, :].rearrange("p m d -> p (m d)"), ps[:, 4:8, :].rearrange("p b n -> p (b n)")
                          ).then_inc(v_tok_ready, 1)

            b_pw0 = sum(n for _, n in VECTORS[:[n for n, _ in VECTORS].index("b_pw")])
            with dve.Fori(0, KT // 2) as i:
                for j in range(2):
                    ga = gate_a[:, bass.ds(2 * i + j, 1)].rearrange("p o (a b) -> p (o a) b", a=2)
                    gb = gate_b[:, bass.ds(2 * i + j, 1)].rearrange("p o (a b) -> p (o a) b", a=2)
                    m_no, taken = B_MIX + 2 * j, B_MIX // 2 + j + 1
                    dve.wait_ge(block_done, m_no + 1 + 4 * i)
                    stt(gb, out_view(0), prm[:, 1, bass.ds(2 * i + (b_pw0 + j), 1)], gb, ALU.add, ALU.mult
                        ).then_inc(out_taken[0], 1)
                    dve.wait_ge(block_done, m_no + 2 + 4 * i)
                    tt(ga, out_view(1), ga, ALU.mult).then_inc(out_taken[1], 1)
                    dve.wait_ge(out_taken[0], taken + 2 * i)
                    dve.wait_ge(out_taken[1], taken + 2 * i)
                    tt(gb, ga, gb, ALU.add).then_inc(merged, 1)
            dve.wait_ge(merged, KT)
            for m in range(KT):
                dve.wait_ge(mixed_hi, m + 1)
                tt(h_lo[:, m], gate_b[:, m], h_hi[:, m].bitcast(F32), ALU.subtract).then_inc(mixed_lo, 1)

            def post_take(post, o, m):
                dve.wait_ge(post.squares, post.tiles + m + 1)
                V.tensor_copy(two(y_buf[:, m]), out_view(o % 2)).then_inc(out_taken[o % 2], 1)
                if m:
                    dve.wait_ge(post.added, post.tiles + m)
                    ins = tt(sq_acc[:, :], sq_acc[:, :], sq_tmp[:, m % 2], ALU.add)
                else:
                    ins = V.tensor_copy(sq_acc[:, :], sq_tmp[:, 0])
                ins.then_inc(post.added, 1)

            def post_add(post, gain):
                dve.wait_ge(post.rsqrt, post.turn + 1)
                dve.wait_ge(out_taken[0], post.taken)
                dve.wait_ge(out_taken[1], post.taken)
                for k in range(KT):
                    scaled = stt(y_buf[:, k], y_buf[:, k], prm_col(gain, k), rs[:, :], ALU.mult, ALU.mult)
                    if k % 2:
                        link_v(scaled)
                        tt(x_res[:, k], x_res[:, k], y_buf[:, k], ALU.add).then_inc(post.x_ready, 1)
                    else:
                        scaled.then_inc(branch_scaled, 1)

            for m in range(KT):
                post_take(p_mix, B_OUT + m, m)
                if m == 3:
                    for j in range(1, KT, 2):
                        dve.wait_ge(x2_turned, j + 1)
                        V.tensor_copy(x_res[:, j, 0:T], ps[:, 4 + j % 4, :]).then_inc(x2_taken_v, 1)
            dve.wait_ge(x2_taken_a, KT // 2 + 1)
            dve.wait_ge(x2_taken_v, KT // 2)
            post_add(p_mix, "g_mix_post")
            p_mix.wait_x(dve, KT - 1)
            p_mix.wait_x(dve, KT - 2)
            dve_scale_split(n_x, x_res, rs[:, :], "g_x_pre", y_buf, h_lo, h_hi)

            V.memset(prob_z[:, :, :], 0.0)
            link_v(V.tensor_reduce(head_pick[:, :], ident[0:B * XH, 0:B * XH].rearrange("p (b h) -> p h b", b=B),
                                   AX.X, ALU.add))

            def head_max(h):
                for t in range(0, T // P, 2):
                    dve.wait_ge(score_mm, 4 * h + t + 2)
                    ins = V.tensor_reduce(stat[:, 0, 4 * h + t:4 * h + t + 2],
                                          ps[:, 4 + 2 * (h % 2) + t // 2, :].rearrange("p (t m) -> p t m", m=MEM),
                                          AX.X, ALU.max, negate=True)
                link_v(ins)
                ts(stat[:, 0, 4 * h:4 * h + 4], stat[:, 0, 4 * h:4 * h + 4], XHD ** -0.5, None, ALU.mult
                   ).then_inc(attn_max, 1)

            def head_norm(h):
                dve.wait_ge(attn_exp, 4 * h + 4)
                link_v(V.reciprocal(stat[:, 1, 4 * h:4 * h + 4], stat[:, 1, 4 * h:4 * h + 4]))
                for t in range(T // P):
                    ins = ts(prob[:, t], prob[:, t], stat[:, 1, 4 * h + t:4 * h + t + 1], None, ALU.mult)
                ins.then_inc(prob_ready, 1)

            def o_low(h):
                dve.wait_ge(o_hi, h + 1)
                tt(h_lo[:, 2 * h:2 * h + 2, 0:T], ps[:, 2:4, :], h_hi[:, 2 * h:2 * h + 2, 0:T].bitcast(F32), ALU.subtract
                   ).then_inc(o_lo, 1)

            def sample_scores(b):
                dve.wait_ge(q_landed[b % 2], 16 * (b // 2 + 1))
                for m in range(2):
                    t = 2 * b + m
                    dve.wait_ge(cache_landed[t % CACHE_SLOTS], 16 * (t // CACHE_SLOTS + 1))
                    for h in range(XH):
                        keys = cache[:, t % CACHE_SLOTS, XHD * h:XHD * (h + 1)]
                        ins = V.tensor_tensor_reduce(keys, keys, q_bc[:, b % 2, XHD * h:XHD * (h + 1)], 1.0, 0.0,
                                                     ALU.mult, ALU.add, sc[:, m, XH * b + h:XH * b + h + 1])
                    ins.then_inc(k_used, 1)

            head_max(0)
            head_norm(0)
            head_max(1)
            sample_scores(0)
            sample_scores(1)
            for h in range(1, XH):
                head_norm(h)
                o_low(h - 1)
                if h + 1 < XH:
                    head_max(h + 1)
                sample_scores(2 * h)
                sample_scores(2 * h + 1)
            o_low(XH - 1)
            dve.wait_ge(sc_turned, 1)
            link_v(V.tensor_reduce(stat_s[:, 0:1], ps[0:B * XH, 4, 0:MEM], AX.X, ALU.max, negate=True))
            ts(stat_s[:, 0:1], stat_s[:, 0:1], XHD ** -0.5, None, ALU.mult).then_inc(sc_max, 1)
            dve.wait_ge(sc_exp, 1)
            link_v(V.reciprocal(stat_s[:, 1:2], stat_s[:, 1:2]))
            ts(prob_s[:, :], prob_s[:, :], stat_s[:, 1:2], None, ALU.mult).then_inc(prob_s_ready, 1)
            dve.wait_ge(prob_s_turned, 1)
            back = ps[:, 5, 0:2 * B * XH].rearrange("p (m n) -> p m n", m=2)
            for b in range(B):
                ins = V.tensor_copy(prob_z[:, :, (B + 1) * XH * b:(B + 1) * XH * b + XH], back[:, :, XH * b:XH * (b + 1)])
            ins.then_inc(prob_z_ready, 1)
            dve.wait_ge(v_used, 2 * B)
            for h in range(XH):
                src = ps[0:B * XH, 6 + h // 2, XHD * (h % 2):XHD * (h % 2 + 1)]
                if h == 0:
                    link_v(ts(o_pick[:, :], src, head_pick[:, 0:1], None, ALU.mult))
                else:
                    ins = stt(o_pick[:, :], src, head_pick[:, h:h + 1], o_pick[:, :], ALU.mult, ALU.add)
                    (link_v(ins) if h < XH - 1 else ins.then_inc(o_picked, 1))
            dve.wait_ge(o_hi, XH + 1)
            for d in range(2):
                ins = tt(h_lo[:, d:KT:2, T:NT], ps[:, 4, B * XH * d:B * XH * (d + 1)].rearrange("p (b h) -> p h b", b=B),
                         h_hi[:, d:KT:2, T:NT].bitcast(F32), ALU.subtract)
            ins.then_inc(o_lo, 1)

            for m in range(KT):
                post_take(p_x, B_O + m, m)
            post_add(p_x, "g_x_post")
            p_x.wait_x(dve, KT - 1)
            p_x.wait_x(dve, KT - 2)
            dve_scale_split(n_ffn, x_res, rs[:, :], "g_ffn_pre", y_buf, h_lo, h_hi)

            with dve.Fori(0, FT // 2) as i:
                for j in range(2):
                    b = B_UP + 2 * j + 1
                    dve.wait_ge(block_done, b + 1 + 4 * i)
                    dve.wait_ge(out_taken[0], B_UP // 2 + j + 1 + 2 * i)
                    if j == 1:
                        dve.wait_ge(f_lo_ready, 2 * i + 1)
                    tt(two(f_tmp[:, j]), out_view(1), two(silu[:, :]), ALU.mult).then_inc(out_taken[1], 1)
                    dve.wait_ge(out_taken[1], B_UP // 2 + j + 1 + 2 * i)
                    dve.wait_ge(f_hi_ready, 2 * i + j + 1)
                    at = bass.ds(2 * i + j, 1)
                    tt(f_lo[:, at].rearrange("p o n -> p (o n)"), f_tmp[:, j],
                       f_hi[:, at].rearrange("p o n -> p (o n)").bitcast(F32), ALU.subtract).then_inc(f_lo_ready, 1)
            for m in range(KT):
                post_take(p_ffn, B_DOWN + m, m)
            post_add(p_ffn, "g_ffn_post")
            for j in (1, 3):
                dve.wait_ge(y_turns, j + 1)
                V.tensor_copy(y_tok[:, j].rearrange("p (a n) -> p a n", a=2), ps[:, 2 * j:2 * j + 2, :]
                              ).then_inc(y_turn_v, 1)


_OUTS = [(1, T, D), (B, 1, D), (1, 1, C // HS, HS, HS), (1, 1, W_RWKV), (1, 1, TAPS - 1, C), (1, 1, MEM, XH, XHD),
         (1, 1, MEM, XH, XHD), (1, B, C // HS, HS, HS), (1, B, W_RWKV), (1, B, TAPS - 1, C)]


def kernel(**inputs):
    import numpy as _np
    import concourse.bacc as _bacc
    from concourse import mybir as _mybir
    from concourse.bass_utils import run_bass_kernel_spmd as _run

    nc = _bacc.Bacc("TRN2", target_bir_lowering=False, num_devices=1)
    arrays, args, outs = {}, {}, []
    for name, a in inputs.items():
        a = _np.ascontiguousarray(a)
        arrays[f"in_{name}_dram"] = a
        args[name] = nc.dram_tensor(f"in_{name}_dram", a.shape, _mybir.dt.from_np(a.dtype), kind="ExternalInput").ap()
    for i, shape in enumerate(_OUTS):
        outs.append(nc.dram_tensor(f"out_{i}_dram", shape, _mybir.dt.float32, kind="ExternalOutput").ap())
    hybrid_step_kernel(nc, args, outs)
    r = _run(nc, [arrays], core_ids=[0])
    return tuple(r.results[0][f"out_{i}_dram"] for i in range(len(_OUTS)))
```
